# Optimizing a Trainium2 kernel written in Bass

```python
import math
import numpy as np
import jax
import jax.numpy as jnp
from jax import lax

D_MODEL = 2048
BATCH = 1
SEQ = 256
DEPTH = 1

N_META = 16
GRID_W = 64
C_HY = 1024
HY_ORDER = 2
HY_EMB = 33
HY_HID = 64
SHORT_K = 3
C_FN = 1024
FN_GROUPS = 4
C_NA = 1024
NA_HEADS = 16
NA_HEAD_DIM = C_NA // NA_HEADS
NA_KH_MAX = 8
NA_KW = 16
NA_QB = 16
NA_KU = 32
N_BRANCH = 3
EPS = 1e-6
NEG_INF = -1e30
SPLIT_SIZES = ((HY_ORDER + 1) * C_HY, C_HY, C_FN, C_FN, 3 * C_NA, C_NA, N_BRANCH * D_MODEL)
N_IN = sum(SPLIT_SIZES)

kernel_name = 'hybrid_hyena_fnet_natten_encoder'

def rmsnorm(x, g):
    xf = x.astype(jnp.float32)
    y = xf * lax.rsqrt(jnp.mean(xf * xf, axis=-1, keepdims=True) + EPS)
    return (y * g.astype(jnp.float32)).astype(x.dtype)

def short_conv(x, w, b):
    L = x.shape[1]
    p = SHORT_K // 2
    xp = jnp.pad(x, ((0, 0), (p, p), (0, 0)))
    y = xp[:, 0:L] * w[0]
    for j in range(1, SHORT_K):
        y = y + xp[:, j:j + L] * w[j]
    return y + b

def hyena_filters(L, w1, b1, w2, b2, w3, b3, w4, freq, decay):
    f32 = jnp.float32
    t = jnp.linspace(0.0, 1.0, L, dtype=f32)[:, None]
    bands = (HY_EMB - 1) // 2
    w = 2.0 * math.pi * jnp.arange(L, dtype=f32)[:, None] / L
    f = jnp.linspace(1e-4, bands - 1, bands, dtype=f32)[None, :]
    z = jnp.concatenate([t, jnp.cos(f * w), -jnp.sin(f * w)], axis=-1)
    fr = freq.astype(f32)
    h = jnp.sin(fr * (z @ w1.astype(f32) + b1.astype(f32)))
    h = jnp.sin(fr * (h @ w2.astype(f32) + b2.astype(f32)))
    h = jnp.sin(fr * (h @ w3.astype(f32) + b3.astype(f32)))
    h = (h @ w4.astype(f32)).reshape(L, HY_ORDER, 2, C_HY)
    h = h * jnp.exp(-t[:, :, None, None] * jnp.abs(decay.astype(f32)))
    hf = h[:, :, 0]
    hb = h[:, :, 1]
    k = jnp.concatenate([hf, jnp.zeros((1, HY_ORDER, C_HY), f32), hb[1:][::-1]], axis=0)
    return jnp.fft.rfft(k, axis=0)

def fftconv(v, kf, skip):
    L = v.shape[1]
    vf = jnp.fft.rfft(v.astype(jnp.float32), n=2 * L, axis=1)
    y = jnp.fft.irfft(vf * kf[None], n=2 * L, axis=1)[:, :L]
    return y + v.astype(jnp.float32) * skip.astype(jnp.float32)

def hyena_mixer(u, x1, x2, kf, skip):
    z = fftconv(u, kf[:, 0], skip[0])
    z = x1.astype(jnp.float32) * z
    z = fftconv(z, kf[:, 1], skip[1])
    z = x2.astype(jnp.float32) * z
    return z.astype(u.dtype)

def fourier_mixer(xb):
    B, L, C = xb.shape
    xg = xb.astype(jnp.float32).reshape(B, L, FN_GROUPS, C // FN_GROUPS)
    y = jnp.fft.fft2(xg, axes=(1, 3), norm='ortho').real
    return y.reshape(B, L, C).astype(xb.dtype)

def na_tables(rows):
    kh = min(NA_KH_MAX, rows)
    rs = np.clip(np.arange(rows) - kh // 2, 0, rows - kh)
    cs = np.clip(np.arange(GRID_W) - NA_KW // 2, 0, GRID_W - NA_KW)
    ncb = GRID_W // NA_QB
    cu = np.clip(np.arange(ncb) * NA_QB - NA_KW // 2, 0, GRID_W - NA_KU)
    col_idx = cu[:, None] + np.arange(NA_KU)[None, :]
    qcol = np.arange(ncb)[:, None] * NA_QB + np.arange(NA_QB)[None, :]
    kcol = col_idx[:, None, :]
    qcs = cs[qcol][:, :, None]
    mask = (kcol >= qcs) & (kcol < qcs + NA_KW)
    dc_idx = np.clip(kcol - qcol[:, :, None] + NA_KW - 1, 0, 2 * NA_KW - 2)
    return kh, rs, col_idx, mask, dc_idx

def neighborhood_attention(q, k, v, rpb, meta_bias):
    B, Lt, _ = q.shape
    n = Lt - N_META
    rows = n // GRID_W
    kh, rs, col_idx, mask, dc_idx = na_tables(rows)
    H, dh = NA_HEADS, NA_HEAD_DIM
    scale = dh ** -0.5
    f32 = jnp.float32

    def heads(t):
        return t.reshape(B, Lt, H, dh).transpose(0, 2, 1, 3)

    qh, kh_, vh = heads(q), heads(k), heads(v)
    q_m, k_m, v_m = qh[:, :, :N_META], kh_[:, :, :N_META], vh[:, :, :N_META]

    def grid(t):
        return t[:, :, N_META:].reshape(B, H, rows, GRID_W, dh)

    q_g, k_g, v_g = grid(qh), grid(kh_), grid(vh)
    mb = meta_bias.astype(f32)
    rpb32 = rpb.astype(f32)

    s_m = jnp.einsum('bhqd,bhmd->bhqm', q_m, k_m).astype(f32) * scale + mb[None, :, None, :]
    o_m = jnp.einsum('bhqm,bhmd->bhqd', jax.nn.softmax(s_m, axis=-1).astype(v.dtype), v_m)

    ncb = GRID_W // NA_QB

    def row(args):
        q_r, r, r0 = args
        kb = lax.dynamic_slice_in_dim(k_g, r0, kh, axis=2)[:, :, :, col_idx]
        vb = lax.dynamic_slice_in_dim(v_g, r0, kh, axis=2)[:, :, :, col_idx]
        qb = q_r.reshape(B, H, ncb, NA_QB, dh)
        s_g = jnp.einsum('bhnqd,bhrnkd->bhnqrk', qb, kb).astype(f32) * scale
        dr = r0 + jnp.arange(kh, dtype=jnp.int32) - r + (NA_KH_MAX - 1)
        bias = jnp.take(rpb32, dr, axis=1)[:, :, dc_idx]
        s_g = s_g + bias.transpose(0, 2, 3, 1, 4)[None]
        s_g = jnp.where(mask[:, :, None, :], s_g, NEG_INF)
        s_x = jnp.einsum('bhnqd,bhmd->bhnqm', qb, k_m).astype(f32) * scale + mb[None, :, None, None, :]
        s = jnp.concatenate([s_g.reshape(B, H, ncb, NA_QB, kh * NA_KU), s_x], axis=-1)
        p = jax.nn.softmax(s, axis=-1).astype(v.dtype)
        p_g = p[..., :kh * NA_KU].reshape(B, H, ncb, NA_QB, kh, NA_KU)
        p_x = p[..., kh * NA_KU:]
        o = jnp.einsum('bhnqrk,bhrnkd->bhnqd', p_g, vb) + jnp.einsum('bhnqm,bhmd->bhnqd', p_x, v_m)
        return o.reshape(B, H, GRID_W, dh)

    o_rows = lax.map(row, (jnp.moveaxis(q_g, 2, 0), jnp.arange(rows, dtype=jnp.int32),
                           jnp.asarray(rs, dtype=jnp.int32)))
    o_g = jnp.moveaxis(o_rows, 0, 2).reshape(B, H, n, dh)
    o = jnp.concatenate([o_m, o_g], axis=2)
    return o.transpose(0, 2, 1, 3).reshape(B, Lt, C_NA)

def mixer_layer(h, norm_g, w_in, conv_w, conv_b, w1, b1, w2, b2, w3, b3, w4, freq, decay, skip,
                rpb, meta_bias, w_a, w_b, w_c, w_out):
    L = h.shape[1]
    xn = rmsnorm(h, norm_g)
    z = xn @ w_in
    idx = [int(i) for i in np.cumsum(SPLIT_SIZES)[:-1]]
    hy_in, hy_gate, fn_in, fn_gate, qkv, na_gate, merge = jnp.split(z, idx, axis=-1)
    hy_in = short_conv(hy_in, conv_w, conv_b)
    u, x1, x2 = jnp.split(hy_in, HY_ORDER + 1, axis=-1)
    kf = hyena_filters(L, w1, b1, w2, b2, w3, b3, w4, freq, decay)
    y_a = hyena_mixer(u, x1, x2, kf, skip) * jax.nn.silu(hy_gate)
    y_b = fourier_mixer(fn_in) * jax.nn.silu(fn_gate)
    q, k, v = jnp.split(qkv, 3, axis=-1)
    y_c = neighborhood_attention(q, k, v, rpb, meta_bias) * jax.nn.silu(na_gate)
    g_a, g_b, g_c = jnp.split(jax.nn.sigmoid(merge), N_BRANCH, axis=-1)
    m = g_a * (y_a @ w_a) + g_b * (y_b @ w_b) + g_c * (y_c @ w_c)
    return h + m @ w_out

def setup_inputs(seed: int = 0) -> dict:
    key = jax.random.key(seed)
    ks = jax.random.split(key, 24)

    def nrm(k, shape, std):
        return std * jax.random.normal(k, shape, jnp.float32)

    L = SEQ + N_META
    decay0 = jnp.linspace(math.log(1e-2) / 1.5, math.log(1e-2) / 0.3, C_HY, dtype=jnp.float32)
    return {
        'x': nrm(ks[0], (BATCH, SEQ, D_MODEL), 1.0),
        'meta_tokens': nrm(ks[1], (N_META, D_MODEL), 1.0),
        'norm_g': 1.0 + nrm(ks[2], (DEPTH, D_MODEL), 0.02),
        'w_in': nrm(ks[3], (DEPTH, D_MODEL, N_IN), D_MODEL ** -0.5),
        'hy_conv_w': nrm(ks[4], (DEPTH, SHORT_K, (HY_ORDER + 1) * C_HY), SHORT_K ** -0.5),
        'hy_conv_b': nrm(ks[5], (DEPTH, (HY_ORDER + 1) * C_HY), 0.02),
        'hy_flt_w1': nrm(ks[6], (DEPTH, HY_EMB, HY_HID), HY_EMB ** -0.5),
        'hy_flt_b1': nrm(ks[7], (DEPTH, HY_HID), 0.1),
        'hy_flt_w2': nrm(ks[8], (DEPTH, HY_HID, HY_HID), HY_HID ** -0.5),
        'hy_flt_b2': nrm(ks[9], (DEPTH, HY_HID), 0.1),
        'hy_flt_w3': nrm(ks[10], (DEPTH, HY_HID, HY_HID), HY_HID ** -0.5),
        'hy_flt_b3': nrm(ks[11], (DEPTH, HY_HID), 0.1),
        'hy_flt_w4': nrm(ks[12], (DEPTH, HY_HID, HY_ORDER * 2 * C_HY), 0.5 * L ** -0.5),
        'hy_flt_freq': 1.0 + nrm(ks[13], (DEPTH, HY_HID), 0.1),
        'hy_decay': jnp.broadcast_to(decay0, (DEPTH, HY_ORDER, 2, C_HY)) + nrm(ks[14], (DEPTH, HY_ORDER, 2, C_HY), 0.1),
        'hy_skip': nrm(ks[15], (DEPTH, HY_ORDER, C_HY), 0.5),
        'na_rpb': nrm(ks[16], (DEPTH, NA_HEADS, 2 * NA_KH_MAX - 1, 2 * NA_KW - 1), 0.1),
        'na_meta_bias': nrm(ks[17], (DEPTH, NA_HEADS, N_META), 0.1),
        'w_branch_a': nrm(ks[18], (DEPTH, C_HY, D_MODEL), C_HY ** -0.5),
        'w_branch_b': nrm(ks[19], (DEPTH, C_FN, D_MODEL), C_FN ** -0.5),
        'w_branch_c': nrm(ks[20], (DEPTH, C_NA, D_MODEL), C_NA ** -0.5),
        'w_out': nrm(ks[21], (DEPTH, D_MODEL, D_MODEL), D_MODEL ** -0.5),
        'final_g': 1.0 + nrm(ks[22], (D_MODEL,), 0.02),
    }

def reference(x, meta_tokens, norm_g, w_in, hy_conv_w, hy_conv_b, hy_flt_w1, hy_flt_b1, hy_flt_w2,
              hy_flt_b2, hy_flt_w3, hy_flt_b3, hy_flt_w4, hy_flt_freq, hy_decay, hy_skip, na_rpb,
              na_meta_bias, w_branch_a, w_branch_b, w_branch_c, w_out, final_g):
    B = x.shape[0]
    meta = jnp.broadcast_to(meta_tokens[None].astype(x.dtype), (B, N_META, D_MODEL))
    h = jnp.concatenate([meta, x], axis=1)
    for i in range(DEPTH):
        h = mixer_layer(h, norm_g[i], w_in[i], hy_conv_w[i], hy_conv_b[i],
                        hy_flt_w1[i], hy_flt_b1[i], hy_flt_w2[i], hy_flt_b2[i], hy_flt_w3[i], hy_flt_b3[i],
                        hy_flt_w4[i], hy_flt_freq[i], hy_decay[i], hy_skip[i],
                        na_rpb[i], na_meta_bias[i], w_branch_a[i], w_branch_b[i], w_branch_c[i], w_out[i])
    return rmsnorm(h, final_g)[:, N_META:]


_drawn_inputs = setup_inputs


def setup_inputs(seed=0):
    import zlib

    import numpy as np

    out = dict(_drawn_inputs(seed))
    spreads = {}
    factors = {'norm_g': 4.802,
     'hy_conv_b': 3.776,
     'na_rpb': 50.936,
     'na_meta_bias': 173.157,
     'final_g': 22.656}
    for name, (base, spread) in spreads.items():
        noise = np.random.default_rng([zlib.crc32(name.encode()), seed]).standard_normal(out[name].shape)
        drawn = base * np.exp(spread * noise) if base else spread * noise
        out[name] = jnp.asarray(drawn.astype(out[name].dtype))
    for name, factor in factors.items():
        out[name] = (out[name] * factor).astype(out[name].dtype)
    return out
```

```python
from contextlib import ExitStack
import math

import numpy as np

import concourse.bass as bass
from concourse import mybir

F32 = mybir.dt.float32
F32R = mybir.dt.float32r
ALU = mybir.AluOpType
ACT = mybir.ActivationFunctionType

D = 2048
L = 272
NM = 16
NG = L - NM
C = 1024
CC = 256
CH = C // CC
KT = D // 128
EPS = 1e-6
GRID_W = 64
KW = 16
HEADS = 16
HC = HEADS // CH
RPB_R, RPB_C = 15, 31
HID, EMB = 64, 33
FFT_N = 2 * L
TOK = [(NM, 128), (NM + 128, 128), (0, NM)]
BLOCKS = [("u", 0, L), ("q", 6 * C, NG), ("k", 7 * C, L), ("v", 8 * C, L), ("x1", C, L), ("x2", 2 * C, L),
          ("hgate", 3 * C, NG), ("fin", 4 * C, L), ("ngate", 9 * C, NG), ("fgate", 5 * C, NG)]
NBLK = len(BLOCKS)
S1 = 2 * NBLK
W2 = CH * S1
JB = D // CC
S2 = 18
W3 = W2 + JB // 2 * S2
NW = W3 + 2 * JB
NCONST = 4
FORDER = (0, 2, 1)
TWO_PI = 2.0 * math.pi
MAGIC = 1.5 * 2.0 ** 23
BT = NM + 6 * GRID_W + NM
CLAMP = 3.1415925


def constants():
    pos = np.arange(L, dtype=np.float64)
    om = TWO_PI * (pos + 0.5) / FFT_N

    def rows(m):
        out = np.zeros((128, 3, m.shape[1]), np.float64)
        for t, (p, n) in enumerate(TOK):
            out[:n, t] = m[p:p + n]
        return out

    def slab(*parts):
        flat = np.concatenate([p.reshape(128, -1) for p in parts], axis=1)
        out = np.zeros((128, 2048), np.float32)
        out[:, :flat.shape[1]] = flat
        return out

    lag = pos[:, None] * om[None, :]
    half = (pos[:, None] + 0.5) * om[None, :]
    filt = np.stack([rows(np.cos(lag)), rows(-np.sin(lag))], axis=2)
    sym = np.stack([rows(np.cos(half)), rows(-np.sin(half))], axis=2)
    ch = np.arange(CC, dtype=np.float64)
    ang = TWO_PI * ((ch[:, None] * ch[None, :]) % CC) / CC
    fch = np.concatenate([np.cos(ang), np.sin(ang)], axis=1).reshape(2, 128, 2 * CC).transpose(1, 0, 2)
    angl = TWO_PI * ((pos[:, None] * pos[None, NM:]) % L) / L
    norm = 1.0 / math.sqrt(L * CC)
    ftok = np.stack([rows(np.cos(angl) * norm), rows(-np.sin(angl) * norm)], axis=2)
    tables = np.stack([slab(filt), slab(sym), slab(fch), slab(ftok)])

    f32 = np.float32
    t = np.linspace(0.0, 1.0, L, dtype=f32)[:, None]
    bands = (EMB - 1) // 2
    w = f32(TWO_PI) * np.arange(L, dtype=f32)[:, None] / f32(L)
    f = np.linspace(1e-4, bands - 1, bands, dtype=f32)[None, :]
    z = np.concatenate([t, np.cos(f * w), -np.sin(f * w)], axis=-1).astype(f32)
    negt = np.zeros((128, 3), f32)
    for i, (p, n) in enumerate(TOK):
        negt[:n, i] = -t[p:p + n, 0]
    col = np.arange(GRID_W)
    cs = np.clip(col - KW // 2, 0, GRID_W - KW)
    seen = (col[None, :] >= cs[:, None]) & (col[None, :] < cs[:, None] + KW)
    mask = np.where(seen, 0.0, -1e30).astype(f32)
    mask = mask[::-1]
    return tables, np.ascontiguousarray(z.T), negt, np.concatenate([mask, mask]), np.eye(128, dtype=f32)


def build(nc, x, meta, w_stream, tables, zT, negt_in, mask_in, ident_in, params_in, mlp_in, w1, w2, w3, w4,
          decay, rpb, mbias, final_g, out):
    kg_dram = nc.dram_tensor("kspec_grid", [CH, 2, 128, 2 * 2 * CC], F32, kind="Internal").ap()
    km_dram = nc.dram_tensor("kspec_meta", [CH, 2, NM, 2 * CC], F32, kind="Internal").ap()
    y_dram = nc.dram_tensor("branch_y", [3, 128, 2 * CH, NG], F32, kind="Internal").ap()

    at = [(nc.sbuf_base + 63) // 64 * 64]

    def place(name, shape, dt=F32):
        t = nc.alloc_sbuf_tensor_at(name, shape, dt, offset=at[0])
        at[0] += (4 * int(np.prod(shape[1:])) + 63) // 64 * 64
        assert at[0] <= nc.sbuf_usable_end, (name, at[0])
        return t

    params = place("params", [128, 128])
    ident = place("ident", [128, 128])
    negt = place("negt", [128, 3])
    mask = place("mask", [128, GRID_W])
    stat = place("stat", [128, 16])
    raw = place("raw", [128, 4, 8 * CC])
    xn_at = at[0]
    xn_hi = place("xn_hi", [128, KT, L], F32R)
    xn_lo = place("xn_lo", [128, KT, L], F32R)
    xn_end = at[0]
    split_at = at[0]
    w_hi = place("w_hi", [128, 2, 8, CC], F32R)
    w_lo = place("w_lo", [128, 2, 8, CC], F32R)
    split_end = at[0]
    mix_at = at[0]
    sym_hi = place("sym_hi", [128, 3, 2, L], F32R)
    sym_lo = place("sym_lo", [128, 3, 2, L], F32R)
    fch_hi = place("fch_hi", [128, 2, 2 * CC], F32R)
    fch_lo = place("fch_lo", [128, 2, 2 * CC], F32R)
    ftok_hi = place("ftok_hi", [128, 3, 2, NG], F32R)
    ftok_lo = place("ftok_lo", [128, 3, 2, NG], F32R)
    work_at = at[0]
    kspec = place("kspec", [128, 3, 2, CC])
    bias_t = place("bias_t", [128, HC, BT])
    spec_at = at[0]
    y_hi = place("y_hi", [128, 3, 2, CC], F32R)
    y_lo = place("y_lo", [128, 3, 2, CC], F32R)
    at[0] = spec_at
    p2_hi = place("p2_hi", [128, 3, 2, CC], F32R)
    p2_lo = place("p2_lo", [128, 3, 2, CC], F32R)
    uT_hi = place("uT_hi", [128, 3, CC], F32R)
    uT_lo = place("uT_lo", [128, 3, CC], F32R)
    vT_hi = place("vT_hi", [128, 3, CC], F32R)
    vT_lo = place("vT_lo", [128, 3, CC], F32R)
    pT_hi = place("pT_hi", [128, 3, NG], F32R)
    pT_lo = place("pT_lo", [128, 3, NG], F32R)
    qk_at = at[0]
    q_hi = place("q_hi", [128, 2, NG], F32R)
    q_lo = place("q_lo", [128, 2, NG], F32R)
    k_hi = place("k_hi", [128, 2, L + NM], F32R)
    k_lo = place("k_lo", [128, 2, L + NM], F32R)
    qk_end = at[0]
    at[0] = qk_at
    fi_hi = place("fi_hi", [128, 2, L], F32R)
    fi_lo = place("fi_lo", [128, 2, L], F32R)
    at[0] = qk_end
    u = place("u", [128, 2, L])
    x1 = place("x1", [128, 2, L])
    x2 = place("x2", [128, 2, L])
    v = place("v", [128, 2, L])
    o = place("o", [128, 2, NG])
    gate = place("gate", [128, 2, NG])
    gexp = place("gexp", [128, 2, NG])
    prod = place("prod", [128, 3, 2, CC])
    sco = place("sco", [128, 2, L])
    ystage = place("ystage", [128, 2, NG])
    at[0] = work_at
    xin = place("xin", [128, 3, D])
    filt_hi = place("filt_hi", [128, 3, 2, L], F32R)
    filt_lo = place("filt_lo", [128, 3, 2, L], F32R)
    kstage = place("kstage", [128, 2, 2, 2, CC])
    kmstage = place("kmstage", [NM, 2, 2, CC])
    absd = place("absd", [128, 2, 2, CC])
    w4s = place("w4s", [HID, 2, 2, CC])
    mlpw = place("mlpw", [HID, 3 * HID + 4])
    zt = place("zt", [EMB, L])
    hid = place("hid", [HID, L])
    red = place("red", [HID, 4, L])
    hm = place("hm", [128, 2, 2, CC])
    sd = place("sd", [128, 2, 2, CC])
    at[0] = split_at
    sd_hi = place("sd_hi", [128, 3, 2, 2, CC], F32R)
    sd_lo = place("sd_lo", [128, 3, 2, 2, CC], F32R)
    envel = place("envel", [128, 2, 2, 2, CC])
    assert at[0] <= split_end
    at[0] = mix_at
    m_hi = place("m_hi", [128, KT, NG], F32R)
    m_lo = place("m_lo", [128, KT, NG], F32R)
    m_end = at[0]
    at[0] = mix_at
    y_raw = place("y_raw", [128, 3, 2 * CH * NG])
    at[0] = m_end
    yb_hi = place("yb_hi", [128, 3, 2 * CH, NG], F32R)
    yb_lo = place("yb_lo", [128, 3, 2 * CH, NG], F32R)
    mgate = place("mgate", [128, 2, 2, NG])
    msum = place("msum", [128, 2, NG])
    mterm = place("mterm", [128, 2, NG])
    at[0] = xn_at
    h = place("h", [128, 2, D])
    fg = place("fg", [128, D])
    at[0] = m_end
    sq = place("sq", [128, D])

    CW, CB, SK, NGC = 0, 72, 96, 112
    with ExitStack() as ctx:
        ps = ctx.enter_context(nc.psum_tensor("ps", [128, 8, 512], F32))

        def sem(name):
            return ctx.enter_context(nc.semaphore(name))

        w_landed = [sem(f"w_landed{i}") for i in range(4)]
        hi_done = sem("hi_done")
        lo_done = sem("lo_done")
        slab_used = sem("slab_used")
        x_landed = sem("x_landed")
        small_landed = sem("small_landed")
        w4_landed = sem("w4_landed")
        dec_landed = sem("dec_landed")
        mlp_mm = sem("mlp_mm")
        mlp_red = sem("mlp_red")
        mlp_sin = sem("mlp_sin")
        x_sq = sem("x_sq")
        x_var = sem("x_var")
        x_std = sem("x_std")
        x_scaled = sem("x_scaled")
        xt_mm = sem("xt_mm")
        xt_hi = sem("xt_hi")
        xt_lo = sem("xt_lo")
        dec_abs = sem("dec_abs")
        env_done = sem("env_done")
        h4_mm = sem("h4_mm")
        h4_read = sem("h4_read")
        sd_done = sem("sd_done")
        sdhi_done = sem("sdhi_done")
        sdlo_done = sem("sdlo_done")
        k_mm = sem("k_mm")
        k_evac = sem("k_evac")
        k_written = sem("k_written")
        a_ev = sem("a_ev")
        proj_read = sem("proj_read")
        t_mm = sem("t_mm")
        t_hi = sem("t_hi")
        t_lo = sem("t_lo")
        fwd_mm = sem("fwd_mm")
        y_full = sem("y_full")
        yhi_done = sem("yhi_done")
        ylo_done = sem("ylo_done")
        inv_mm = sem("inv_mm")
        z_done = sem("z_done")
        s_mm = sem("s_mm")
        smax_done = sem("smax_done")
        exp_done = sem("exp_done")
        p_done = sem("p_done")
        pt_mm = sem("pt_mm")
        pt_hi = sem("pt_hi")
        pt_lo = sem("pt_lo")
        pv_mm = sem("pv_mm")
        o_done = sem("o_done")
        n1_mm = sem("n1_mm")
        n1_hi = sem("n1_hi")
        n1_lo = sem("n1_lo")
        n2_mm = sem("n2_mm")
        ya_done = sem("ya_done")
        yb_done = sem("yb_done")
        yc_done = sem("yc_done")
        y_written = sem("y_written")
        k_landed = sem("k_landed")
        b_landed = sem("b_landed")
        b_ready = sem("b_ready")
        y_landed = [sem(f"y_landed{i}") for i in range(3)]
        bhi_done = sem("bhi_done")
        blo_done = sem("blo_done")
        gate_done = sem("gate_done")
        br_read = sem("br_read")
        msum_done = sem("msum_done")
        mhi_done = sem("mhi_done")
        mlo_done = sem("mlo_done")
        h_landed = sem("h_landed")
        h_sum = sem("h_sum")
        f_sq = sem("f_sq")
        f_var = sem("f_var")
        f_std = sem("f_std")
        f_done = sem("f_done")
        out_written = sem("out_written")
        dve_link = sem("dve_link")

        block = ctx.enter_context(nc.Block())
        SMALL = 10

        @block.sync
        def _(sp):
            sp.dma_start(raw[:, 0, :], tables[0]).then_inc(w_landed[0], 16)
            sp.dma_start(xin[:, 0, :], x[0:128, :]).then_inc(x_landed, 16)
            sp.dma_start(xin[:, 1, :], x[128:256, :]).then_inc(x_landed, 16)
            sp.dma_start(xin[0:NM, 2, :], meta).then_inc(x_landed, 16)
            for i in range(1, NCONST):
                sp.dma_start(raw[:, i, :], tables[i]).then_inc(w_landed[i], 16)
            with sp.Fori(0, CH) as c:
                for t in range(S1):
                    sp.wait_ge(lo_done, c * S1 + t + 1)
                    sp.dma_start(raw[:, t % 4, :], w_stream[bass.ds(c * S1 + t, 1), :, :].rearrange("a p n -> p (a n)")
                                 ).then_inc(w_landed[t % 4], 16)
            with sp.Fori(0, JB // 2) as i:
                for t in range(S2):
                    sp.wait_ge(lo_done, i * S2 + (W2 + t + 2))
                    sp.dma_start(raw[:, t % 3, :],
                                 w_stream[bass.ds(i * S2 + (W2 + t), 1), :, :].rearrange("a p n -> p (a n)")
                                 ).then_inc(w_landed[t % 3], 16)
            with sp.Fori(0, JB // 2) as i:
                for t in range(4):
                    sp.wait_ge(lo_done, i * 4 + (W3 + t + 2))
                    sp.dma_start(raw[:, t % 4, :],
                                 w_stream[bass.ds(i * 4 + (W3 + t), 1), :, :].rearrange("a p n -> p (a n)")
                                 ).then_inc(w_landed[t % 4], 16)
            for tt in range(2):
                sp.wait_ge(f_done, tt + 1)
                sp.dma_start(out[128 * tt:128 * tt + 128, :], h[:, tt, :]).then_inc(out_written, 16)
            sp.wait_ge(out_written, 32)

        @block.gpsimd
        def _(pool):
            pool.dma_start(zt[:, :], zT).then_inc(small_landed, 16)
            pool.dma_start(mlpw[0:EMB, 0:HID], w1).then_inc(small_landed, 16)
            pool.dma_start(mlpw[:, HID:2 * HID], w2).then_inc(small_landed, 16)
            pool.dma_start(mlpw[:, 2 * HID:3 * HID], w3).then_inc(small_landed, 16)
            pool.dma_start(mlpw[:, 3 * HID:], mlp_in).then_inc(small_landed, 16)
            pool.dma_start(negt[:, :], negt_in).then_inc(small_landed, 16)
            pool.dma_start(ident[:, :], ident_in).then_inc(small_landed, 16)
            pool.dma_start(params[:, :], params_in).then_inc(small_landed, 16)
            pool.dma_start(mask[0:64, :], mask_in[0:64, :]).then_inc(k_written, 16)
            pool.dma_start(mask[64:128, :], mask_in[64:128, :]).then_inc(y_written, 16)

            def load_filter(c):
                pool.dma_start(w4s[:, :, :, :].rearrange("p a b n -> p (a b n)"),
                               w4[bass.ds(c, 1), :, :].rearrange("a p n -> p (a n)")).then_inc(w4_landed, 16)
                pool.dma_start(absd[:, :, :, :].rearrange("p a b n -> p (a b n)"),
                               decay[bass.ds(c, 1), :].rearrange("a n -> (a n)").partition_broadcast(128)
                               ).then_inc(dec_landed, 16)

            def store_spectrum(c):
                pool.wait_ge(k_evac, c * 6 + 10)
                pool.dma_start(kg_dram[bass.ds(c, 1), :, :, :].rearrange("a o p n -> p (a o) n"),
                               kstage[:, :, :, :, :].rearrange("p o f r n -> p o (f r n)")).then_inc(k_written, 16)
                pool.dma_start(km_dram[bass.ds(c, 1), :, :, :].rearrange("a o p n -> p (a o) n"),
                               kmstage[:, :, :, :].rearrange("p o r n -> p o (r n)")).then_inc(k_written, 16)

            load_filter(0)
            with pool.Fori(1, CH) as c:
                pool.wait_ge(h4_mm, c * 3)
                pool.wait_ge(env_done, c * 3)
                load_filter(c)
                store_spectrum(c - 1)
            store_spectrum(CH - 1)
            pool.wait_ge(k_written, 16 + 32 * CH)
            pool.wait_ge(k_mm, 6 * CH)
            pool.wait_ge(xt_mm, KT)

            def load_bias(c):
                for s in range(2):
                    for hh in range(HC):
                        src = bass.AP(rpb.tensor, c * (HC * RPB_R * RPB_C) + ((hh * RPB_R + 5 - s) * RPB_C + KW - GRID_W),
                                      [[1, GRID_W], [RPB_C, 6], [1, GRID_W]])
                        pool.dma_start(bias_t[64 * s:64 * s + 64, hh, NM:NM + 6 * GRID_W].rearrange(
                            "p (j k) -> p j k", j=6), src).then_inc(b_landed, 16)
                for lo in (0, NM + 6 * GRID_W):
                    pool.dma_start(bias_t[:, :, lo:lo + NM],
                                   mbias[bass.ds(c, 1), :].rearrange("a (h m) -> (a h) m", h=HC).partition_broadcast(128)
                                   ).then_inc(b_landed, 16)
                pool.wait_ge(b_landed, (c + 1) * (16 * (2 * HC + 2)))
                for hh in range(HC):
                    grid = bias_t[:, hh, NM:NM + 6 * GRID_W].rearrange("p (j k) -> p j k", j=6)
                    msk = mask[:, :].rearrange("p (a k) -> p a k", a=1).broadcast_to([128, 6, GRID_W])
                    last = nc.gpsimd.tensor_tensor(grid, grid, msk, ALU.add)
                last.then_inc(b_ready, 1)

            def load_spectrum(c, order):
                pool.dma_start(kspec[:, 0:2, :, :].rearrange("p f r n -> p (f r n)"),
                               kg_dram[bass.ds(c, 1), order, :, :].rearrange("a p n -> p (a n)")).then_inc(k_landed, 16)
                pool.dma_start(kspec[0:NM, 2, :, :].rearrange("p r n -> p (r n)"),
                               km_dram[bass.ds(c, 1), order, :, :].rearrange("a p n -> p (a n)")).then_inc(k_landed, 16)

            def second_order(c):
                pool.wait_ge(y_full, c * 6 + 3)
                load_spectrum(c, 1)

            def store_y(c, branch, done):
                pool.wait_ge(done, c + 1)
                pool.dma_start(y_dram[branch, :, bass.ds(c * 2, 2), :], ystage[:, :, :]).then_inc(y_written, 16)

            load_bias(0)
            load_spectrum(0, 0)
            with pool.Fori(1, CH) as c:
                second_order(c - 1)
                store_y(c - 1, 0, ya_done)
                store_y(c - 1, 2, yc_done)
                pool.wait_ge(smax_done, c * HC)
                load_bias(c)
                pool.wait_ge(y_full, c * 6)
                load_spectrum(c, 0)
                store_y(c - 1, 1, yb_done)
            second_order(CH - 1)
            store_y(CH - 1, 0, ya_done)
            store_y(CH - 1, 2, yc_done)
            store_y(CH - 1, 1, yb_done)
            pool.wait_ge(y_written, 16 + 48 * CH)
            for b in range(3):
                pool.dma_start(y_raw[:, b, :], y_dram[b].rearrange("p k n -> p (k n)")).then_inc(y_landed[b], 16)
            pool.wait_ge(slab_used, W3)
            for tt in range(2):
                pool.dma_start(h[:, tt, :], x[128 * tt:128 * tt + 128, :]).then_inc(h_landed, 16)
            pool.dma_start(fg[:, :], final_g.partition_broadcast(128)).then_inc(h_landed, 16)

        def slot_main(c, t):
            return t % 4, (c * 5 + (t // 4 + 2)) * 16

        def slot_merge(i, t):
            return t % 3, (i * 6 + (t // 3 + 22)) * 16

        def slot_out(i, t):
            return t % 4, (i + ((46 if t % 4 < 3 else 22) + t // 4)) * 16

        @block.tensor
        def _(pe):
            mm = nc.tensor.matmul

            def three(out_ap, a_hi, a_lo, b_hi, b_lo, first, last, skip=False):
                mm(out_ap, a_hi, b_hi, start=first, stop=False)
                mm(out_ap, a_hi, b_lo, start=False, stop=False)
                return mm(out_ap, a_lo, b_hi, start=False, stop=last)

            pe.wait_ge(small_landed, 16 * 8)
            for layer in range(3):
                if layer == 0:
                    ins = mm(ps[0:HID, 7, 0:L], mlpw[0:EMB, 0:HID], zt[:, :], start=True, stop=True)
                else:
                    pe.wait_ge(mlp_sin, layer)
                    ins = mm(ps[0:HID, 7, 0:L], mlpw[:, HID * layer:HID * layer + HID], hid[:, :], start=True, stop=True)
                ins.then_inc(mlp_mm, 1)
            pe.wait_ge(x_scaled, 3)
            for k in range(KT):
                if k >= 4:
                    pe.wait_ge(xt_lo, k - 3)
                for t, (p, n) in enumerate(TOK):
                    last = nc.tensor.transpose(ps[:, k % 4, p:p + n], xin[0:n, t, 128 * k:128 * k + 128], ident[0:n, 0:n])
                last.then_inc(xt_mm, 1)
            pe.wait_ge(mlp_sin, 3)
            pe.wait_ge(xt_lo, KT)
            pe.wait_ge(lo_done, 1)
            with pe.Fori(0, CH) as c:
                pe.wait_ge(w4_landed, c * 16 + 16)
                for j, t in enumerate(FORDER):
                    p, n = TOK[t]
                    b = 4 + 2 * (j % 2)
                    if j == 2:
                        pe.wait_ge(h4_read, c * 3 + 1)
                    for o_ in range(2):
                        last = mm(ps[0:n, b + o_, :], hid[:, p:p + n], w4s[:, o_, :, :].rearrange("p d n -> p (d n)"),
                                  start=True, stop=True)
                    last.then_inc(h4_mm, 1)
                pe.wait_ge(sdlo_done, c * 3 + 3)
                for f, (fp, fn) in enumerate(TOK):
                    for ri in range(2):
                        e = 2 * f + ri
                        pe.wait_ge(k_evac, c * 6 + e + 1)
                        for t, (p, n) in enumerate(TOK):
                            sl = (slice(0, n), t, ri)
                            last = three(ps[0:fn, e % 4, :], filt_hi[0:n, t, ri, fp:fp + fn], filt_lo[0:n, t, ri, fp:fp + fn],
                                         sd_hi[sl].rearrange("p o n -> p (o n)"), sd_lo[sl].rearrange("p o n -> p (o n)"),
                                         t == 0, t == 2)
                        last.then_inc(k_mm, 1)

            def proj_slab(par, bank, half, p0):
                for nt in range(2):
                    for k in range(8):
                        last = three(ps[:, bank + nt, 0:L - p0], w_hi[:, par, k, 128 * nt:128 * nt + 128],
                                     w_lo[:, par, k, 128 * nt:128 * nt + 128], xn_hi[:, 8 * half + k, p0:L],
                                     xn_lo[:, 8 * half + k, p0:L], half == 0 and k == 0, half == 1 and k == 7)
                last.then_inc(slab_used, 1)

            def turn(src, bank):
                for t, (p, n) in enumerate(TOK):
                    for i in range(2):
                        dst = ps[:, bank, CC * t + 128 * i:CC * t + 128 * i + 128] if t < 2 else \
                            ps[0:n, bank + 1, 128 * i:128 * i + 128]
                        last = nc.tensor.transpose(dst, src[:, i, p:p + n], ident[:, :])
                last.then_inc(t_mm, 1)

            def forward(f, bank):
                fp, fn = TOK[f]
                for ri in range(2):
                    for t, (p, n) in enumerate(TOK):
                        last = three(ps[0:fn, bank, CC * ri:CC * ri + CC], sym_hi[0:n, t, ri, fp:fp + fn],
                                     sym_lo[0:n, t, ri, fp:fp + fn], uT_hi[0:n, t, :], uT_lo[0:n, t, :], t == 0, t == 2)
                last.then_inc(fwd_mm, 1)

            def inverse(p0):
                for i in range(2):
                    for e in range(6):
                        f, ri = e // 2, e % 2
                        n = TOK[f][1]
                        last = three(ps[:, 4 + i, 0:L - p0], y_hi[0:n, f, ri, 128 * i:128 * i + 128],
                                     y_lo[0:n, f, ri, 128 * i:128 * i + 128], sym_hi[0:n, f, ri, p0:L],
                                     sym_lo[0:n, f, ri, p0:L], e == 0, e == 5)
                last.then_inc(inv_mm, 1)

            def scores(hh):
                i, r = hh // 2, slice(64 * (hh % 2), 64 * (hh % 2) + 64)
                for a in range(2):
                    ks = slice(NM, NM + L) if a == 0 else slice(0, L)
                    last = three(ps[:, 6 + a, 0:L], q_hi[r, i, 128 * a:128 * a + 128], q_lo[r, i, 128 * a:128 * a + 128],
                                 k_hi[r, i, ks], k_lo[r, i, ks], True, True)
                last.then_inc(s_mm, 1)

            def turn_p():
                for a in range(2):
                    g0 = 0 if a == 0 else NM
                    m0 = NG if a == 0 else 0
                    for kt in range(2):
                        nc.tensor.transpose(ps[:, 6, NG * kt + 128 * a:NG * kt + 128 * a + 128],
                                            sco[:, a, g0 + 128 * kt:g0 + 128 * kt + 128], ident[:, :])
                    last = nc.tensor.transpose(ps[0:NM, 7, 128 * a:128 * a + 128], sco[:, a, m0:m0 + NM], ident[:, :])
                last.then_inc(pt_mm, 1)

            def attend(hh):
                i = hh // 2
                for t, (p, n) in enumerate(TOK):
                    last = three(ps[:, 7, NG:2 * NG], vT_hi[0:n, t, 128 * i:128 * i + 128], vT_lo[0:n, t, 128 * i:128 * i + 128],
                                 pT_hi[0:n, t, :], pT_lo[0:n, t, :], t == 0, t == 2)
                last.then_inc(pv_mm, 1)

            def fnet_channels(t, bank):
                p, n = TOK[t]
                for i in range(2):
                    last = three(ps[0:n, bank, :], fi_hi[:, i, p:p + n], fi_lo[:, i, p:p + n], fch_hi[:, i, :], fch_lo[:, i, :],
                                 i == 0, i == 1)
                last.then_inc(n1_mm, 1)

            def fnet_tokens():
                for i in range(2):
                    for e in range(6):
                        t, ri = e // 2, e % 2
                        n = TOK[t][1]
                        last = three(ps[:, 4, NG * i:NG * i + NG], p2_hi[0:n, t, ri, 128 * i:128 * i + 128],
                                     p2_lo[0:n, t, ri, 128 * i:128 * i + 128], ftok_hi[0:n, t, ri, :], ftok_lo[0:n, t, ri, :],
                                     e == 0, e == 5)
                last.then_inc(n2_mm, 1)

            pe.wait_ge(lo_done, NCONST)
            with pe.Fori(0, CH) as c:
                for t in range(S1):
                    name, _, n = BLOCKS[t // 2]
                    if t % 2 == 0:
                        pe.wait_ge(proj_read, c * NBLK + (t // 2 + 1))
                    pe.wait_ge(lo_done, c * S1 + (NCONST + t + 1))
                    proj_slab(t % 2, 2 * (t // 2 % 2), t % 2, L - n)
                    if t == 3:
                        pe.wait_ge(proj_read, c * NBLK + 3)
                        turn(u, 4)
                    if t == 4:
                        pe.wait_ge(t_lo, c * 3 + 1)
                        forward(0, 4)
                        forward(1, 5)
                    if t == 5:
                        pe.wait_ge(y_full, c * 6 + 1)
                        forward(2, 4)
                    if t == 6:
                        pe.wait_ge(proj_read, c * NBLK + 5)
                        scores(0)
                    if t == 7:
                        pe.wait_ge(p_done, c * HC + 1)
                        turn_p()
                    if t == 8:
                        pe.wait_ge(proj_read, c * NBLK + 6)
                        pe.wait_ge(pt_lo, c * HC + 1)
                        turn(v, 6)
                    if t == 9:
                        pe.wait_ge(t_lo, c * 3 + 2)
                        scores(1)
                        pe.wait_ge(ylo_done, c * 6 + 3)
                        inverse(0)
                    if t in (10, 12, 14):
                        hh = (t - 8) // 2
                        pe.wait_ge(p_done, c * HC + hh + 1)
                        attend(hh - 1)
                        turn_p()
                    if t in (11, 13):
                        hh = (t - 7) // 2
                        pe.wait_ge(o_done, c * HC + hh - 1)
                        scores(hh)
                    if t == 11:
                        pe.wait_ge(z_done, c + 1)
                        turn(x1, 4)
                    if t == 12:
                        pe.wait_ge(t_lo, c * 3 + 3)
                        forward(0, 4)
                        forward(1, 5)
                    if t == 13:
                        pe.wait_ge(y_full, c * 6 + 4)
                        forward(2, 4)
                    if t == 15:
                        pe.wait_ge(ylo_done, c * 6 + 6)
                        inverse(NM)
                        pe.wait_ge(o_done, c * HC + 3)
                        attend(3)
                    if t == 16:
                        pe.wait_ge(proj_read, c * NBLK + 10)
                        pe.wait_ge(ya_done, c + 1)
                        fnet_channels(0, 4)
                        fnet_channels(1, 5)
                    if t == 17:
                        pe.wait_ge(n1_lo, c * 3 + 1)
                        fnet_channels(2, 4)
                    if t == 19:
                        pe.wait_ge(n1_lo, c * 3 + 3)
                        fnet_tokens()

            with pe.Fori(0, JB // 2) as i:
                for t in range(S2):
                    b, part = t % 9 // 3, t % 3
                    m = t // 3
                    pair = 2 * ((2 * m + (part == 2)) % 4)
                    if part == 0:
                        pe.wait_ge(gate_done, i * 6 + (m + 1))
                        if m == 0:
                            pe.wait_ge(proj_read, NBLK * CH + 1)
                        if m == 1:
                            pe.wait_ge(yb_done, CH)
                    if part == 2:
                        pe.wait_ge(br_read, i * 6 + (m + 1))
                        if m == 0:
                            pe.wait_ge(proj_read, NBLK * CH + 2)
                        pe.wait_ge(blo_done, b + 1)
                    pe.wait_ge(lo_done, i * S2 + (NCONST + W2 + t + 1))
                    if part < 2:
                        proj_slab(t % 2, pair, part, NM)
                    else:
                        for nt in range(2):
                            for k in range(8):
                                last = three(ps[:, pair + nt, 0:NG], w_hi[:, t % 2, k, 128 * nt:128 * nt + 128],
                                             w_lo[:, t % 2, k, 128 * nt:128 * nt + 128], yb_hi[:, b, k, :], yb_lo[:, b, k, :],
                                             k == 0, k == 7)
                        last.then_inc(slab_used, 1)

            with pe.Fori(0, JB // 2) as i:
                for t in range(4):
                    if t % 2 == 0:
                        pe.wait_ge(h_sum, i * 2 + (t // 2 + 1))
                    if t == 0:
                        pe.wait_ge(gate_done, 3 * JB + 2)
                        pe.wait_ge(mlo_done, JB // 2)
                    if t == 1:
                        pe.wait_ge(mlo_done, JB)
                    pe.wait_ge(lo_done, i * 4 + (NCONST + W3 + t + 1))
                    for tt in range(2):
                        for k in range(8):
                            kk = 8 * (t % 2) + k
                            last = three(ps[:, 2 * (t // 2) + tt, 0:CC], m_hi[:, kk, 128 * tt:128 * tt + 128],
                                         m_lo[:, kk, 128 * tt:128 * tt + 128], w_hi[:, t % 2, k, :], w_lo[:, t % 2, k, :],
                                         kk == 0, kk == KT - 1)
                    last.then_inc(slab_used, 1)

        @block.scalar
        def _(act):
            A = nc.scalar.activation

            def split(where, par, w):
                slot, landed = where
                act.wait_ge(w_landed[slot], landed)
                act.wait_ge(slab_used, w - 1)
                A(w_hi[:, par, :, :].rearrange("p k n -> p (k n)"), raw[:, slot, :], ACT.Copy).then_inc(hi_done, 1)

            def split_const(i, dst, n):
                act.wait_ge(w_landed[i], 16)
                A(dst, raw[:, i, 0:n], ACT.Copy).then_inc(hi_done, 1)

            split_const(0, filt_hi[:, :, :, :].rearrange("p a b n -> p (a b n)"), 6 * L)
            act.wait_ge(x_landed, 48)
            for t, (p, n) in enumerate(TOK):
                if t:
                    act.wait_ge(x_sq, t)
                A(ps[0:n, 0:4, :].rearrange("p a n -> p (a n)"), xin[0:n, t, :], ACT.Square,
                  accum_out=stat[0:n, t:t + 1]).then_inc(x_sq, 1)
            act.wait_ge(x_var, 3)
            for t, (p, n) in enumerate(TOK):
                last = A(stat[0:n, 8 + t:9 + t], stat[0:n, 4 + t:5 + t], ACT.Sqrt)
            last.then_inc(x_std, 1)
            for layer in range(3):
                act.wait_ge(mlp_red, layer + 1)
                A(hid[:, :], red[:, 0, :], ACT.Sin).then_inc(mlp_sin, 1)
            for k in range(KT):
                act.wait_ge(xt_mm, k + 1)
                ins = A(xn_hi[:, k, :], ps[:, k % 4, 0:L], ACT.Copy, scale=params[:, NGC + k:NGC + k + 1])
                ins.then_inc(xt_hi, 1)
            with act.Fori(0, CH) as c:
                act.wait_ge(dec_landed, c * 16 + 16)
                A(absd[:, :, :, :], absd[:, :, :, :], ACT.Abs).then_inc(dec_abs, 1)
                act.wait_ge(dec_abs, c + 1)
                for j, t in enumerate(FORDER):
                    n = TOK[t][1]
                    if j == 2:
                        act.wait_ge(h4_read, c * 3 + 1)
                    A(envel[0:n, j % 2, :, :, :], absd[0:n, :, :, :], ACT.Exp, scale=negt[0:n, t:t + 1]).then_inc(env_done, 1)
                for j, t in enumerate(FORDER):
                    n = TOK[t][1]
                    act.wait_ge(sd_done, c * 3 + j + 1)
                    A(sd_hi[0:n, t, :, :, :], sd[0:n, :, :, :], ACT.Copy).then_inc(sdhi_done, 1)
                act.wait_ge(k_written, c * 32 + 16)
                for f, (fp, fn) in enumerate(TOK):
                    for ri in range(2):
                        e = 2 * f + ri
                        act.wait_ge(k_mm, c * 6 + e + 1)
                        dst = kstage[:, :, f, ri, :] if f < 2 else kmstage[:, :, ri, :]
                        A(dst, ps[0:fn, e % 4, :].rearrange("p (o n) -> p o n", o=2), ACT.Copy,
                          scale=2.0 / FFT_N).then_inc(k_evac, 1)
            split_const(1, sym_hi[:, :, :, :].rearrange("p a b n -> p (a b n)"), 6 * L)
            split_const(2, fch_hi[:, :, :].rearrange("p a n -> p (a n)"), 4 * CC)
            split_const(3, ftok_hi[:, :, :, :].rearrange("p a b n -> p (a b n)"), 6 * NG)
            for w in range(2):
                act.wait_ge(w_landed[w], 32)
                A(w_hi[:, w, :, :].rearrange("p k n -> p (k n)"), raw[:, w, :], ACT.Copy).then_inc(hi_done, 1)

            act.wait_ge(k_written, 16 + 32 * CH)

            def evac(c, name, b):
                bank = 2 * (b % 2)
                act.wait_ge(slab_used, c * S1 + (2 * b + 2))
                src = ps[:, bank:bank + 2, 0:L]
                src16 = ps[:, bank:bank + 2, 0:NG]
                if name in ("u", "x1", "x2"):
                    dst = {"u": u, "x1": x1, "x2": x2}[name]
                    t0 = {"u": 0, "x1": 8, "x2": 16}[name]
                    for i in range(2):
                        ins = A(dst[:, i, :], ps[:, bank + i, 0:L], ACT.Identity,
                                bias=params[:, bass.ds(c * 2 + (CB + t0 + i), 1)],
                                scale=params[:, bass.ds(c * 2 + (CW + 24 + t0 + i), 1)])
                elif name == "q":
                    for i in range(2):
                        ins = A(q_hi[:, i, :].rearrange("p (r n) -> p r n", r=4),
                                ps[:, bank + i, 0:NG].rearrange("p (r n) -> p r n", r=4)[:, :, ::-1], ACT.Copy, scale=0.125)
                elif name == "k":
                    A(k_hi[:, :, 0:L], src, ACT.Copy)
                    ins = A(k_hi[:, :, L:L + NM], ps[:, bank:bank + 2, 0:NM], ACT.Copy)
                elif name == "fin":
                    ins = A(fi_hi[:, :, :], src, ACT.Copy)
                else:
                    act.wait_ge(proj_read, c * NBLK + {"hgate": 2, "ngate": 9, "fgate": 11}[name])
                    ins = A(gexp[:, :, :], src16, ACT.Exp, scale=-1.0)
                ins.then_inc(a_ev, 1)

            def turned(n_th, done, dst, bank, ready, w=CC):
                act.wait_ge(ready, n_th)
                A(dst[:, 0:2, :], ps[:, bank, :].rearrange("p (t n) -> p t n", t=2), ACT.Copy)
                A(dst[0:NM, 2, :], ps[0:NM, bank + 1, 0:w], ACT.Copy).then_inc(done, 1)

            def spectra(c, fs, order):
                for f in fs:
                    n = TOK[f][1]
                    act.wait_ge(y_full, c * 6 + (3 * order + f + 1))
                    A(y_hi[0:n, f, :, :], prod[0:n, 2, :, :], ACT.Copy).then_inc(yhi_done, 1)

            def soft(c, hh):
                act.wait_ge(smax_done, c * HC + hh + 1)
                for a in range(2):
                    ins = A(sco[:, a, :], sco[:, a, :], ACT.Exp, bias=stat[:, 2 + a:3 + a], accum_out=stat[:, 4 + a:5 + a])
                ins.then_inc(exp_done, 1)

            with act.Fori(0, CH) as c:
                for t in range(S1):
                    split(slot_main(c, t + 2), t % 2, c * S1 + (t + 2))
                    if t % 2 and BLOCKS[t // 2][0] != "v":
                        evac(c, BLOCKS[t // 2][0], t // 2)
                    if t == 3:
                        turned(c * 3 + 1, t_hi, uT_hi, 4, t_mm)
                    if t == 4:
                        spectra(c, (0, 1), 0)
                    if t == 5:
                        spectra(c, (2,), 0)
                    if t == 6:
                        soft(c, 0)
                    if t == 8:
                        turned(c * 3 + 2, t_hi, vT_hi, 6, t_mm)
                    if t in (7, 10, 12, 14):
                        turned(c * HC + {7: 1, 10: 2, 12: 3, 14: 4}[t], pt_hi, pT_hi, 6, pt_mm, NG)
                    if t == 11:
                        turned(c * 3 + 3, t_hi, uT_hi, 4, t_mm)
                    if t in (9, 11, 13):
                        soft(c, (t - 7) // 2)
                    if t == 12:
                        spectra(c, (0, 1), 1)
                    if t == 13:
                        spectra(c, (2,), 1)
                    if t == 16:
                        for f in range(2):
                            act.wait_ge(n1_mm, c * 3 + f + 1)
                            A(p2_hi[:, f, :, :], ps[:, 4 + f, :].rearrange("p (r n) -> p r n", r=2), ACT.Copy).then_inc(n1_hi, 1)
                    if t == 17:
                        act.wait_ge(n1_mm, c * 3 + 3)
                        A(p2_hi[0:NM, 2, :, :], ps[0:NM, 4, :].rearrange("p (r n) -> p r n", r=2), ACT.Copy).then_inc(n1_hi, 1)

            A(stat[:, 13:14], params[:, 0:1], ACT.Copy).then_inc(gate_done, 2)
            for b in range(3):
                act.wait_ge(y_landed[b], 16)
                A(yb_hi[:, b, :, :].rearrange("p k n -> p (k n)"), y_raw[:, b, :], ACT.Copy).then_inc(bhi_done, 1)
            with act.Fori(0, JB // 2) as i:
                for t in range(S2):
                    split(slot_merge(i, t + 2), t % 2, i * S2 + (W2 + t + 2))
                    m = t // 3
                    pair = 2 * ((2 * m) % 4)
                    if t % 3 == 1:
                        act.wait_ge(slab_used, i * S2 + (W2 + t + 1))
                        act.wait_ge(br_read, i * 6 + (m + 1))
                        A(mgate[:, m % 2, :, :], ps[:, pair:pair + 2, 0:NG], ACT.Sigmoid).then_inc(gate_done, 1)
                    if t % 9 == 8:
                        jj = t // 9
                        act.wait_ge(msum_done, i * 2 + (jj + 1))
                        A(m_hi[:, bass.ds(i * 4 + 2 * jj, 2), :], msum[:, :, :], ACT.Copy).then_inc(mhi_done, 1)
            with act.Fori(0, JB // 2 - 1) as i:
                for t in range(4):
                    split(slot_out(i, t + 2), t % 2, i * 4 + (W3 + t + 2))
            for t in range(2):
                split(slot_out(JB // 2 - 1, t + 2), t % 2, NW - 2 + t)
            act.wait_ge(h_sum, JB + 2)
            for tt in range(2):
                if tt:
                    act.wait_ge(f_sq, tt)
                A(sq[:, :], h[:, tt, :], ACT.Square, accum_out=stat[:, tt:tt + 1]).then_inc(f_sq, 1)
                act.wait_ge(f_var, tt + 1)
                A(stat[:, 8 + tt:9 + tt], stat[:, 4 + tt:5 + tt], ACT.Sqrt).then_inc(f_std, 1)

        @block.vector
        def _(dve):
            V = nc.vector

            def lo_part(dst, src, hi):
                return V.tensor_tensor(dst, src, hi.bitcast(F32), ALU.subtract)

            def split(where, par, w):
                dve.wait_ge(hi_done, w + (NCONST + 1))
                lo_part(w_lo[:, par, :, :].rearrange("p k n -> p (k n)"), raw[:, where[0], :],
                        w_hi[:, par, :, :].rearrange("p k n -> p (k n)")).then_inc(lo_done, 1)

            def split_const(i, dst, hi, n):
                dve.wait_ge(hi_done, i + 1)
                lo_part(dst, raw[:, i, 0:n], hi).then_inc(lo_done, 1)

            class turn:
                n, c, per = 0, None, 0

            def link(ins):
                turn.n += 1
                ins.then_inc(dve_link, 1)
                dve.wait_ge(dve_link, turn.n if turn.c is None else turn.c * turn.per + turn.n)

            def enter(c, per):
                turn.c, turn.per, turn.before = c, per, turn.n

            def leave(times):
                assert turn.n - turn.before == turn.per, turn.n - turn.before
                turn.c, turn.n = None, turn.before + times * turn.per

            def flat4(t_):
                return t_[:, :, :, :].rearrange("p a b n -> p (a b n)")

            split_const(0, flat4(filt_lo), flat4(filt_hi), 6 * L)
            dve.wait_ge(x_sq, 3)
            for t, (p, n) in enumerate(TOK):
                V.tensor_scalar(stat[0:n, 4 + t:5 + t], stat[0:n, t:t + 1], 1.0 / D, EPS, ALU.mult, ALU.add).then_inc(x_var, 1)

            def mlp_layer(layer):
                dve.wait_ge(mlp_mm, layer + 1)
                link(V.tensor_scalar(red[:, 0, :], ps[0:HID, 7, 0:L], mlpw[:, 3 * HID + layer:3 * HID + layer + 1],
                                     mlpw[:, 3 * HID + 3:3 * HID + 4], ALU.add, ALU.mult))
                link(V.tensor_scalar(red[:, 1, :], red[:, 0, :], 1.0 / TWO_PI, MAGIC, ALU.mult, ALU.add))
                link(V.tensor_scalar(red[:, 2, :], red[:, 1, :], -MAGIC, None, ALU.add))
                c1 = float(np.float32(6.28125))
                c2 = float(np.float32(TWO_PI - c1))
                c3 = float(np.float32(TWO_PI - c1 - c2))
                link(V.scalar_tensor_tensor(red[:, 1, :], red[:, 2, :], -c1, red[:, 0, :], ALU.mult, ALU.add))
                link(V.scalar_tensor_tensor(red[:, 3, :], red[:, 2, :], -c2, red[:, 1, :], ALU.mult, ALU.add))
                link(V.scalar_tensor_tensor(red[:, 1, :], red[:, 2, :], -c3, red[:, 3, :], ALU.mult, ALU.add))
                V.tensor_scalar(red[:, 0, :], red[:, 1, :], CLAMP, -CLAMP, ALU.min, ALU.max).then_inc(mlp_red, 1)

            mlp_layer(0)
            dve.wait_ge(x_std, 1)
            for t, (p, n) in enumerate(TOK):
                link(V.reciprocal(stat[0:n, 12 + t:13 + t], stat[0:n, 8 + t:9 + t]))
            for t, (p, n) in enumerate(TOK):
                V.tensor_scalar(xin[0:n, t, :], xin[0:n, t, :], stat[0:n, 12 + t:13 + t], None, ALU.mult).then_inc(x_scaled, 1)
            mlp_layer(1)
            mlp_layer(2)
            for k in range(KT):
                dve.wait_ge(xt_hi, k + 1)
                ins = V.scalar_tensor_tensor(xn_lo[:, k, :], ps[:, k % 4, 0:L], params[:, NGC + k:NGC + k + 1],
                                             xn_hi[:, k, :].bitcast(F32), ALU.mult, ALU.subtract)
                ins.then_inc(xt_lo, 1)
            V.memset(stat[:, 15:16], 0.0).then_inc(k_evac, 4)
            with dve.Fori(0, CH) as c:
                enter(c, 1)
                for j, t in enumerate(FORDER):
                    n = TOK[t][1]
                    b = 4 + 2 * (j % 2)
                    dve.wait_ge(env_done, c * 3 + j + 1)
                    if t == 2:
                        link(V.memset(envel[0:1, j % 2, :, 1, :], 0.0))
                    dve.wait_ge(h4_mm, c * 3 + j + 1)
                    V.tensor_tensor(hm[0:n, :, :, :].rearrange("p o d n -> p o (d n)"), ps[0:n, b:b + 2, :],
                                    envel[0:n, j % 2, :, :, :].rearrange("p o d n -> p o (d n)"), ALU.mult).then_inc(h4_read, 1)
                    dve.wait_ge(h4_read, c * 3 + j + 1)
                    V.tensor_tensor(sd[0:n, 0, :, :], hm[0:n, :, 0, :], hm[0:n, :, 1, :], ALU.add)
                    V.tensor_tensor(sd[0:n, 1, :, :], hm[0:n, :, 0, :], hm[0:n, :, 1, :], ALU.subtract).then_inc(sd_done, 1)
                    dve.wait_ge(sdhi_done, c * 3 + j + 1)
                    lo_part(sd_lo[0:n, t, :, :, :], sd[0:n, :, :, :], sd_hi[0:n, t, :, :, :]).then_inc(sdlo_done, 1)
            leave(CH)
            split_const(1, flat4(sym_lo), flat4(sym_hi), 6 * L)
            split_const(2, fch_lo[:, :, :].rearrange("p a n -> p (a n)"), fch_hi[:, :, :].rearrange("p a n -> p (a n)"), 4 * CC)
            split_const(3, flat4(ftok_lo), flat4(ftok_hi), 6 * NG)
            V.memset(stat[:, 11:12], 0.0).then_inc(proj_read, 2)
            for w in range(2):
                split((w,), w, w)

            def evac(c, name, b):
                bank = 2 * (b % 2)
                src = ps[:, bank:bank + 2, 0:L]
                src16 = ps[:, bank:bank + 2, 0:NG]
                if name == "v":
                    dve.wait_ge(slab_used, c * S1 + (2 * b + 2))
                    V.tensor_copy(v[:, :, :], src).then_inc(proj_read, 1)
                    return
                dve.wait_ge(a_ev, c * (NBLK - 1) + (b + 1 if b < 3 else b))
                if name in ("u", "x1", "x2"):
                    dst = {"u": u, "x1": x1, "x2": x2}[name]
                    t0 = {"u": 0, "x1": 8, "x2": 16}[name]

                    def tap(j, i, to, frm):
                        return V.scalar_tensor_tensor(dst[:, i, to], ps[:, bank + i, frm],
                                                      params[:, bass.ds(c * 2 + (CW + 24 * j + t0 + i), 1)], dst[:, i, to],
                                                      ALU.mult, ALU.add)

                    tap(0, 0, slice(1, L), slice(0, L - 1))
                    link(tap(0, 1, slice(1, L), slice(0, L - 1)))
                    tap(2, 0, slice(0, L - 1), slice(1, L))
                    ins = tap(2, 1, slice(0, L - 1), slice(1, L))
                elif name == "q":
                    for i in range(2):
                        ins = V.scalar_tensor_tensor(q_lo[:, i, :].rearrange("p (r n) -> p r n", r=4),
                                                     ps[:, bank + i, 0:NG].rearrange("p (r n) -> p r n", r=4)[:, :, ::-1], 0.125,
                                                     q_hi[:, i, :].rearrange("p (r n) -> p r n", r=4).bitcast(F32),
                                                     ALU.mult, ALU.subtract)
                elif name == "k":
                    lo_part(k_lo[:, :, 0:L], src, k_hi[:, :, 0:L])
                    ins = lo_part(k_lo[:, :, L:L + NM], ps[:, bank:bank + 2, 0:NM], k_hi[:, :, L:L + NM])
                elif name == "fin":
                    ins = lo_part(fi_lo[:, :, :], src, fi_hi[:, :, :])
                else:
                    link(V.tensor_scalar(gexp[:, :, :], gexp[:, :, :], 1.0, None, ALU.add))
                    link(V.reciprocal(gexp[:, :, :], gexp[:, :, :]))
                    ins = V.tensor_tensor(gate[:, :, :], src16, gexp[:, :, :], ALU.mult)
                ins.then_inc(proj_read, 1)

            def turned(n_th, hi_ready, done, dst, hi, bank, w=CC):
                dve.wait_ge(hi_ready, n_th)
                lo_part(dst[:, 0:2, :], ps[:, bank, :].rearrange("p (t n) -> p t n", t=2), hi[:, 0:2, :])
                lo_part(dst[0:NM, 2, :], ps[0:NM, bank + 1, 0:w], hi[0:NM, 2, :]).then_inc(done, 1)

            def spectra(c, fs, order):
                for f in fs:
                    n = TOK[f][1]
                    nth = 3 * order + f + 1
                    if f == 0:
                        dve.wait_ge(k_landed, c * 64 + 32 * (order + 1))
                    dve.wait_ge(fwd_mm, c * 6 + nth)
                    bank = ps[0:n, 4 + f % 2, :].rearrange("p (r n) -> p r n", r=2)
                    V.tensor_tensor(prod[0:n, 0, :, :], bank, kspec[0:n, f, :, :], ALU.mult)
                    link(V.tensor_tensor(prod[0:n, 1, :, :], bank, kspec[0:n, f, ::-1, :], ALU.mult))
                    V.tensor_tensor(prod[0:n, 2, 0, :], prod[0:n, 0, 0, :], prod[0:n, 0, 1, :], ALU.subtract)
                    V.tensor_tensor(prod[0:n, 2, 1, :], prod[0:n, 1, 0, :], prod[0:n, 1, 1, :], ALU.add).then_inc(y_full, 1)
                    dve.wait_ge(yhi_done, c * 6 + nth)
                    lo_part(y_lo[0:n, f, :, :], prod[0:n, 2, :, :], y_hi[0:n, f, :, :]).then_inc(ylo_done, 1)

            def soft(c, hh):
                if hh == 0:
                    dve.wait_ge(b_ready, c + 1)
                dve.wait_ge(s_mm, c * HC + hh + 1)
                V.memset(stat[:, 11:12], 0.0)
                for a in range(2):
                    b0 = NM + 2 * GRID_W if a == 0 else 0
                    ins = V.tensor_tensor_reduce(sco[:, a, :], ps[:, 6 + a, 0:L], bias_t[:, hh, b0:b0 + L], 1.0, -3.0e38,
                                                 ALU.add, ALU.max, stat[:, 6 + a:7 + a])
                link(ins)
                V.tensor_scalar(stat[:, 2:4], stat[:, 6:8], -1.0, None, ALU.mult).then_inc(smax_done, 1)
                dve.wait_ge(exp_done, c * HC + hh + 1)
                link(V.reciprocal(stat[:, 8:10], stat[:, 4:6]))
                for a in range(2):
                    ins = V.tensor_scalar(sco[:, a, :], sco[:, a, :], stat[:, 8 + a:9 + a], None, ALU.mult)
                ins.then_inc(p_done, 1)

            def attended(c, hh):
                r = slice(64 * (hh % 2), 64 * (hh % 2) + 64)
                dve.wait_ge(pv_mm, c * HC + hh + 1)
                V.tensor_copy(o[r, hh // 2, :].rearrange("p (r n) -> p r n", r=4),
                              ps[r, 7, NG:2 * NG].rearrange("p (r n) -> p r n", r=4)[:, :, ::-1]).then_inc(o_done, 1)

            with dve.Fori(0, CH) as c:
                enter(c, 26)
                for t in range(S1):
                    split(slot_main(c, t + 2), t % 2, c * S1 + (t + 2))
                    if t % 2:
                        evac(c, BLOCKS[t // 2][0], t // 2)
                    if t == 3:
                        turned(c * 3 + 1, t_hi, t_lo, uT_lo, uT_hi, 4)
                    if t == 4:
                        spectra(c, (0, 1), 0)
                    if t == 5:
                        spectra(c, (2,), 0)
                    if t == 6:
                        soft(c, 0)
                    if t == 8:
                        turned(c * 3 + 2, t_hi, t_lo, vT_lo, vT_hi, 6)
                    if t in (7, 10, 12, 14):
                        turned(c * HC + {7: 1, 10: 2, 12: 3, 14: 4}[t], pt_hi, pt_lo, pT_lo, pT_hi, 6, NG)
                    if t in (10, 12, 14):
                        attended(c, (t - 10) // 2)
                    if t in (9, 11, 13):
                        soft(c, (t - 7) // 2)
                    if t == 9:
                        dve.wait_ge(inv_mm, c * 2 + 1)
                        for i in range(2):
                            ins = V.scalar_tensor_tensor(u[:, i, :], u[:, i, :], params[:, bass.ds(c * 2 + (SK + i), 1)],
                                                         ps[:, 4 + i, 0:L], ALU.mult, ALU.add)
                        link(ins)
                        V.tensor_tensor(x1[:, :, :], x1[:, :, :], u[:, :, :], ALU.mult).then_inc(z_done, 1)
                    if t == 11:
                        turned(c * 3 + 3, t_hi, t_lo, uT_lo, uT_hi, 4)
                    if t == 12:
                        spectra(c, (0, 1), 1)
                    if t == 13:
                        spectra(c, (2,), 1)
                    if t == 15:
                        dve.wait_ge(inv_mm, c * 2 + 2)
                        for i in range(2):
                            ins = V.scalar_tensor_tensor(u[:, i, NM:L], x1[:, i, NM:L],
                                                         params[:, bass.ds(c * 2 + (SK + 8 + i), 1)],
                                                         ps[:, 4 + i, 0:NG], ALU.mult, ALU.add)
                        link(ins)
                        link(V.tensor_tensor(u[:, :, NM:L], u[:, :, NM:L], x2[:, :, NM:L], ALU.mult))
                        dve.wait_ge(y_written, c * 48 + 16)
                        V.tensor_tensor(ystage[:, :, :], u[:, :, NM:L], gate[:, :, :], ALU.mult).then_inc(ya_done, 1)
                        attended(c, 3)
                    if t == 16:
                        for f in range(2):
                            dve.wait_ge(n1_hi, c * 3 + f + 1)
                            lo_part(p2_lo[:, f, :, :], ps[:, 4 + f, :].rearrange("p (r n) -> p r n", r=2),
                                    p2_hi[:, f, :, :]).then_inc(n1_lo, 1)
                    if t == 17:
                        dve.wait_ge(n1_hi, c * 3 + 3)
                        lo_part(p2_lo[0:NM, 2, :, :], ps[0:NM, 4, :].rearrange("p (r n) -> p r n", r=2),
                                p2_hi[0:NM, 2, :, :]).then_inc(n1_lo, 1)
                        dve.wait_ge(y_written, c * 48 + 32)
                        dve.wait_ge(proj_read, c * NBLK + 11)
                        V.tensor_tensor(ystage[:, :, :], o[:, :, :], gate[:, :, :], ALU.mult).then_inc(yc_done, 1)
                    if t == 19:
                        dve.wait_ge(n2_mm, c + 1)
                        dve.wait_ge(y_written, c * 48 + 48)
                        dve.wait_ge(proj_read, c * NBLK + 12)
                        V.tensor_tensor(ystage[:, :, :], ps[:, 4, :].rearrange("p (i n) -> p i n", i=2), gate[:, :, :],
                                        ALU.mult).then_inc(yb_done, 1)
            leave(CH)

            V.memset(stat[:, 10:11], 0.0).then_inc(br_read, 2)
            V.memset(stat[:, 14:15], 0.0).then_inc(h_sum, 2)
            for b in range(3):
                dve.wait_ge(bhi_done, b + 1)
                lo_part(yb_lo[:, b, :, :].rearrange("p k n -> p (k n)"), y_raw[:, b, :],
                        yb_hi[:, b, :, :].rearrange("p k n -> p (k n)")).then_inc(blo_done, 1)
            with dve.Fori(0, JB // 2) as i:
                enter(i, 2)
                for t in range(S2):
                    split(slot_merge(i, t + 2), t % 2, i * S2 + (W2 + t + 2))
                    m = t // 3
                    pair = 2 * ((2 * m + 1) % 4)
                    if t % 3 == 2:
                        dve.wait_ge(slab_used, i * S2 + (W2 + t + 1))
                        dve.wait_ge(gate_done, i * 6 + (m + 3))
                        src = ps[:, pair:pair + 2, 0:NG]
                        if m % 3 == 0:
                            V.tensor_tensor(msum[:, :, :], mgate[:, m % 2, :, :], src, ALU.mult).then_inc(br_read, 1)
                        else:
                            V.tensor_tensor(mterm[:, :, :], mgate[:, m % 2, :, :], src, ALU.mult).then_inc(br_read, 1)
                            dve.wait_ge(br_read, i * 6 + (m + 3))
                            ins = V.tensor_tensor(msum[:, :, :], msum[:, :, :], mterm[:, :, :], ALU.add)
                            if m % 3 == 1:
                                link(ins)
                            else:
                                ins.then_inc(msum_done, 1)
                    if t % 9 == 8:
                        jj = t // 9
                        dve.wait_ge(mhi_done, i * 2 + (jj + 1))
                        lo_part(m_lo[:, bass.ds(i * 4 + 2 * jj, 2), :], msum[:, :, :],
                                m_hi[:, bass.ds(i * 4 + 2 * jj, 2), :]).then_inc(mlo_done, 1)
            leave(JB // 2)

            dve.wait_ge(h_landed, 48)

            def add_block(i, nb):
                dve.wait_ge(slab_used, i * 4 + (W3 + 2 * nb + 2))
                cols = h[:, :, bass.ds(i * (2 * CC) + CC * nb, CC)]
                V.tensor_tensor(cols, cols, ps[:, 2 * nb:2 * nb + 2, 0:CC], ALU.add).then_inc(h_sum, 1)

            with dve.Fori(0, JB // 2 - 1) as i:
                for t in range(4):
                    split(slot_out(i, t + 2), t % 2, i * 4 + (W3 + t + 2))
                    if t % 2:
                        add_block(i, t // 2)
            for t in range(4):
                if t < 2:
                    split(slot_out(JB // 2 - 1, t + 2), t % 2, NW - 2 + t)
                if t % 2:
                    add_block(JB // 2 - 1, t // 2)
            for tt in range(2):
                dve.wait_ge(f_sq, tt + 1)
                V.tensor_scalar(stat[:, 4 + tt:5 + tt], stat[:, tt:tt + 1], 1.0 / D, EPS, ALU.mult, ALU.add).then_inc(f_var, 1)
                dve.wait_ge(f_std, tt + 1)
                link(V.reciprocal(stat[:, 6 + tt:7 + tt], stat[:, 8 + tt:9 + tt]))
                V.scalar_tensor_tensor(h[:, tt, :], h[:, tt, :], stat[:, 6 + tt:7 + tt], fg[:, :], ALU.mult,
                                       ALU.mult).then_inc(f_done, 1)


def slab_stream(w_in, wa, wb, wc, wo):
    def slab(w, k0, c0):
        return w[k0:k0 + 1024, c0:c0 + CC].reshape(8, 128, CC).transpose(1, 0, 2).reshape(128, 8 * CC)

    slabs = []
    for c in range(CH):
        for _, col, _ in BLOCKS:
            for half in range(2):
                slabs.append(slab(w_in, 1024 * half, col + CC * c))
    for j in range(JB):
        for b, w in enumerate((wa, wb, wc)):
            for half in range(2):
                slabs.append(slab(w_in, 1024 * half, 10 * C + D * b + CC * j))
            slabs.append(slab(w, 0, CC * j))
    for j in range(JB):
        for half in range(2):
            slabs.append(slab(wo, 1024 * half, CC * j))
    assert len(slabs) == NW
    return np.stack(slabs)


def kernel(x, meta_tokens, norm_g, w_in, hy_conv_w, hy_conv_b, hy_flt_w1, hy_flt_b1, hy_flt_w2, hy_flt_b2, hy_flt_w3,
           hy_flt_b3, hy_flt_w4, hy_flt_freq, hy_decay, hy_skip, na_rpb, na_meta_bias, w_branch_a, w_branch_b,
           w_branch_c, w_out, final_g):
    import concourse.bacc as bacc
    from concourse.bass_utils import run_bass_kernel_spmd

    def host(a):
        return np.asarray(a)

    tables, zT, negt, mask, ident = constants()
    by_tile = lambda a, n: host(a).reshape(-1, n, 128).transpose(2, 0, 1).reshape(128, -1)
    arrays = {
        "x": host(x)[0],
        "meta": host(meta_tokens),
        "w_stream": slab_stream(host(w_in)[0], host(w_branch_a)[0], host(w_branch_b)[0], host(w_branch_c)[0], host(w_out)[0]),
        "tables": tables,
        "zT": zT,
        "negt_in": negt,
        "mask_in": mask,
        "ident_in": ident,
        "params_in": np.concatenate([by_tile(hy_conv_w, 24), by_tile(hy_conv_b, 24), by_tile(hy_skip, 8),
                                     by_tile(norm_g, 16)], axis=1),
        "mlp_in": np.stack([host(hy_flt_b1)[0], host(hy_flt_b2)[0], host(hy_flt_b3)[0], host(hy_flt_freq)[0]], axis=1),
        "w1": host(hy_flt_w1)[0],
        "w2": host(hy_flt_w2)[0],
        "w3": host(hy_flt_w3)[0],
        "w4": host(hy_flt_w4)[0].reshape(HID, 4, CH, CC).transpose(2, 0, 1, 3).reshape(CH, HID, 4 * CC),
        "decay": host(hy_decay)[0].reshape(4, CH, CC).transpose(1, 0, 2).reshape(CH, 4 * CC),
        "rpb": host(na_rpb)[0].reshape(-1),
        "mbias": host(na_meta_bias)[0].reshape(CH, HC * NM),
        "final_g": host(final_g),
    }
    arrays = {n: np.ascontiguousarray(a) for n, a in arrays.items()}
    nc = bacc.Bacc("TRN2", target_bir_lowering=False, num_devices=1)
    args = {n: nc.dram_tensor(n, a.shape, mybir.dt.from_np(a.dtype), kind="ExternalInput").ap() for n, a in arrays.items()}
    out = nc.dram_tensor("out", [NG, D], F32, kind="ExternalOutput").ap()
    build(nc, out=out, **args)
    r = run_bass_kernel_spmd(nc, [arrays], core_ids=[0])
    return r.results[0]["out"].reshape(1, NG, D)
```

```python
from contextlib import ExitStack
import math

import numpy as np

import concourse.bass as bass
from concourse import mybir

F32 = mybir.dt.float32
F32R = mybir.dt.float32r
ALU = mybir.AluOpType
ACT = mybir.ActivationFunctionType

D = 2048
L = 272
NM = 16
NG = L - NM
C = 1024
CC = 256
CH = C // CC
KT = D // 128
EPS = 1e-6
GRID_W = 64
KW = 16
HEADS = 16
HC = HEADS // CH
RPB_R, RPB_C = 15, 31
HID, EMB = 64, 33
FFT_N = 2 * L
TOK = [(NM, 128), (NM + 128, 128), (0, NM)]
BLOCKS = [("u", 0, L), ("q", 6 * C, NG), ("k", 7 * C, L), ("v", 8 * C, L), ("x1", C, L), ("x2", 2 * C, L),
          ("hgate", 3 * C, NG), ("fin", 4 * C, L), ("ngate", 9 * C, NG), ("fgate", 5 * C, NG)]
NBLK = len(BLOCKS)
S1 = 2 * NBLK
W2 = CH * S1
JB = D // CC
S2 = 18
W3 = W2 + JB // 2 * S2
NW = W3 + 2 * JB
NCONST = 4
STACK = 64 + NM
BRANCHES = (0, 2, 1)
FORDER = (0, 2, 1)
TWO_PI = 2.0 * math.pi
MAGIC = 1.5 * 2.0 ** 23
BT = NM + 6 * GRID_W + NM
CLAMP = 3.1415925


def constants():
    pos = np.arange(L, dtype=np.float64)
    om = TWO_PI * (pos + 0.5) / FFT_N

    def rows(m):
        out = np.zeros((128, 3, m.shape[1]), np.float64)
        for t, (p, n) in enumerate(TOK):
            for row in (0,) if t < 2 else (0, 32, 64):
                out[row:row + n, t] = m[p:p + n]
        return out

    def slab(*parts):
        flat = np.concatenate([p.reshape(128, -1) for p in parts], axis=1)
        out = np.zeros((128, 2048), np.float32)
        out[:, :flat.shape[1]] = flat
        return out

    lag = pos[:, None] * om[None, :]
    half = (pos[:, None] + 0.5) * om[None, :]
    filt = np.stack([rows(np.cos(lag)), rows(-np.sin(lag))], axis=2)
    sym = np.stack([rows(np.cos(half)), rows(-np.sin(half))], axis=2)
    ch = np.arange(CC, dtype=np.float64)
    ang = TWO_PI * ((ch[:, None] * ch[None, :]) % CC) / CC
    fch = np.concatenate([np.cos(ang), np.sin(ang)], axis=1).reshape(2, 128, 2 * CC).transpose(1, 0, 2)
    angl = TWO_PI * ((pos[:, None] * pos[None, NM:]) % L) / L
    norm = 1.0 / math.sqrt(L * CC)
    ftok = np.stack([rows(np.cos(angl) * norm), rows(-np.sin(angl) * norm)], axis=2)
    tables = np.stack([slab(filt), slab(sym), slab(fch), slab(ftok)])

    f32 = np.float32
    t = np.linspace(0.0, 1.0, L, dtype=f32)[:, None]
    bands = (EMB - 1) // 2
    w = f32(TWO_PI) * np.arange(L, dtype=f32)[:, None] / f32(L)
    f = np.linspace(1e-4, bands - 1, bands, dtype=f32)[None, :]
    z = np.concatenate([t, np.cos(f * w), -np.sin(f * w)], axis=-1).astype(f32)
    negt = np.zeros((128, 3), f32)
    for i, (p, n) in enumerate(TOK):
        negt[:n, i] = -t[p:p + n, 0]
    col = np.arange(GRID_W)
    cs = np.clip(col - KW // 2, 0, GRID_W - KW)
    seen = (col[None, :] >= cs[:, None]) & (col[None, :] < cs[:, None] + KW)
    mask = np.where(seen, 0.0, -1e30).astype(f32)
    mask = mask[::-1]
    return tables, np.ascontiguousarray(z.T), negt, np.concatenate([mask, mask]), np.eye(128, dtype=f32)


def build(nc, x, meta, w_stream, tables, zT, negt_in, mask_in, ident_in, params_in, mlp_in, w1, w2, w3, w4,
          decay, rpb, mbias, final_g, out):
    kg_dram = nc.dram_tensor("kspec_grid", [CH, 2, 128, 2 * 2 * CC], F32, kind="Internal").ap()
    km_dram = nc.dram_tensor("kspec_meta", [CH, 2, NM, 2 * CC], F32, kind="Internal").ap()
    y_dram = nc.dram_tensor("branch_y", [3, 128, 2 * CH, NG], F32, kind="Internal").ap()

    at = [(nc.sbuf_base + 63) // 64 * 64]

    def place(name, shape, dt=F32):
        t = nc.alloc_sbuf_tensor_at(name, shape, dt, offset=at[0])
        at[0] += (4 * int(np.prod(shape[1:])) + 63) // 64 * 64
        assert at[0] <= nc.sbuf_usable_end, (name, at[0])
        return t

    params = place("params", [128, 128])
    ident = place("ident", [128, 128])
    negt = place("negt", [128, 3])
    mask = place("mask", [128, GRID_W])
    stat = place("stat", [128, 16])
    raw = place("raw", [128, 4, 8 * CC])
    xn_at = at[0]
    xn_hi = place("xn_hi", [128, KT, L], F32R)
    xn_lo = place("xn_lo", [128, KT, L], F32R)
    xn_end = at[0]
    split_at = at[0]
    w_hi = place("w_hi", [128, 2, 8, CC], F32R)
    w_lo = place("w_lo", [128, 2, 8, CC], F32R)
    split_end = at[0]
    mix_at = at[0]
    sym_hi = place("sym_hi", [128, 3, 2, L], F32R)
    sym_lo = place("sym_lo", [128, 2, 2, L], F32R)
    fch_hi = place("fch_hi", [128, 2, 2 * CC], F32R)
    fch_lo = place("fch_lo", [128, 2, 2 * CC], F32R)
    ftok_hi = place("ftok_hi", [128, 3, 2, NG], F32R)
    ftok_lo = place("ftok_lo", [128, 2, 2, NG], F32R)
    work_at = at[0]
    kspec = place("kspec", [128, 3, 2, CC])
    bias_t = place("bias_t", [128, HC, BT])
    y_hi = place("y_hi", [128, 3, 2, CC], F32R)
    y_lo = place("y_lo", [128, 2, 2, CC], F32R)
    p2_hi, p2_lo = y_hi, y_lo
    uT_hi = place("uT_hi", [128, 3, CC], F32R)
    uT_lo = place("uT_lo", [128, 2, CC], F32R)
    vT_hi = place("vT_hi", [128, 3, CC], F32R)
    vT_lo = place("vT_lo", [128, 2, CC], F32R)
    pT_hi = place("pT_hi", [128, 3, NG], F32R)
    pT_lo = place("pT_lo", [128, 2, NG], F32R)
    qk_at = at[0]
    q_hi = place("q_hi", [128, 2, NG], F32R)
    q_lo = place("q_lo", [128, 2, NG], F32R)
    k_hi = place("k_hi", [128, 2, L + NM], F32R)
    k_lo = place("k_lo", [128, 2, L + NM], F32R)
    qk_end = at[0]
    at[0] = qk_at
    fi_hi = place("fi_hi", [128, 2, L], F32R)
    fi_lo = place("fi_lo", [128, 2, L], F32R)
    at[0] = qk_end
    u = place("u", [128, 2, L])
    x1 = place("x1", [128, 2, L])
    x2 = place("x2", [128, 2, L])
    v = place("v", [128, 2, L])
    o = place("o", [128, 2, NG])
    gate = place("gate", [128, 2, NG])
    gexp = place("gexp", [128, 2, NG])
    prod = place("prod", [128, 3, 2, CC])
    sco = place("sco", [128, 2, L])
    ystage = place("ystage", [128, 2, NG])
    at[0] = work_at
    xin = place("xin", [128, 3, D])
    filt_hi = place("filt_hi", [128, 3, 2, L], F32R)
    filt_lo = place("filt_lo", [128, 2, 2, L], F32R)
    kstage = place("kstage", [128, 2, 2, 2, CC])
    kmstage = place("kmstage", [NM, 2, 2, CC])
    absd = place("absd", [128, 2, 2, 2, CC])
    w4s = place("w4s", [HID, 2, 2, 2, CC])
    hid = place("hid", [HID, L])
    mlp_at = at[0]
    mlpw = place("mlpw", [HID, 3 * HID + 4])
    zt = place("zt", [EMB, L])
    red = place("red", [HID, 4, L])
    at[0] = mlp_at
    hm = place("hm", [128, 2, 2, CC])
    sd = place("sd", [128, 2, 2, CC])
    at[0] = work_at
    sd_hi = place("sd_hi", [128, 3, 2, 2, CC], F32R)
    sd_lo = place("sd_lo", [128, 2, 2, 2, CC], F32R)
    at[0] = split_end - 4 * 8 * CC
    envel = place("envel", [128, 2, 2, 2, CC])
    at[0] = mix_at
    m_hi = place("m_hi", [128, KT, NG], F32R)
    m_lo = place("m_lo", [128, KT, NG], F32R)
    m_end = at[0]
    at[0] = mix_at
    y_raw = place("y_raw", [128, 3, 2 * CH * NG])
    at[0] = m_end
    yb_hi = place("yb_hi", [128, 3, 2 * CH, NG], F32R)
    yb_lo = place("yb_lo", [128, 3, 2 * CH, NG], F32R)
    mgate = place("mgate", [128, 2, 2, NG])
    msum = place("msum", [128, 2, NG])
    mterm = place("mterm", [128, 2, NG])
    at[0] = xn_at
    h = place("h", [128, 2, D])
    fg = place("fg", [128, D])
    at[0] = m_end
    sq = place("sq", [128, D])

    CW, CB, SK, NGC = 0, 72, 96, 112
    with ExitStack() as ctx:
        ps = ctx.enter_context(nc.psum_tensor("ps", [128, 8, 512], F32))

        def sem(name):
            return ctx.enter_context(nc.semaphore(name))

        w_landed = [sem(f"w_landed{i}") for i in range(4)]
        hi_done = sem("hi_done")
        lo_done = sem("lo_done")
        slab_used = sem("slab_used")
        x_landed = sem("x_landed")
        small_landed = sem("small_landed")
        w4_landed = [sem(f"w4_landed{i}") for i in range(2)]
        dec_landed = [sem(f"dec_landed{i}") for i in range(2)]
        mlp_mm = sem("mlp_mm")
        mlp_red = sem("mlp_red")
        mlp_sin = sem("mlp_sin")
        x_sq = sem("x_sq")
        x_var = sem("x_var")
        x_std = sem("x_std")
        x_scaled = sem("x_scaled")
        xt_mm = sem("xt_mm")
        xt_hi = sem("xt_hi")
        xt_lo = sem("xt_lo")
        dec_abs = sem("dec_abs")
        env_done = sem("env_done")
        h4_mm = sem("h4_mm")
        h4_read = sem("h4_read")
        sd_done = sem("sd_done")
        sdhi_done = sem("sdhi_done")
        sdlo_done = sem("sdlo_done")
        k_mm = sem("k_mm")
        k_evac = sem("k_evac")
        k_written = sem("k_written")
        a_ev = sem("a_ev")
        proj_read = sem("proj_read")
        t_mm = sem("t_mm")
        t_hi = sem("t_hi")
        t_lo = sem("t_lo")
        fwd_mm = sem("fwd_mm")
        y_full = sem("y_full")
        yhi_done = sem("yhi_done")
        ylo_done = sem("ylo_done")
        inv_mm = sem("inv_mm")
        z_done = sem("z_done")
        s_mm = sem("s_mm")
        smax_done = sem("smax_done")
        exp_done = sem("exp_done")
        p_done = sem("p_done")
        pt_mm = sem("pt_mm")
        pt_hi = sem("pt_hi")
        pt_lo = sem("pt_lo")
        pv_mm = sem("pv_mm")
        o_done = sem("o_done")
        n1_mm = sem("n1_mm")
        n1_hi = sem("n1_hi")
        n1_lo = sem("n1_lo")
        n2_mm = sem("n2_mm")
        ya_done = sem("ya_done")
        yb_done = sem("yb_done")
        yc_done = sem("yc_done")
        y_written = sem("y_written")
        k_landed = sem("k_landed")
        b_landed = sem("b_landed")
        b_ready = sem("b_ready")
        y_landed = [sem(f"y_landed{i}") for i in range(3)]
        bhi_done = sem("bhi_done")
        blo_done = sem("blo_done")
        gate_done = sem("gate_done")
        br_read = sem("br_read")
        msum_done = sem("msum_done")
        mhi_done = sem("mhi_done")
        mlo_done = sem("mlo_done")
        h_landed = sem("h_landed")
        h_sum = sem("h_sum")
        f_sq = sem("f_sq")
        f_var = sem("f_var")
        f_std = sem("f_std")
        f_done = sem("f_done")
        out_written = sem("out_written")
        zeroed = sem("zeroed")
        dve_link = sem("dve_link")

        block = ctx.enter_context(nc.Block())
        SMALL = 10

        @block.sync
        def _(sp):
            sp.dma_start(raw[:, 0, :], tables[0]).then_inc(w_landed[0], 16)
            sp.dma_start(xin[:, 0, :], x[0:128, :]).then_inc(x_landed, 16)
            sp.dma_start(xin[:, 1, :], x[128:256, :]).then_inc(x_landed, 16)
            sp.dma_start(xin[0:NM, 2, :], meta).then_inc(x_landed, 16)
            for i in range(1, NCONST):
                sp.dma_start(raw[:, i, :], tables[i]).then_inc(w_landed[i], 16)
            with sp.Fori(0, CH) as c:
                for t in range(S1):
                    sp.wait_ge(lo_done, c * S1 + t + 1)
                    sp.dma_start(raw[:, t % 4, :], w_stream[bass.ds(c * S1 + t, 1), :, :].rearrange("a p n -> p (a n)")
                                 ).then_inc(w_landed[t % 4], 16)
            with sp.Fori(0, JB // 2) as i:
                for t in range(S2):
                    sp.wait_ge(lo_done, i * S2 + (W2 + t + 2))
                    sp.dma_start(raw[:, t % 3, :],
                                 w_stream[bass.ds(i * S2 + (W2 + t), 1), :, :].rearrange("a p n -> p (a n)")
                                 ).then_inc(w_landed[t % 3], 16)
            with sp.Fori(0, JB // 2) as i:
                for t in range(4):
                    sp.wait_ge(lo_done, i * 4 + (W3 + t + 2))
                    sp.dma_start(raw[:, t % 4, :],
                                 w_stream[bass.ds(i * 4 + (W3 + t), 1), :, :].rearrange("a p n -> p (a n)")
                                 ).then_inc(w_landed[t % 4], 16)
            for tt in range(2):
                sp.wait_ge(f_done, tt + 1)
                sp.dma_start(out[128 * tt:128 * tt + 128, :], h[:, tt, :]).then_inc(out_written, 16)
            sp.wait_ge(out_written, 32)

        @block.gpsimd
        def _(pool):
            pool.dma_start(zt[:, :], zT).then_inc(small_landed, 16)
            pool.dma_start(mlpw[0:EMB, 0:HID], w1).then_inc(small_landed, 16)
            pool.dma_start(mlpw[:, HID:2 * HID], w2).then_inc(small_landed, 16)
            pool.dma_start(mlpw[:, 2 * HID:3 * HID], w3).then_inc(small_landed, 16)
            pool.dma_start(mlpw[:, 3 * HID:], mlp_in).then_inc(small_landed, 16)
            pool.dma_start(negt[:, :], negt_in).then_inc(small_landed, 16)
            pool.dma_start(ident[:, :], ident_in).then_inc(small_landed, 16)
            pool.dma_start(params[:, :], params_in).then_inc(small_landed, 16)
            pool.dma_start(mask[0:64, :], mask_in[0:64, :]).then_inc(k_written, 16)
            pool.dma_start(mask[64:128, :], mask_in[64:128, :]).then_inc(y_written, 16)

            def load_filter(c, par):
                pool.dma_start(w4s[:, par, :, :, :].rearrange("p a b n -> p (a b n)"),
                               w4[bass.ds(c, 1), :, :].rearrange("a p n -> p (a n)")).then_inc(w4_landed[par], 16)
                pool.dma_start(absd[:, par, :, :, :].rearrange("p a b n -> p (a b n)"),
                               decay[bass.ds(c, 1), :].rearrange("a n -> (a n)").partition_broadcast(128)
                               ).then_inc(dec_landed[par], 16)

            def store_spectrum(c):
                pool.wait_ge(k_evac, c * 6 + 12)
                pool.dma_start(kg_dram[bass.ds(c, 1), :, :, :].rearrange("a o p n -> p (a o) n"),
                               kstage[:, :, :, :, :].rearrange("p o f r n -> p o (f r n)")).then_inc(k_written, 16)
                pool.dma_start(km_dram[bass.ds(c, 1), :, :, :].rearrange("a o p n -> p (a o) n"),
                               kmstage[:, :, :, :].rearrange("p o r n -> p o (r n)")).then_inc(k_written, 16)

            load_filter(0, 0)
            load_filter(1, 1)
            for c in range(CH):
                if c + 2 < CH:
                    pool.wait_ge(h4_mm, c * 3 + 3)
                    pool.wait_ge(env_done, c * 3 + 3)
                    load_filter(c + 2, c % 2)
                store_spectrum(c)
            pool.wait_ge(k_written, 16 + 32 * CH)
            pool.wait_ge(k_mm, 6 * CH)
            pool.wait_ge(xt_mm, KT)
            for stacked in (uT_hi[0:STACK, 2, :], vT_hi[0:STACK, 2, :], pT_hi[0:STACK, 2, :],
                            y_hi[0:STACK, 2, :, :].rearrange("p r n -> p (r n)")):
                last = nc.gpsimd.memset(stacked.bitcast(F32), 0.0)
            last.then_inc(zeroed, 1)

            def load_bias(c):
                for s in range(2):
                    for hh in range(HC):
                        src = bass.AP(rpb.tensor, c * (HC * RPB_R * RPB_C) + ((hh * RPB_R + 5 - s) * RPB_C + KW - GRID_W),
                                      [[1, GRID_W], [RPB_C, 6], [1, GRID_W]])
                        pool.dma_start(bias_t[64 * s:64 * s + 64, hh, NM:NM + 6 * GRID_W].rearrange(
                            "p (j k) -> p j k", j=6), src).then_inc(b_landed, 16)
                for lo in (0, NM + 6 * GRID_W):
                    pool.dma_start(bias_t[:, :, lo:lo + NM],
                                   mbias[bass.ds(c, 1), :].rearrange("a (h m) -> (a h) m", h=HC).partition_broadcast(128)
                                   ).then_inc(b_landed, 16)
                pool.wait_ge(b_landed, (c + 1) * (16 * (2 * HC + 2)))
                for hh in range(HC):
                    grid = bias_t[:, hh, NM:NM + 6 * GRID_W].rearrange("p (j k) -> p j k", j=6)
                    msk = mask[:, :].rearrange("p (a k) -> p a k", a=1).broadcast_to([128, 6, GRID_W])
                    last = nc.gpsimd.tensor_tensor(grid, grid, msk, ALU.add)
                last.then_inc(b_ready, 1)

            def load_spectrum(c, order):
                pool.dma_start(kspec[:, 0:2, :, :].rearrange("p f r n -> p (f r n)"),
                               kg_dram[bass.ds(c, 1), order, :, :].rearrange("a p n -> p (a n)")).then_inc(k_landed, 16)
                pool.dma_start(kspec[0:NM, 2, :, :].rearrange("p r n -> p (r n)"),
                               km_dram[bass.ds(c, 1), order, :, :].rearrange("a p n -> p (a n)")).then_inc(k_landed, 16)

            def second_order(c):
                pool.wait_ge(y_full, c * 6 + 3)
                load_spectrum(c, 1)

            def store_y(c, branch, done):
                pool.wait_ge(done, c + 1)
                pool.dma_start(y_dram[branch, :, bass.ds(c * 2, 2), :], ystage[:, :, :]).then_inc(y_written, 16)

            load_bias(0)
            load_spectrum(0, 0)
            def load_y(place_, branch, written):
                pool.wait_ge(y_written, written)
                pool.dma_start(y_raw[:, place_, :], y_dram[branch].rearrange("p k n -> p (k n)")).then_inc(y_landed[place_], 16)

            with pool.Fori(1, CH) as c:
                second_order(c - 1)
                store_y(c - 1, 0, ya_done)
                store_y(c - 1, 2, yc_done)
                pool.wait_ge(smax_done, c * HC)
                load_bias(c)
                pool.wait_ge(y_full, c * 6)
                load_spectrum(c, 0)
                store_y(c - 1, 1, yb_done)
            second_order(CH - 1)
            store_y(CH - 1, 0, ya_done)
            pool.wait_ge(inv_mm, 2 * CH)
            load_y(0, 0, 48 * CH - 16)
            store_y(CH - 1, 2, yc_done)
            pool.wait_ge(n1_mm, 3 * CH)
            load_y(1, 2, 48 * CH)
            store_y(CH - 1, 1, yb_done)
            pool.wait_ge(n2_mm, CH)
            load_y(2, 1, 48 * CH + 16)
            pool.wait_ge(slab_used, W3)
            for tt in range(2):
                pool.dma_start(h[:, tt, :], x[128 * tt:128 * tt + 128, :]).then_inc(h_landed, 16)
            pool.dma_start(fg[:, :], final_g.partition_broadcast(128)).then_inc(h_landed, 16)

        def slot_main(c, t):
            return t % 4, (c * 5 + (t // 4 + 2)) * 16

        def slot_merge(i, t):
            return t % 3, (i * 6 + (t // 3 + 22)) * 16

        def slot_out(i, t):
            return t % 4, (i + ((46 if t % 4 < 3 else 22) + t // 4)) * 16

        @block.tensor
        def _(pe):
            mm = nc.tensor.matmul

            def three(out_ap, a_hi, a_lo, b_hi, b_lo, first, last, skip=False):
                mm(out_ap, a_hi, b_hi, start=first, stop=False)
                mm(out_ap, a_hi, b_lo, start=False, stop=False)
                return mm(out_ap, a_lo, b_hi, start=False, stop=last)

            def stacked(out_ap, a, b, first, last):
                return mm(out_ap, a, b, start=first, stop=last)

            pe.wait_ge(small_landed, 16 * 8)
            for layer in range(3):
                if layer == 0:
                    ins = mm(ps[0:HID, 7, 0:L], mlpw[0:EMB, 0:HID], zt[:, :], start=True, stop=True)
                else:
                    pe.wait_ge(mlp_sin, layer)
                    ins = mm(ps[0:HID, 7, 0:L], mlpw[:, HID * layer:HID * layer + HID], hid[:, :], start=True, stop=True)
                ins.then_inc(mlp_mm, 1)
            pe.wait_ge(x_scaled, 3)
            for k in range(KT):
                if k >= 4:
                    pe.wait_ge(xt_lo, k - 3)
                for t, (p, n) in enumerate(TOK):
                    last = nc.tensor.transpose(ps[:, k % 4, p:p + n], xin[0:n, t, 128 * k:128 * k + 128], ident[0:n, 0:n])
                last.then_inc(xt_mm, 1)
            pe.wait_ge(mlp_sin, 3)
            pe.wait_ge(xt_lo, KT)
            pe.wait_ge(lo_done, 1)

            def make_h4(c, j, par):
                p, n = TOK[FORDER[j]]
                if j == 0:
                    pe.wait_ge(w4_landed[par], (c - par) * 8 + 16)
                pe.wait_ge(h4_read, c * 3 + (j + 1))
                for o_ in range(2):
                    last = mm(ps[0:n, 6 + o_, :], hid[:, p:p + n], w4s[:, par, o_, :, :].rearrange("p d n -> p (d n)"),
                              start=True, stop=True)
                last.then_inc(h4_mm, 1)

            def add_spectra(c, j, es):
                t = FORDER[j]
                n = TOK[t][1]
                for e in es:
                    f, ri = e // 2, e % 2
                    fp, fn = TOK[f]
                    if j == 0:
                        pe.wait_ge(k_evac, c * 6 + (e + 1))
                    if e == 0:
                        pe.wait_ge(sdlo_done, c * 3 + (j + 1))
                    if t == 2:
                        last = mm(ps[0:fn, e, :], filt_hi[0:STACK, t, ri, fp:fp + fn],
                                  sd_hi[0:STACK, t, ri, :, :].rearrange("p o n -> p (o n)"), start=False, stop=False)
                    else:
                        last = three(ps[0:fn, e, :], filt_hi[0:n, t, ri, fp:fp + fn], filt_lo[0:n, t, ri, fp:fp + fn],
                                     sd_hi[0:n, t, ri, :, :].rearrange("p o n -> p (o n)"),
                                     sd_lo[0:n, t, ri, :, :].rearrange("p o n -> p (o n)"), j == 0, j == 2)
                    if j == 2:
                        last.then_inc(k_mm, 1)

            def filters(c, par, more):
                for j in range(3):
                    add_spectra(c, j, (0, 1, 2))
                    if j == 0:
                        make_h4(c, 2, par)
                    elif more:
                        make_h4(c + 1, j - 1, 1 - par)
                    add_spectra(c, j, (3, 4, 5))

            make_h4(0, 0, 0)
            make_h4(0, 1, 0)
            with pe.Fori(0, CH // 2 - 1) as cc:
                filters(cc * 2, 0, True)
                filters(cc * 2 + 1, 1, True)
            filters(CH - 2, 0, True)
            filters(CH - 1, 1, False)

            def proj_slab(par, bank, half, p0):
                for nt in range(2):
                    for k in range(8):
                        last = three(ps[:, bank + nt, 0:L - p0], w_hi[:, par, k, 128 * nt:128 * nt + 128],
                                     w_lo[:, par, k, 128 * nt:128 * nt + 128], xn_hi[:, 8 * half + k, p0:L],
                                     xn_lo[:, 8 * half + k, p0:L], half == 0 and k == 0, half == 1 and k == 7)
                last.then_inc(slab_used, 1)

            def turn(src, bank):
                for t, (p, n) in enumerate(TOK):
                    for i in range(2):
                        dst = ps[:, bank, CC * t + 128 * i:CC * t + 128 * i + 128] if t < 2 else \
                            ps[0:n, bank + 1, 128 * i:128 * i + 128]
                        last = nc.tensor.transpose(dst, src[:, i, p:p + n], ident[:, :])
                last.then_inc(t_mm, 1)

            def forward(f, bank):
                fp, fn = TOK[f]
                for ri in range(2):
                    for t in range(2):
                        three(ps[0:fn, bank, CC * ri:CC * ri + CC], sym_hi[:, t, ri, fp:fp + fn],
                              sym_lo[:, t, ri, fp:fp + fn], uT_hi[:, t, :], uT_lo[:, t, :], t == 0, False)
                    last = stacked(ps[0:fn, bank, CC * ri:CC * ri + CC], sym_hi[0:STACK, 2, ri, fp:fp + fn],
                                   uT_hi[0:STACK, 2, :], False, True)
                last.then_inc(fwd_mm, 1)

            def inverse(p0):
                for i in range(2):
                    for e in range(4):
                        f, ri = e // 2, e % 2
                        three(ps[:, 4 + i, 0:L - p0], y_hi[:, f, ri, 128 * i:128 * i + 128],
                              y_lo[:, f, ri, 128 * i:128 * i + 128], sym_hi[:, f, ri, p0:L], sym_lo[:, f, ri, p0:L],
                              e == 0, False)
                    for ri in range(2):
                        last = stacked(ps[:, 4 + i, 0:L - p0], y_hi[0:STACK, 2, ri, 128 * i:128 * i + 128],
                                       sym_hi[0:STACK, 2, ri, p0:L], False, ri == 1)
                last.then_inc(inv_mm, 1)

            def scores(hh):
                i, r = hh // 2, slice(64 * (hh % 2), 64 * (hh % 2) + 64)
                for a in range(2):
                    ks = slice(NM, NM + L) if a == 0 else slice(0, L)
                    last = three(ps[:, 6 + a, 0:L], q_hi[r, i, 128 * a:128 * a + 128], q_lo[r, i, 128 * a:128 * a + 128],
                                 k_hi[r, i, ks], k_lo[r, i, ks], True, True)
                last.then_inc(s_mm, 1)

            def turn_p():
                for a in range(2):
                    g0 = 0 if a == 0 else NM
                    m0 = NG if a == 0 else 0
                    for kt in range(2):
                        nc.tensor.transpose(ps[:, 6, NG * kt + 128 * a:NG * kt + 128 * a + 128],
                                            sco[:, a, g0 + 128 * kt:g0 + 128 * kt + 128], ident[:, :])
                    last = nc.tensor.transpose(ps[0:NM, 7, 128 * a:128 * a + 128], sco[:, a, m0:m0 + NM], ident[:, :])
                last.then_inc(pt_mm, 1)

            def attend(hh):
                i = hh // 2
                for t in range(2):
                    three(ps[:, 7, NG:2 * NG], vT_hi[:, t, 128 * i:128 * i + 128], vT_lo[:, t, 128 * i:128 * i + 128],
                          pT_hi[:, t, :], pT_lo[:, t, :], t == 0, False)
                stacked(ps[:, 7, NG:2 * NG], vT_hi[0:STACK, 2, 128 * i:128 * i + 128], pT_hi[0:STACK, 2, :], False,
                        True).then_inc(pv_mm, 1)

            def fnet_channels(t, bank):
                p, n = TOK[t]
                for i in range(2):
                    last = three(ps[0:n, bank, :], fi_hi[:, i, p:p + n], fi_lo[:, i, p:p + n], fch_hi[:, i, :], fch_lo[:, i, :],
                                 i == 0, i == 1)
                last.then_inc(n1_mm, 1)

            def fnet_tokens():
                for i in range(2):
                    for e in range(4):
                        t, ri = e // 2, e % 2
                        three(ps[:, 4, NG * i:NG * i + NG], p2_hi[:, t, ri, 128 * i:128 * i + 128],
                              p2_lo[:, t, ri, 128 * i:128 * i + 128], ftok_hi[:, t, ri, :], ftok_lo[:, t, ri, :], e == 0, False)
                    for ri in range(2):
                        last = stacked(ps[:, 4, NG * i:NG * i + NG], p2_hi[0:STACK, 2, ri, 128 * i:128 * i + 128],
                                       ftok_hi[0:STACK, 2, ri, :], False, ri == 1)
                last.then_inc(n2_mm, 1)

            pe.wait_ge(lo_done, NCONST)
            with pe.Fori(0, CH) as c:
                for t in range(S1):
                    name, _, n = BLOCKS[t // 2]
                    if t % 2 == 0:
                        pe.wait_ge(proj_read, c * NBLK + (t // 2 + 1))
                    pe.wait_ge(lo_done, c * S1 + (NCONST + t + 1))
                    proj_slab(t % 2, 2 * (t // 2 % 2), t % 2, L - n)
                    if t == 3:
                        pe.wait_ge(proj_read, c * NBLK + 3)
                        turn(u, 4)
                    if t == 4:
                        pe.wait_ge(t_lo, c * 3 + 1)
                        forward(0, 4)
                        forward(1, 5)
                    if t == 5:
                        pe.wait_ge(y_full, c * 6 + 1)
                        forward(2, 4)
                    if t == 6:
                        pe.wait_ge(proj_read, c * NBLK + 5)
                        scores(0)
                    if t == 7:
                        pe.wait_ge(p_done, c * HC + 1)
                        turn_p()
                    if t == 8:
                        pe.wait_ge(proj_read, c * NBLK + 6)
                        pe.wait_ge(pt_lo, c * HC + 1)
                        turn(v, 6)
                    if t == 9:
                        pe.wait_ge(t_lo, c * 3 + 2)
                        scores(1)
                        pe.wait_ge(ylo_done, c * 6 + 3)
                        inverse(0)
                    if t in (10, 12, 14):
                        hh = (t - 8) // 2
                        pe.wait_ge(p_done, c * HC + hh + 1)
                        attend(hh - 1)
                        turn_p()
                    if t in (11, 13):
                        hh = (t - 7) // 2
                        pe.wait_ge(o_done, c * HC + hh - 1)
                        scores(hh)
                    if t == 11:
                        pe.wait_ge(z_done, c + 1)
                        turn(x1, 4)
                    if t == 12:
                        pe.wait_ge(t_lo, c * 3 + 3)
                        forward(0, 4)
                        forward(1, 5)
                    if t == 13:
                        pe.wait_ge(y_full, c * 6 + 4)
                        forward(2, 4)
                    if t == 15:
                        pe.wait_ge(ylo_done, c * 6 + 6)
                        inverse(NM)
                        pe.wait_ge(o_done, c * HC + 3)
                        attend(3)
                    if t == 16:
                        pe.wait_ge(proj_read, c * NBLK + 10)
                        pe.wait_ge(ya_done, c + 1)
                        fnet_channels(0, 4)
                        fnet_channels(1, 5)
                    if t == 17:
                        pe.wait_ge(n1_lo, c * 3 + 1)
                        fnet_channels(2, 4)
                    if t == 19:
                        pe.wait_ge(n1_lo, c * 3 + 3)
                        fnet_tokens()

            with pe.Fori(0, JB // 2) as i:
                for t in range(S2):
                    b, part = t % 9 // 3, t % 3
                    m = t // 3
                    pair = 2 * ((2 * m + (part == 2)) % 4)
                    if part == 0:
                        pe.wait_ge(gate_done, i * 6 + (m + 1))
                        if m == 0:
                            pe.wait_ge(proj_read, NBLK * CH + 1)
                        if m == 1:
                            pe.wait_ge(yb_done, CH)
                    if part == 2:
                        pe.wait_ge(br_read, i * 6 + (m + 1))
                        if m == 0:
                            pe.wait_ge(proj_read, NBLK * CH + 2)
                        pe.wait_ge(blo_done, b + 1)
                    pe.wait_ge(lo_done, i * S2 + (NCONST + W2 + t + 1))
                    if part < 2:
                        proj_slab(t % 2, pair, part, NM)
                    else:
                        for nt in range(2):
                            for k in range(8):
                                last = three(ps[:, pair + nt, 0:NG], w_hi[:, t % 2, k, 128 * nt:128 * nt + 128],
                                             w_lo[:, t % 2, k, 128 * nt:128 * nt + 128], yb_hi[:, b, k, :], yb_lo[:, b, k, :],
                                             k == 0, k == 7)
                        last.then_inc(slab_used, 1)

            with pe.Fori(0, JB // 2) as i:
                for t in range(4):
                    if t % 2 == 0:
                        pe.wait_ge(h_sum, i * 2 + (t // 2 + 1))
                    if t == 0:
                        pe.wait_ge(gate_done, 3 * JB + 2)
                        pe.wait_ge(mlo_done, JB // 2)
                    if t == 1:
                        pe.wait_ge(mlo_done, JB)
                    pe.wait_ge(lo_done, i * 4 + (NCONST + W3 + t + 1))
                    for tt in range(2):
                        for k in range(8):
                            kk = 8 * (t % 2) + k
                            last = three(ps[:, 2 * (t // 2) + tt, 0:CC], m_hi[:, kk, 128 * tt:128 * tt + 128],
                                         m_lo[:, kk, 128 * tt:128 * tt + 128], w_hi[:, t % 2, k, :], w_lo[:, t % 2, k, :],
                                         kk == 0, kk == KT - 1)
                    last.then_inc(slab_used, 1)

        @block.scalar
        def _(act):
            A = nc.scalar.activation

            def split(where, par, w):
                slot, landed = where
                act.wait_ge(w_landed[slot], landed)
                act.wait_ge(slab_used, w - 1)
                A(w_hi[:, par, :, :].rearrange("p k n -> p (k n)"), raw[:, slot, :], ACT.Copy).then_inc(hi_done, 1)

            def split_const(i, dst, n):
                act.wait_ge(w_landed[i], 16)
                A(dst, raw[:, i, 0:n], ACT.Copy).then_inc(hi_done, 1)

            split_const(0, filt_hi[:, :, :, :].rearrange("p a b n -> p (a b n)"), 6 * L)
            act.wait_ge(x_landed, 48)
            for t, (p, n) in enumerate(TOK):
                if t:
                    act.wait_ge(x_sq, t)
                A(ps[0:n, 0:4, :].rearrange("p a n -> p (a n)"), xin[0:n, t, :], ACT.Square,
                  accum_out=stat[0:n, t:t + 1]).then_inc(x_sq, 1)
            act.wait_ge(x_var, 3)
            for t, (p, n) in enumerate(TOK):
                last = A(stat[0:n, 8 + t:9 + t], stat[0:n, 4 + t:5 + t], ACT.Sqrt)
            last.then_inc(x_std, 1)
            for layer in range(3):
                act.wait_ge(mlp_red, layer + 1)
                A(hid[:, :], red[:, 0, :], ACT.Sin).then_inc(mlp_sin, 1)
            for k in range(KT):
                act.wait_ge(xt_mm, k + 1)
                ins = A(xn_hi[:, k, :], ps[:, k % 4, 0:L], ACT.Copy, scale=params[:, NGC + k:NGC + k + 1])
                ins.then_inc(xt_hi, 1)

            def magnitudes(c, par):
                act.wait_ge(dec_landed[par], (c - par) * 8 + 16)
                A(absd[:, par, :, :, :], absd[:, par, :, :, :], ACT.Abs).then_inc(dec_abs, 1)
                act.wait_ge(dec_abs, c + 1)

            def envelope(c, j, par):
                t = FORDER[j]
                n = TOK[t][1]
                act.wait_ge(h4_read, c * 3 + j)
                A(envel[0:n, (par + j) % 2, :, :, :], absd[0:n, par, :, :, :], ACT.Exp, scale=negt[0:n, t:t + 1]).then_inc(env_done, 1)

            def sd_high(c, j):
                t = FORDER[j]
                n = TOK[t][1]
                act.wait_ge(sd_done, c * 3 + j + 1)
                ins = A(sd_hi[0:n, t, :, :, :], sd[0:n, :, :, :], ACT.Copy)
                if t == 2:
                    ins = A(sd_hi[32:32 + n, t, :, :, :], sd[0:n, :, :, :], ACT.Copy)
                ins.then_inc(sdhi_done, 1)

            def store_spectra(c, k_stored):
                act.wait_ge(k_written, k_stored)
                for e in range(6):
                    f, ri = e // 2, e % 2
                    act.wait_ge(k_mm, c * 6 + (e + 1))
                    dst = kstage[:, :, f, ri, :] if f < 2 else kmstage[:, :, ri, :]
                    A(dst, ps[0:TOK[f][1], e, :].rearrange("p (o n) -> p o n", o=2), ACT.Copy,
                      scale=2.0 / FFT_N).then_inc(k_evac, 1)

            act.wait_ge(xt_mm, KT)
            magnitudes(0, 0)
            A(envel[:, 0, :, :, :], absd[:, 0, :, :, :], ACT.Exp, scale=negt[:, 0:1]).then_inc(env_done, 1)
            envelope(0, 1, 0)
            for c in range(CH):
                sd_high(c, 0)
                if c:
                    store_spectra(c - 1, 16 + 32 * (c - 1))
                envelope(c, 2, c % 2)
                sd_high(c, 1)
                if c + 1 < CH:
                    magnitudes(c + 1, (c + 1) % 2)
                    envelope(c + 1, 0, (c + 1) % 2)
                sd_high(c, 2)
                if c + 1 < CH:
                    envelope(c + 1, 1, (c + 1) % 2)
            store_spectra(CH - 1, 16 + 32 * (CH - 1))
            split_const(1, sym_hi[:, :, :, :].rearrange("p a b n -> p (a b n)"), 6 * L)
            split_const(2, fch_hi[:, :, :].rearrange("p a n -> p (a n)"), 4 * CC)
            split_const(3, ftok_hi[:, :, :, :].rearrange("p a b n -> p (a b n)"), 6 * NG)
            for w in range(2):
                act.wait_ge(w_landed[w], 32)
                A(w_hi[:, w, :, :].rearrange("p k n -> p (k n)"), raw[:, w, :], ACT.Copy).then_inc(hi_done, 1)

            act.wait_ge(k_written, 16 + 32 * CH)
            act.wait_ge(zeroed, 1)

            def evac(c, name, b):
                bank = 2 * (b % 2)
                act.wait_ge(slab_used, c * S1 + (2 * b + 2))
                src = ps[:, bank:bank + 2, 0:L]
                src16 = ps[:, bank:bank + 2, 0:NG]
                if name in ("u", "x1", "x2"):
                    dst = {"u": u, "x1": x1, "x2": x2}[name]
                    t0 = {"u": 0, "x1": 8, "x2": 16}[name]
                    for i in range(2):
                        ins = A(dst[:, i, :], ps[:, bank + i, 0:L], ACT.Identity,
                                bias=params[:, bass.ds(c * 2 + (CB + t0 + i), 1)],
                                scale=params[:, bass.ds(c * 2 + (CW + 24 + t0 + i), 1)])
                elif name == "q":
                    for i in range(2):
                        ins = A(q_hi[:, i, :].rearrange("p (r n) -> p r n", r=4),
                                ps[:, bank + i, 0:NG].rearrange("p (r n) -> p r n", r=4)[:, :, ::-1], ACT.Copy, scale=0.125)
                elif name == "k":
                    A(k_hi[:, :, 0:L], src, ACT.Copy)
                    ins = A(k_hi[:, :, L:L + NM], ps[:, bank:bank + 2, 0:NM], ACT.Copy)
                elif name == "fin":
                    ins = A(fi_hi[:, :, :], src, ACT.Copy)
                else:
                    act.wait_ge(proj_read, c * NBLK + {"hgate": 2, "ngate": 9, "fgate": 11}[name])
                    ins = A(gexp[:, :, :], src16, ACT.Exp, scale=-1.0)
                ins.then_inc(a_ev, 1)

            def turned(n_th, done, dst, bank, ready, w=CC, twin=32):
                act.wait_ge(ready, n_th)
                A(dst[:, 0:2, :], ps[:, bank, :].rearrange("p (t n) -> p t n", t=2), ACT.Copy)
                A(dst[0:NM, 2, :], ps[0:NM, bank + 1, 0:w], ACT.Copy)
                A(dst[twin:twin + NM, 2, :], ps[0:NM, bank + 1, 0:w], ACT.Copy).then_inc(done, 1)

            def spectra(c, fs, order):
                for f in fs:
                    n = TOK[f][1]
                    act.wait_ge(y_full, c * 6 + (3 * order + f + 1))
                    ins = A(y_hi[0:n, f, :, :], prod[0:n, 2, :, :], ACT.Copy)
                    if f == 2:
                        ins = A(y_hi[32:32 + n, f, :, :], prod[0:n, 2, :, :], ACT.Copy)
                    ins.then_inc(yhi_done, 1)

            def soft(c, hh):
                act.wait_ge(smax_done, c * HC + hh + 1)
                for a in range(2):
                    ins = A(sco[:, a, :], sco[:, a, :], ACT.Exp, bias=stat[:, 2 + a:3 + a], accum_out=stat[:, 4 + a:5 + a])
                ins.then_inc(exp_done, 1)

            with act.Fori(0, CH) as c:
                for t in range(S1):
                    split(slot_main(c, t + 2), t % 2, c * S1 + (t + 2))
                    if t % 2 and BLOCKS[t // 2][0] != "v":
                        evac(c, BLOCKS[t // 2][0], t // 2)
                    if t == 3:
                        turned(c * 3 + 1, t_hi, uT_hi, 4, t_mm)
                    if t == 4:
                        spectra(c, (0, 1), 0)
                    if t == 5:
                        spectra(c, (2,), 0)
                    if t == 6:
                        soft(c, 0)
                    if t == 8:
                        turned(c * 3 + 2, t_hi, vT_hi, 6, t_mm)
                    if t in (7, 10, 12, 14):
                        turned(c * HC + {7: 1, 10: 2, 12: 3, 14: 4}[t], pt_hi, pT_hi, 6, pt_mm, NG, 64)
                    if t == 11:
                        turned(c * 3 + 3, t_hi, uT_hi, 4, t_mm)
                    if t in (9, 11, 13):
                        soft(c, (t - 7) // 2)
                    if t == 12:
                        spectra(c, (0, 1), 1)
                    if t == 13:
                        spectra(c, (2,), 1)
                    if t == 16:
                        for f in range(2):
                            act.wait_ge(n1_mm, c * 3 + f + 1)
                            A(p2_hi[:, f, :, :], ps[:, 4 + f, :].rearrange("p (r n) -> p r n", r=2), ACT.Copy).then_inc(n1_hi, 1)
                    if t == 17:
                        act.wait_ge(n1_mm, c * 3 + 3)
                        for row in (0, 32):
                            ins = A(p2_hi[row:row + NM, 2, :, :], ps[0:NM, 4, :].rearrange("p (r n) -> p r n", r=2), ACT.Copy)
                        ins.then_inc(n1_hi, 1)

            A(stat[:, 13:14], params[:, 0:1], ACT.Copy).then_inc(gate_done, 2)

            def split_branch(b):
                act.wait_ge(y_landed[b], 16)
                A(yb_hi[:, b, :, :].rearrange("p k n -> p (k n)"), y_raw[:, b, :], ACT.Copy).then_inc(bhi_done, 1)

            def merge_turn(i, first):
                for t in range(S2):
                    if first and t in (1, 3, 5):
                        split_branch((t - 1) // 2)
                    split(slot_merge(i, t + 2), t % 2, i * S2 + (W2 + t + 2))
                    m = t // 3
                    pair = 2 * ((2 * m) % 4)
                    if t % 3 == 1:
                        act.wait_ge(slab_used, i * S2 + (W2 + t + 1))
                        act.wait_ge(br_read, i * 6 + (m + 1))
                        A(mgate[:, m % 2, :, :], ps[:, pair:pair + 2, 0:NG], ACT.Sigmoid).then_inc(gate_done, 1)
                    if t % 9 == 8:
                        jj = t // 9
                        act.wait_ge(msum_done, i * 2 + (jj + 1))
                        A(m_hi[:, bass.ds(i * 4 + 2 * jj, 2), :], msum[:, :, :], ACT.Copy).then_inc(mhi_done, 1)

            act.wait_ge(n2_mm, CH)
            merge_turn(0, True)
            with act.Fori(1, JB // 2) as i:
                merge_turn(i, False)
            with act.Fori(0, JB // 2 - 1) as i:
                for t in range(4):
                    split(slot_out(i, t + 2), t % 2, i * 4 + (W3 + t + 2))
            for t in range(2):
                split(slot_out(JB // 2 - 1, t + 2), t % 2, NW - 2 + t)
            act.wait_ge(h_sum, JB + 2)
            for tt in range(2):
                if tt:
                    act.wait_ge(f_sq, tt)
                A(sq[:, :], h[:, tt, :], ACT.Square, accum_out=stat[:, tt:tt + 1]).then_inc(f_sq, 1)
                act.wait_ge(f_var, tt + 1)
                A(stat[:, 8 + tt:9 + tt], stat[:, 4 + tt:5 + tt], ACT.Sqrt).then_inc(f_std, 1)

        @block.vector
        def _(dve):
            V = nc.vector

            def lo_part(dst, src, hi):
                return V.tensor_tensor(dst, src, hi.bitcast(F32), ALU.subtract)

            def split(where, par, w):
                dve.wait_ge(hi_done, w + (NCONST + 1))
                lo_part(w_lo[:, par, :, :].rearrange("p k n -> p (k n)"), raw[:, where[0], :],
                        w_hi[:, par, :, :].rearrange("p k n -> p (k n)")).then_inc(lo_done, 1)

            def split_const(i, dst, hi, n):
                dve.wait_ge(hi_done, i + 1)
                lo_part(dst, raw[:, i, 0:n], hi).then_inc(lo_done, 1)

            def split_stacked(i, dst, hi, n):
                dve.wait_ge(hi_done, i + 1)
                lo_part(dst[:, 0:2, :, :].rearrange("p a b n -> p (a b n)"), raw[:, i, 0:4 * n],
                        hi[:, 0:2, :, :].rearrange("p a b n -> p (a b n)"))
                part = hi[32:32 + NM, 2, :, :].rearrange("p b n -> p (b n)")
                lo_part(part, raw[32:32 + NM, i, 4 * n:6 * n], part).then_inc(lo_done, 1)

            class turn:
                n, c, per = 0, None, 0

            def link(ins):
                turn.n += 1
                ins.then_inc(dve_link, 1)
                dve.wait_ge(dve_link, turn.n if turn.c is None else turn.c * turn.per + turn.n)

            def enter(c, per):
                turn.c, turn.per, turn.before = c, per, turn.n

            def leave(times):
                assert turn.n - turn.before == turn.per, turn.n - turn.before
                turn.c, turn.n = None, turn.before + times * turn.per

            split_stacked(0, filt_lo, filt_hi, L)
            dve.wait_ge(x_sq, 3)
            for t, (p, n) in enumerate(TOK):
                V.tensor_scalar(stat[0:n, 4 + t:5 + t], stat[0:n, t:t + 1], 1.0 / D, EPS, ALU.mult, ALU.add).then_inc(x_var, 1)

            def mlp_layer(layer):
                dve.wait_ge(mlp_mm, layer + 1)
                link(V.tensor_scalar(red[:, 0, :], ps[0:HID, 7, 0:L], mlpw[:, 3 * HID + layer:3 * HID + layer + 1],
                                     mlpw[:, 3 * HID + 3:3 * HID + 4], ALU.add, ALU.mult))
                link(V.tensor_scalar(red[:, 1, :], red[:, 0, :], 1.0 / TWO_PI, MAGIC, ALU.mult, ALU.add))
                link(V.tensor_scalar(red[:, 2, :], red[:, 1, :], -MAGIC, None, ALU.add))
                c1 = float(np.float32(6.28125))
                c2 = float(np.float32(TWO_PI - c1))
                c3 = float(np.float32(TWO_PI - c1 - c2))
                link(V.scalar_tensor_tensor(red[:, 1, :], red[:, 2, :], -c1, red[:, 0, :], ALU.mult, ALU.add))
                link(V.scalar_tensor_tensor(red[:, 3, :], red[:, 2, :], -c2, red[:, 1, :], ALU.mult, ALU.add))
                link(V.scalar_tensor_tensor(red[:, 1, :], red[:, 2, :], -c3, red[:, 3, :], ALU.mult, ALU.add))
                V.tensor_scalar(red[:, 0, :], red[:, 1, :], CLAMP, -CLAMP, ALU.min, ALU.max).then_inc(mlp_red, 1)

            mlp_layer(0)
            dve.wait_ge(x_std, 1)
            for t, (p, n) in enumerate(TOK):
                link(V.reciprocal(stat[0:n, 12 + t:13 + t], stat[0:n, 8 + t:9 + t]))
            for t, (p, n) in enumerate(TOK):
                V.tensor_scalar(xin[0:n, t, :], xin[0:n, t, :], stat[0:n, 12 + t:13 + t], None, ALU.mult).then_inc(x_scaled, 1)
            mlp_layer(1)
            mlp_layer(2)
            for k in range(KT):
                dve.wait_ge(xt_hi, k + 1)
                ins = V.scalar_tensor_tensor(xn_lo[:, k, :], ps[:, k % 4, 0:L], params[:, NGC + k:NGC + k + 1],
                                             xn_hi[:, k, :].bitcast(F32), ALU.mult, ALU.subtract)
                ins.then_inc(xt_lo, 1)
            V.memset(stat[:, 15:16], 0.0).then_inc(k_evac, 6)
            V.memset(stat[:, 14:15], 0.0).then_inc(h4_read, 1)
            V.memset(sd_hi[0:STACK, 2, :, :, :].rearrange("p a b n -> p (a b n)").bitcast(F32), 0.0)
            with dve.Fori(0, CH // 2) as cc:
                enter(cc, 2)
                for par in range(2):
                    for j, t in enumerate(FORDER):
                        n = TOK[t][1]
                        nth = cc * 6 + (3 * par + j + 1)
                        env = envel[0:n, (par + j) % 2, :, :, :]
                        dve.wait_ge(env_done, nth)
                        if t == 2:
                            link(V.memset(env[0:1, :, 1, :], 0.0))
                        dve.wait_ge(h4_mm, nth)
                        V.tensor_tensor(hm[0:n, :, :, :].rearrange("p o d n -> p o (d n)"), ps[0:n, 6:8, :],
                                        env.rearrange("p o d n -> p o (d n)"), ALU.mult).then_inc(h4_read, 1)
                        dve.wait_ge(h4_read, nth + 1)
                        V.tensor_tensor(sd[0:n, 0, :, :], hm[0:n, :, 0, :], hm[0:n, :, 1, :], ALU.add)
                        V.tensor_tensor(sd[0:n, 1, :, :], hm[0:n, :, 0, :], hm[0:n, :, 1, :], ALU.subtract).then_inc(sd_done, 1)
                        dve.wait_ge(sdhi_done, nth)
                        lo = sd_lo[0:n, t, :, :, :] if t < 2 else sd_hi[64:64 + n, t, :, :, :]
                        lo_part(lo, sd[0:n, :, :, :], sd_hi[0:n, t, :, :, :]).then_inc(sdlo_done, 1)
            leave(CH // 2)
            split_stacked(1, sym_lo, sym_hi, L)
            split_const(2, fch_lo[:, :, :].rearrange("p a n -> p (a n)"), fch_hi[:, :, :].rearrange("p a n -> p (a n)"), 4 * CC)
            split_stacked(3, ftok_lo, ftok_hi, NG)
            V.memset(stat[:, 11:12], 0.0).then_inc(proj_read, 2)
            for w in range(2):
                split((w,), w, w)

            def evac(c, name, b):
                bank = 2 * (b % 2)
                src = ps[:, bank:bank + 2, 0:L]
                src16 = ps[:, bank:bank + 2, 0:NG]
                if name == "v":
                    dve.wait_ge(slab_used, c * S1 + (2 * b + 2))
                    V.tensor_copy(v[:, :, :], src).then_inc(proj_read, 1)
                    return
                dve.wait_ge(a_ev, c * (NBLK - 1) + (b + 1 if b < 3 else b))
                if name in ("u", "x1", "x2"):
                    dst = {"u": u, "x1": x1, "x2": x2}[name]
                    t0 = {"u": 0, "x1": 8, "x2": 16}[name]

                    def tap(j, i, to, frm):
                        return V.scalar_tensor_tensor(dst[:, i, to], ps[:, bank + i, frm],
                                                      params[:, bass.ds(c * 2 + (CW + 24 * j + t0 + i), 1)], dst[:, i, to],
                                                      ALU.mult, ALU.add)

                    tap(0, 0, slice(1, L), slice(0, L - 1))
                    link(tap(0, 1, slice(1, L), slice(0, L - 1)))
                    tap(2, 0, slice(0, L - 1), slice(1, L))
                    ins = tap(2, 1, slice(0, L - 1), slice(1, L))
                elif name == "q":
                    for i in range(2):
                        ins = V.scalar_tensor_tensor(q_lo[:, i, :].rearrange("p (r n) -> p r n", r=4),
                                                     ps[:, bank + i, 0:NG].rearrange("p (r n) -> p r n", r=4)[:, :, ::-1], 0.125,
                                                     q_hi[:, i, :].rearrange("p (r n) -> p r n", r=4).bitcast(F32),
                                                     ALU.mult, ALU.subtract)
                elif name == "k":
                    lo_part(k_lo[:, :, 0:L], src, k_hi[:, :, 0:L])
                    ins = lo_part(k_lo[:, :, L:L + NM], ps[:, bank:bank + 2, 0:NM], k_hi[:, :, L:L + NM])
                elif name == "fin":
                    ins = lo_part(fi_lo[:, :, :], src, fi_hi[:, :, :])
                else:
                    link(V.tensor_scalar(gexp[:, :, :], gexp[:, :, :], 1.0, None, ALU.add))
                    link(V.reciprocal(gexp[:, :, :], gexp[:, :, :]))
                    ins = V.tensor_tensor(gate[:, :, :], src16, gexp[:, :, :], ALU.mult)
                ins.then_inc(proj_read, 1)

            def turned(n_th, hi_ready, done, dst, hi, bank, w=CC, row=64):
                dve.wait_ge(hi_ready, n_th)
                lo_part(dst[:, 0:2, :], ps[:, bank, :].rearrange("p (t n) -> p t n", t=2), hi[:, 0:2, :])
                lo_part(hi[row:row + NM, 2, :], ps[0:NM, bank + 1, 0:w], hi[0:NM, 2, :]).then_inc(done, 1)

            def spectra(c, fs, order):
                for f in fs:
                    n = TOK[f][1]
                    nth = 3 * order + f + 1
                    if f == 0:
                        dve.wait_ge(k_landed, c * 64 + 32 * (order + 1))
                    dve.wait_ge(fwd_mm, c * 6 + nth)
                    bank = ps[0:n, 4 + f % 2, :].rearrange("p (r n) -> p r n", r=2)
                    V.tensor_tensor(prod[0:n, 0, :, :], bank, kspec[0:n, f, :, :], ALU.mult)
                    link(V.tensor_tensor(prod[0:n, 1, :, :], bank, kspec[0:n, f, ::-1, :], ALU.mult))
                    V.tensor_tensor(prod[0:n, 2, 0, :], prod[0:n, 0, 0, :], prod[0:n, 0, 1, :], ALU.subtract)
                    V.tensor_tensor(prod[0:n, 2, 1, :], prod[0:n, 1, 0, :], prod[0:n, 1, 1, :], ALU.add).then_inc(y_full, 1)
                    dve.wait_ge(yhi_done, c * 6 + nth)
                    lo_part(y_lo[0:n, f, :, :] if f < 2 else y_hi[64:64 + n, f, :, :], prod[0:n, 2, :, :],
                            y_hi[0:n, f, :, :]).then_inc(ylo_done, 1)

            def soft(c, hh):
                if hh == 0:
                    dve.wait_ge(b_ready, c + 1)
                dve.wait_ge(s_mm, c * HC + hh + 1)
                V.memset(stat[:, 11:12], 0.0)
                for a in range(2):
                    b0 = NM + 2 * GRID_W if a == 0 else 0
                    ins = V.tensor_tensor_reduce(sco[:, a, :], ps[:, 6 + a, 0:L], bias_t[:, hh, b0:b0 + L], 1.0, -3.0e38,
                                                 ALU.add, ALU.max, stat[:, 6 + a:7 + a])
                link(ins)
                V.tensor_scalar(stat[:, 2:4], stat[:, 6:8], -1.0, None, ALU.mult).then_inc(smax_done, 1)
                dve.wait_ge(exp_done, c * HC + hh + 1)
                link(V.reciprocal(stat[:, 8:10], stat[:, 4:6]))
                for a in range(2):
                    ins = V.tensor_scalar(sco[:, a, :], sco[:, a, :], stat[:, 8 + a:9 + a], None, ALU.mult)
                ins.then_inc(p_done, 1)

            def attended(c, hh):
                r = slice(64 * (hh % 2), 64 * (hh % 2) + 64)
                dve.wait_ge(pv_mm, c * HC + hh + 1)
                V.tensor_copy(o[r, hh // 2, :].rearrange("p (r n) -> p r n", r=4),
                              ps[r, 7, NG:2 * NG].rearrange("p (r n) -> p r n", r=4)[:, :, ::-1]).then_inc(o_done, 1)

            with dve.Fori(0, CH) as c:
                enter(c, 26)
                for t in range(S1):
                    split(slot_main(c, t + 2), t % 2, c * S1 + (t + 2))
                    if t % 2:
                        evac(c, BLOCKS[t // 2][0], t // 2)
                    if t == 3:
                        turned(c * 3 + 1, t_hi, t_lo, uT_lo, uT_hi, 4)
                    if t == 4:
                        spectra(c, (0, 1), 0)
                    if t == 5:
                        spectra(c, (2,), 0)
                    if t == 6:
                        soft(c, 0)
                    if t == 8:
                        turned(c * 3 + 2, t_hi, t_lo, vT_lo, vT_hi, 6)
                    if t in (7, 10, 12, 14):
                        turned(c * HC + {7: 1, 10: 2, 12: 3, 14: 4}[t], pt_hi, pt_lo, pT_lo, pT_hi, 6, NG, 32)
                    if t in (10, 12, 14):
                        attended(c, (t - 10) // 2)
                    if t in (9, 11, 13):
                        soft(c, (t - 7) // 2)
                    if t == 9:
                        dve.wait_ge(inv_mm, c * 2 + 1)
                        for i in range(2):
                            ins = V.scalar_tensor_tensor(u[:, i, :], u[:, i, :], params[:, bass.ds(c * 2 + (SK + i), 1)],
                                                         ps[:, 4 + i, 0:L], ALU.mult, ALU.add)
                        link(ins)
                        V.tensor_tensor(x1[:, :, :], x1[:, :, :], u[:, :, :], ALU.mult).then_inc(z_done, 1)
                    if t == 11:
                        turned(c * 3 + 3, t_hi, t_lo, uT_lo, uT_hi, 4)
                    if t == 12:
                        spectra(c, (0, 1), 1)
                    if t == 13:
                        spectra(c, (2,), 1)
                    if t == 15:
                        dve.wait_ge(inv_mm, c * 2 + 2)
                        for i in range(2):
                            ins = V.scalar_tensor_tensor(u[:, i, NM:L], x1[:, i, NM:L],
                                                         params[:, bass.ds(c * 2 + (SK + 8 + i), 1)],
                                                         ps[:, 4 + i, 0:NG], ALU.mult, ALU.add)
                        link(ins)
                        link(V.tensor_tensor(u[:, :, NM:L], u[:, :, NM:L], x2[:, :, NM:L], ALU.mult))
                        dve.wait_ge(y_written, c * 48 + 16)
                        V.tensor_tensor(ystage[:, :, :], u[:, :, NM:L], gate[:, :, :], ALU.mult).then_inc(ya_done, 1)
                        attended(c, 3)
                    if t == 16:
                        for f in range(2):
                            dve.wait_ge(n1_hi, c * 3 + f + 1)
                            lo_part(p2_lo[:, f, :, :], ps[:, 4 + f, :].rearrange("p (r n) -> p r n", r=2),
                                    p2_hi[:, f, :, :]).then_inc(n1_lo, 1)
                    if t == 17:
                        dve.wait_ge(n1_hi, c * 3 + 3)
                        lo_part(p2_hi[64:64 + NM, 2, :, :], ps[0:NM, 4, :].rearrange("p (r n) -> p r n", r=2),
                                p2_hi[0:NM, 2, :, :]).then_inc(n1_lo, 1)
                        dve.wait_ge(y_written, c * 48 + 32)
                        dve.wait_ge(proj_read, c * NBLK + 11)
                        V.tensor_tensor(ystage[:, :, :], o[:, :, :], gate[:, :, :], ALU.mult).then_inc(yc_done, 1)
                    if t == 19:
                        dve.wait_ge(n2_mm, c + 1)
                        dve.wait_ge(y_written, c * 48 + 48)
                        dve.wait_ge(proj_read, c * NBLK + 12)
                        V.tensor_tensor(ystage[:, :, :], ps[:, 4, :].rearrange("p (i n) -> p i n", i=2), gate[:, :, :],
                                        ALU.mult).then_inc(yb_done, 1)
            leave(CH)

            V.memset(stat[:, 10:11], 0.0).then_inc(br_read, 2)
            V.memset(stat[:, 14:15], 0.0).then_inc(h_sum, 2)

            def split_branch(b):
                dve.wait_ge(bhi_done, b + 1)
                lo_part(yb_lo[:, b, :, :].rearrange("p k n -> p (k n)"), y_raw[:, b, :],
                        yb_hi[:, b, :, :].rearrange("p k n -> p (k n)")).then_inc(blo_done, 1)

            def merge_turn(i, first):
                for t in range(S2):
                    if first and t in (1, 3, 5):
                        split_branch((t - 1) // 2)
                    split(slot_merge(i, t + 2), t % 2, i * S2 + (W2 + t + 2))
                    m = t // 3
                    pair = 2 * ((2 * m + 1) % 4)
                    if t % 3 == 2:
                        dve.wait_ge(slab_used, i * S2 + (W2 + t + 1))
                        dve.wait_ge(gate_done, i * 6 + (m + 3))
                        src = ps[:, pair:pair + 2, 0:NG]
                        if m % 3 == 0:
                            V.tensor_tensor(msum[:, :, :], mgate[:, m % 2, :, :], src, ALU.mult).then_inc(br_read, 1)
                        else:
                            V.tensor_tensor(mterm[:, :, :], mgate[:, m % 2, :, :], src, ALU.mult).then_inc(br_read, 1)
                            dve.wait_ge(br_read, i * 6 + (m + 3))
                            ins = V.tensor_tensor(msum[:, :, :], msum[:, :, :], mterm[:, :, :], ALU.add)
                            if m % 3 == 1:
                                link(ins)
                            else:
                                ins.then_inc(msum_done, 1)
                    if t % 9 == 8:
                        jj = t // 9
                        dve.wait_ge(mhi_done, i * 2 + (jj + 1))
                        lo_part(m_lo[:, bass.ds(i * 4 + 2 * jj, 2), :], msum[:, :, :],
                                m_hi[:, bass.ds(i * 4 + 2 * jj, 2), :]).then_inc(mlo_done, 1)

            merge_turn(0, True)
            with dve.Fori(1, JB // 2) as i:
                enter(i - 1, 2)
                merge_turn(i, False)
            leave(JB // 2 - 1)

            dve.wait_ge(h_landed, 48)

            def add_block(i, nb):
                dve.wait_ge(slab_used, i * 4 + (W3 + 2 * nb + 2))
                cols = h[:, :, bass.ds(i * (2 * CC) + CC * nb, CC)]
                V.tensor_tensor(cols, cols, ps[:, 2 * nb:2 * nb + 2, 0:CC], ALU.add).then_inc(h_sum, 1)

            with dve.Fori(0, JB // 2 - 1) as i:
                for t in range(4):
                    split(slot_out(i, t + 2), t % 2, i * 4 + (W3 + t + 2))
                    if t % 2:
                        add_block(i, t // 2)
            for t in range(4):
                if t < 2:
                    split(slot_out(JB // 2 - 1, t + 2), t % 2, NW - 2 + t)
                if t % 2:
                    add_block(JB // 2 - 1, t // 2)
            for tt in range(2):
                dve.wait_ge(f_sq, tt + 1)
                V.tensor_scalar(stat[:, 4 + tt:5 + tt], stat[:, tt:tt + 1], 1.0 / D, EPS, ALU.mult, ALU.add).then_inc(f_var, 1)
                dve.wait_ge(f_std, tt + 1)
                link(V.reciprocal(stat[:, 6 + tt:7 + tt], stat[:, 8 + tt:9 + tt]))
                V.scalar_tensor_tensor(h[:, tt, :], h[:, tt, :], stat[:, 6 + tt:7 + tt], fg[:, :], ALU.mult,
                                       ALU.mult).then_inc(f_done, 1)


def slab_stream(w_in, wa, wb, wc, wo):
    def slab(w, k0, c0):
        return w[k0:k0 + 1024, c0:c0 + CC].reshape(8, 128, CC).transpose(1, 0, 2).reshape(128, 8 * CC)

    slabs = []
    for c in range(CH):
        for _, col, _ in BLOCKS:
            for half in range(2):
                slabs.append(slab(w_in, 1024 * half, col + CC * c))
    for j in range(JB):
        for b in BRANCHES:
            w = (wa, wb, wc)[b]
            for half in range(2):
                slabs.append(slab(w_in, 1024 * half, 10 * C + D * b + CC * j))
            slabs.append(slab(w, 0, CC * j))
    for j in range(JB):
        for half in range(2):
            slabs.append(slab(wo, 1024 * half, CC * j))
    assert len(slabs) == NW
    return np.stack(slabs)


def kernel(x, meta_tokens, norm_g, w_in, hy_conv_w, hy_conv_b, hy_flt_w1, hy_flt_b1, hy_flt_w2, hy_flt_b2, hy_flt_w3,
           hy_flt_b3, hy_flt_w4, hy_flt_freq, hy_decay, hy_skip, na_rpb, na_meta_bias, w_branch_a, w_branch_b,
           w_branch_c, w_out, final_g):
    import concourse.bacc as bacc
    from concourse.bass_utils import run_bass_kernel_spmd

    def host(a):
        return np.asarray(a)

    tables, zT, negt, mask, ident = constants()
    by_tile = lambda a, n: host(a).reshape(-1, n, 128).transpose(2, 0, 1).reshape(128, -1)
    arrays = {
        "x": host(x)[0],
        "meta": host(meta_tokens),
        "w_stream": slab_stream(host(w_in)[0], host(w_branch_a)[0], host(w_branch_b)[0], host(w_branch_c)[0], host(w_out)[0]),
        "tables": tables,
        "zT": zT,
        "negt_in": negt,
        "mask_in": mask,
        "ident_in": ident,
        "params_in": np.concatenate([by_tile(hy_conv_w, 24), by_tile(hy_conv_b, 24), by_tile(hy_skip, 8),
                                     by_tile(norm_g, 16)], axis=1),
        "mlp_in": np.stack([host(hy_flt_b1)[0], host(hy_flt_b2)[0], host(hy_flt_b3)[0], host(hy_flt_freq)[0]], axis=1),
        "w1": host(hy_flt_w1)[0],
        "w2": host(hy_flt_w2)[0],
        "w3": host(hy_flt_w3)[0],
        "w4": host(hy_flt_w4)[0].reshape(HID, 4, CH, CC).transpose(2, 0, 1, 3).reshape(CH, HID, 4 * CC),
        "decay": host(hy_decay)[0].reshape(4, CH, CC).transpose(1, 0, 2).reshape(CH, 4 * CC),
        "rpb": host(na_rpb)[0].reshape(-1),
        "mbias": host(na_meta_bias)[0].reshape(CH, HC * NM),
        "final_g": host(final_g),
    }
    arrays = {n: np.ascontiguousarray(a) for n, a in arrays.items()}
    nc = bacc.Bacc("TRN2", target_bir_lowering=False, num_devices=1)
    args = {n: nc.dram_tensor(n, a.shape, mybir.dt.from_np(a.dtype), kind="ExternalInput").ap() for n, a in arrays.items()}
    out = nc.dram_tensor("out", [NG, D], F32, kind="ExternalOutput").ap()
    build(nc, out=out, **args)
    r = run_bass_kernel_spmd(nc, [arrays], core_ids=[0])
    return r.results[0]["out"].reshape(1, NG, D)
```

```python
from contextlib import ExitStack
import math

import numpy as np

import concourse.bass as bass
from concourse import mybir

F32 = mybir.dt.float32
F32R = mybir.dt.float32r
ALU = mybir.AluOpType
ACT = mybir.ActivationFunctionType

D = 2048
L = 272
NM = 16
NG = L - NM
C = 1024
CC = 256
CH = C // CC
KT = D // 128
EPS = 1e-6
GRID_W = 64
KW = 16
HEADS = 16
HC = HEADS // CH
RPB_R, RPB_C = 15, 31
HID, EMB = 64, 33
FFT_N = 2 * L
TOK = [(NM, 128), (NM + 128, 128), (0, NM)]
BLOCKS = [("u", 0, L), ("q", 6 * C, NG), ("k", 7 * C, L), ("v", 8 * C, L), ("x1", C, L), ("x2", 2 * C, NG + 2),
          ("hgate", 3 * C, NG), ("fin", 4 * C, L), ("ngate", 9 * C, NG), ("fgate", 5 * C, NG)]
NBLK = len(BLOCKS)
S1 = 2 * NBLK
W2 = CH * S1
JB = D // CC
S2 = 18
W3 = W2 + JB // 2 * S2
NW = W3 + 2 * JB
NCONST = 4
FK = CC // 2 + 1
STACK = 64 + NM
BRANCHES = (0, 2, 1)
FORDER = (0, 2, 1)
TWO_PI = 2.0 * math.pi
MAGIC = 1.5 * 2.0 ** 23
BT = NM + 6 * GRID_W + NM
CLAMP = 3.1415925


def constants():
    pos = np.arange(L, dtype=np.float64)
    om = TWO_PI * (pos + 0.5) / FFT_N

    def rows(m):
        out = np.zeros((128, 3, m.shape[1]), np.float64)
        for t, (p, n) in enumerate(TOK):
            for row in (0,) if t < 2 else (0, 32, 64):
                out[row:row + n, t] = m[p:p + n]
        return out

    def slab(*parts):
        flat = np.concatenate([p.reshape(128, -1) for p in parts], axis=1)
        out = np.zeros((128, 2048), np.float32)
        out[:, :flat.shape[1]] = flat
        return out

    lag = pos[:, None] * om[None, :]
    half = (pos[:, None] + 0.5) * om[None, :]
    filt = np.stack([rows(np.cos(lag)), rows(-np.sin(lag))], axis=2)
    sym = np.stack([rows(np.cos(half)), rows(-np.sin(half))], axis=2)
    ch = np.arange(CC, dtype=np.float64)
    ang = TWO_PI * ((ch[:, None] * ch[None, :FK]) % CC) / CC
    fsin = np.sin(ang)
    fsin[:, [0, FK - 1]] = 0.0
    fch = np.concatenate([np.cos(ang), fsin], axis=1).reshape(2, 128, 2 * FK).transpose(1, 0, 2)
    angl = TWO_PI * ((pos[:, None] * pos[None, NM:]) % L) / L
    norm = 1.0 / math.sqrt(L * CC)
    ftok = np.stack([rows(np.cos(angl) * norm), rows(-np.sin(angl) * norm)], axis=2)
    tables = np.stack([slab(filt), slab(sym), slab(fch, rows(np.sin(angl) * norm)), slab(ftok)])

    f32 = np.float32
    t = np.linspace(0.0, 1.0, L, dtype=f32)[:, None]
    bands = (EMB - 1) // 2
    w = f32(TWO_PI) * np.arange(L, dtype=f32)[:, None] / f32(L)
    f = np.linspace(1e-4, bands - 1, bands, dtype=f32)[None, :]
    z = np.concatenate([t, np.cos(f * w), -np.sin(f * w)], axis=-1).astype(f32)
    negt = np.zeros((128, 3), f32)
    for i, (p, n) in enumerate(TOK):
        negt[:n, i] = -t[p:p + n, 0]
    col = np.arange(GRID_W)
    cs = np.clip(col - KW // 2, 0, GRID_W - KW)
    seen = (col[None, :] >= cs[:, None]) & (col[None, :] < cs[:, None] + KW)
    mask = np.where(seen, 0.0, -1e30).astype(f32)
    mask = mask[::-1]
    return tables, np.ascontiguousarray(z.T), negt, np.concatenate([mask, mask]), np.eye(128, dtype=f32)


def build(nc, x, meta, w_stream, tables, zT, negt_in, mask_in, ident_in, params_in, mlp_in, w1, w2, w3, w4,
          decay, rpb, mbias, final_g, out):
    kg_dram = nc.dram_tensor("kspec_grid", [CH, 2, 128, 2 * 2 * CC], F32, kind="Internal").ap()
    km_dram = nc.dram_tensor("kspec_meta", [CH, 2, NM, 2 * CC], F32, kind="Internal").ap()
    y_dram = nc.dram_tensor("branch_y", [3, 128, 2 * CH, NG], F32, kind="Internal").ap()

    at = [(nc.sbuf_base + 63) // 64 * 64]

    def place(name, shape, dt=F32):
        t = nc.alloc_sbuf_tensor_at(name, shape, dt, offset=at[0])
        at[0] += (4 * int(np.prod(shape[1:])) + 63) // 64 * 64
        assert at[0] <= nc.sbuf_usable_end, (name, at[0])
        return t

    params = place("params", [128, 128])
    ident = place("ident", [128, 128])
    negt = place("negt", [128, 3])
    mask = place("mask", [128, GRID_W])
    stat = place("stat", [128, 16])
    raw = place("raw", [128, 4, 8 * CC])
    xn_at = at[0]
    xn_hi = place("xn_hi", [128, KT, L], F32R)
    xn_lo = place("xn_lo", [128, KT, L], F32R)
    xn_end = at[0]
    split_at = at[0]
    w_hi = place("w_hi", [128, 2, 8, CC], F32R)
    w_lo = place("w_lo", [128, 2, 8, CC], F32R)
    split_end = at[0]
    mix_at = at[0]
    sym_hi = place("sym_hi", [128, 3, 2, L], F32R)
    sym_lo = place("sym_lo", [128, 2, 2, L], F32R)
    fch_hi = place("fch_hi", [128, 2, 2 * FK], F32R)
    fch_lo = place("fch_lo", [128, 2, 2 * FK], F32R)
    uT_hi = place("uT_hi", [128, 3, CC], F32R)
    uT_lo = place("uT_lo", [128, 2, CC], F32R)
    ftok_hi = place("ftok_hi", [128, 3, 2, NG], F32R)
    ftok_lo = place("ftok_lo", [128, 2, 2, NG], F32R)
    fsin_hi = place("fsin_hi", [128, 3, NG], F32R)
    fsin_lo = place("fsin_lo", [128, 2, NG], F32R)
    work_at = at[0]
    kspec = place("kspec", [128, 3, 2, CC])
    bias_t = place("bias_t", [128, HC, BT])
    y_hi = place("y_hi", [128, 3, 2, CC], F32R)
    y_lo = place("y_lo", [128, 2, 2, CC], F32R)
    p2_hi, p2_lo = (a[:, :, :, :].rearrange("p t r n -> p t (r n)")[:, :, 0:2 * FK] for a in (y_hi, y_lo))
    vT_hi = place("vT_hi", [128, 3, CC], F32R)
    vT_lo = place("vT_lo", [128, 2, CC], F32R)
    pT_hi = place("pT_hi", [128, 3, NG], F32R)
    pT_lo = place("pT_lo", [128, 2, NG], F32R)
    qk_at = at[0]
    q_hi = place("q_hi", [128, 2, NG], F32R)
    q_lo = place("q_lo", [128, 2, NG], F32R)
    k_hi = place("k_hi", [128, 2, L + NM], F32R)
    k_lo = place("k_lo", [128, 2, L + NM], F32R)
    qk_end = at[0]
    at[0] = qk_at
    fi_hi = place("fi_hi", [128, 2, L], F32R)
    fi_lo = place("fi_lo", [128, 2, L], F32R)
    at[0] = qk_end
    u = place("u", [128, 2, L])
    x1 = place("x1", [128, 2, L])
    x2 = place("x2", [128, 2, L])
    v = place("v", [128, 2, L])
    o = place("o", [128, 2, NG])
    gate = place("gate", [128, 2, NG])
    gexp = place("gexp", [128, 2, NG])
    prod = place("prod", [128, 3, 2, CC])
    sco = place("sco", [128, 2, L])
    ystage = place("ystage", [128, 2, NG])
    at[0] = work_at
    xin = place("xin", [128, 3, D])
    filt_hi = place("filt_hi", [128, 3, 2, L], F32R)
    filt_lo = place("filt_lo", [128, 2, 2, L], F32R)
    kstage = place("kstage", [128, 2, 2, 2, CC])
    kmstage = place("kmstage", [NM, 2, 2, CC])
    absd = place("absd", [128, 2, 2, 2, CC])
    w4s = place("w4s", [HID, 2, 2, 2, CC])
    hid = place("hid", [HID, L])
    mlp_at = at[0]
    mlpw = place("mlpw", [HID, 3 * HID + 4])
    zt = place("zt", [EMB, L])
    red = place("red", [HID, 4, L])
    at[0] = mlp_at
    hm = place("hm", [128, 2, 2, CC])
    sd = place("sd", [128, 2, 2, CC])
    at[0] = work_at
    sd_hi = place("sd_hi", [128, 3, 2, 2, CC], F32R)
    sd_lo = place("sd_lo", [128, 2, 2, 2, CC], F32R)
    at[0] = split_end - 4 * 8 * CC
    envel = place("envel", [128, 2, 2, 2, CC])
    at[0] = mix_at
    m_hi = place("m_hi", [128, KT, NG], F32R)
    m_lo = place("m_lo", [128, KT, NG], F32R)
    m_end = at[0]
    at[0] = mix_at
    y_raw = place("y_raw", [128, 3, 2 * CH * NG])
    at[0] = m_end
    yb_hi = place("yb_hi", [128, 3, 2 * CH, NG], F32R)
    yb_lo = place("yb_lo", [128, 3, 2 * CH, NG], F32R)
    mgate = place("mgate", [128, 2, 2, NG])
    msum = place("msum", [128, 2, NG])
    mterm = place("mterm", [128, 2, NG])
    at[0] = xn_at
    h = place("h", [128, 2, D])
    fg = place("fg", [128, D])
    at[0] = m_end
    hg = place("hg", [128, 2, D])
    fsq = place("fsq", [128, 2, JB])
    fjunk = place("fjunk", [128, 2, D])

    CW, CB, SK, NGC = 0, 72, 96, 112
    with ExitStack() as ctx:
        ps = ctx.enter_context(nc.psum_tensor("ps", [128, 8, 512], F32))

        def sem(name):
            return ctx.enter_context(nc.semaphore(name))

        w_landed = [sem(f"w_landed{i}") for i in range(4)]
        hi_done = sem("hi_done")
        lo_done = sem("lo_done")
        slab_used = sem("slab_used")
        x_landed = [sem(f"x_landed{i}") for i in range(3)]
        first_landed = sem("first_landed")
        mlp_landed = sem("mlp_landed")
        ident_landed = sem("ident_landed")
        small_landed = sem("small_landed")
        w4_landed = [sem(f"w4_landed{i}") for i in range(2)]
        dec_landed = [sem(f"dec_landed{i}") for i in range(2)]
        mlp_mm = sem("mlp_mm")
        mlp_red = sem("mlp_red")
        mlp_sin = sem("mlp_sin")
        x_sq = sem("x_sq")
        x_var = sem("x_var")
        x_std = sem("x_std")
        x_rstd = sem("x_rstd")
        x_scaled = sem("x_scaled")
        x1_scaled = sem("x1_scaled")
        xt_mm = sem("xt_mm")
        xt_hi = sem("xt_hi")
        xt_lo = sem("xt_lo")
        dec_abs = sem("dec_abs")
        env_done = sem("env_done")
        h4_mm = sem("h4_mm")
        h4_read = sem("h4_read")
        sd_zeroed = sem("sd_zeroed")
        sd_done = sem("sd_done")
        sdhi_done = sem("sdhi_done")
        sdlo_done = sem("sdlo_done")
        k_mm = sem("k_mm")
        k_evac = sem("k_evac")
        k_written = sem("k_written")
        a_ev = sem("a_ev")
        proj_read = sem("proj_read")
        t_mm = sem("t_mm")
        t_hi = sem("t_hi")
        t_lo = sem("t_lo")
        fwd_mm = sem("fwd_mm")
        y_full = sem("y_full")
        yhi_done = sem("yhi_done")
        ylo_done = sem("ylo_done")
        inv_mm = sem("inv_mm")
        z_done = sem("z_done")
        s_mm = sem("s_mm")
        smax_done = sem("smax_done")
        exp_done = sem("exp_done")
        p_done = sem("p_done")
        pt_mm = sem("pt_mm")
        pt_hi = sem("pt_hi")
        pt_lo = sem("pt_lo")
        pv_mm = sem("pv_mm")
        o_done = sem("o_done")
        n1_mm = sem("n1_mm")
        n1_hi = sem("n1_hi")
        n1_lo = sem("n1_lo")
        n2_mm = sem("n2_mm")
        ya_done = sem("ya_done")
        yb_done = sem("yb_done")
        yc_done = sem("yc_done")
        y_written = sem("y_written")
        k_landed = sem("k_landed")
        b_landed = sem("b_landed")
        b_ready = sem("b_ready")
        y_landed = [sem(f"y_landed{i}") for i in range(3)]
        bhi_done = sem("bhi_done")
        blo_done = sem("blo_done")
        gate_done = sem("gate_done")
        br_read = sem("br_read")
        msum_done = sem("msum_done")
        mhi_done = sem("mhi_done")
        mlo_done = sem("mlo_done")
        h_landed = sem("h_landed")
        h_sum = sem("h_sum")
        hg_done = sem("hg_done")
        f_sq = sem("f_sq")
        f_var = sem("f_var")
        f_std = sem("f_std")
        f_rstd = sem("f_rstd")
        f_done = sem("f_done")
        f1_done = sem("f1_done")
        out_written = sem("out_written")
        pool_link = sem("pool_link")
        zeroed = sem("zeroed")
        dve_link = sem("dve_link")

        block = ctx.enter_context(nc.Block())
        SMALL = 10

        @block.sync
        def _(sp):
            sp.dma_start(zt[:, :], zT).then_inc(first_landed, 16)
            sp.dma_start(mlpw[0:EMB, 0:HID], w1).then_inc(first_landed, 16)
            sp.dma_start(mlpw[:, 3 * HID:], mlp_in).then_inc(first_landed, 16)
            sp.dma_start(xin[:, 0, :], x[0:128, :]).then_inc(x_landed[0], 16)
            sp.dma_start(xin[:, 1, :], x[128:256, :]).then_inc(x_landed[1], 16)
            sp.dma_start(xin[0:NM, 2, :], meta).then_inc(x_landed[2], 16)
            sp.dma_start(ident[:, :], ident_in).then_inc(ident_landed, 16)
            for i in range(NCONST):
                sp.dma_start(raw[:, i, :], tables[i]).then_inc(w_landed[i], 16)
            with sp.Fori(0, CH) as c:
                for t in range(S1):
                    sp.wait_ge(lo_done, c * S1 + t + 1)
                    sp.dma_start(raw[:, t % 4, :], w_stream[bass.ds(c * S1 + t, 1), :, :].rearrange("a p n -> p (a n)")
                                 ).then_inc(w_landed[t % 4], 16)
            with sp.Fori(0, JB // 2) as i:
                for t in range(S2):
                    sp.wait_ge(lo_done, i * S2 + (W2 + t + 2))
                    sp.dma_start(raw[:, t % 3, :],
                                 w_stream[bass.ds(i * S2 + (W2 + t), 1), :, :].rearrange("a p n -> p (a n)")
                                 ).then_inc(w_landed[t % 3], 16)
            with sp.Fori(0, JB // 2) as i:
                for t in range(4):
                    sp.wait_ge(lo_done, i * 4 + (W3 + t + 2))
                    sp.dma_start(raw[:, t % 4, :],
                                 w_stream[bass.ds(i * 4 + (W3 + t), 1), :, :].rearrange("a p n -> p (a n)")
                                 ).then_inc(w_landed[t % 4], 16)
            for half in range(2):
                cols = slice(half * D // 2, (half + 1) * D // 2)
                for tt, done in enumerate((f_done, f1_done)):
                    sp.wait_ge(done, half + 1)
                    sp.dma_start(out[128 * tt:128 * tt + 128, cols], hg[:, tt, cols]).then_inc(out_written, 16)
            sp.wait_ge(out_written, 64)

        @block.gpsimd
        def _(pool):
            pool.dma_start(mlpw[:, HID:2 * HID], w2).then_inc(mlp_landed, 16)
            pool.dma_start(mlpw[:, 2 * HID:3 * HID], w3).then_inc(mlp_landed, 16)
            pool.dma_start(params[:, :], params_in).then_inc(small_landed, 16)
            pool.dma_start(negt[:, :], negt_in).then_inc(small_landed, 16)
            pool.dma_start(mask[0:64, :], mask_in[0:64, :]).then_inc(k_written, 16)
            pool.dma_start(mask[64:128, :], mask_in[64:128, :]).then_inc(y_written, 16)

            def load_filter(c, par):
                pool.dma_start(w4s[:, par, :, :, :].rearrange("p a b n -> p (a b n)"),
                               w4[bass.ds(c, 1), :, :].rearrange("a p n -> p (a n)")).then_inc(w4_landed[par], 16)
                pool.dma_start(absd[:, par, :, :, :].rearrange("p a b n -> p (a b n)"),
                               decay[bass.ds(c, 1), :].rearrange("a n -> (a n)").partition_broadcast(128)
                               ).then_inc(dec_landed[par], 16)

            def store_spectrum(c):
                pool.wait_ge(k_evac, c * 6 + 12)
                pool.dma_start(kg_dram[bass.ds(c, 1), :, :, :].rearrange("a o p n -> p (a o) n"),
                               kstage[:, :, :, :, :].rearrange("p o f r n -> p o (f r n)")).then_inc(k_written, 16)
                pool.dma_start(km_dram[bass.ds(c, 1), :, :, :].rearrange("a o p n -> p (a o) n"),
                               kmstage[:, :, :, :].rearrange("p o r n -> p o (r n)")).then_inc(k_written, 16)

            load_filter(0, 0)
            load_filter(1, 1)

            def const_low(i, dst, src, hi):
                pool.wait_ge(hi_done, i + 1)
                if i:
                    pool.wait_ge(lo_done, i)
                return nc.gpsimd.tensor_tensor(dst, src, hi.bitcast(F32), ALU.subtract)

            def const_stacked(i, dst, hi, n):
                const_low(i, dst[:, 0:2, :, :].rearrange("p a b n -> p (a b n)"), raw[:, i, 0:4 * n],
                          hi[:, 0:2, :, :].rearrange("p a b n -> p (a b n)")).then_inc(pool_link, 1)
                pool.wait_ge(pool_link, {0: 1, 1: 2, 3: 5}[i])
                part = hi[32:32 + NM, 2, :, :].rearrange("p b n -> p (b n)")
                const_low(i, part, raw[32:32 + NM, i, 4 * n:6 * n], part).then_inc(lo_done, 1)

            const_stacked(0, filt_lo, filt_hi, L)
            pool.wait_ge(lo_done, 1)
            pool.wait_ge(xt_mm, KT)
            nc.gpsimd.memset(sd_hi[0:STACK, 2, :, :, :].rearrange("p a b n -> p (a b n)").bitcast(F32), 0.0).then_inc(sd_zeroed, 1)
            pool.wait_ge(sd_zeroed, 1)
            for c in range(CH):
                if c == 0:
                    const_stacked(1, sym_lo, sym_hi, L)
                if c == 1:
                    const_low(2, fch_lo[:, :, :].rearrange("p a n -> p (a n)"), raw[:, 2, 0:4 * FK],
                              fch_hi[:, :, :].rearrange("p a n -> p (a n)")).then_inc(pool_link, 1)
                    pool.wait_ge(pool_link, 3)
                    const_low(2, fsin_lo[:, :, :].rearrange("p a n -> p (a n)"), raw[:, 2, 4 * FK:4 * FK + 2 * NG],
                              fsin_hi[:, 0:2, :].rearrange("p a n -> p (a n)")).then_inc(pool_link, 1)
                    pool.wait_ge(pool_link, 4)
                    part = fsin_hi[32:32 + NM, 2, :]
                    const_low(2, part, raw[32:32 + NM, 2, 4 * FK + 2 * NG:4 * FK + 3 * NG], part).then_inc(lo_done, 1)
                if c == 2:
                    const_stacked(3, ftok_lo, ftok_hi, NG)
                if c + 2 < CH:
                    pool.wait_ge(h4_mm, c * 3 + 3)
                    pool.wait_ge(env_done, c * 3 + 3)
                    load_filter(c + 2, c % 2)
                store_spectrum(c)
            pool.wait_ge(k_written, 16 + 32 * CH)
            pool.wait_ge(k_mm, 6 * CH)
            pool.wait_ge(xt_mm, KT)
            pool.wait_ge(lo_done, NCONST)
            for stacked in (uT_hi[0:STACK, 2, :], vT_hi[0:STACK, 2, :], pT_hi[0:STACK, 2, :],
                            y_hi[0:STACK, 2, :, :].rearrange("p r n -> p (r n)")):
                last = nc.gpsimd.memset(stacked.bitcast(F32), 0.0)
            last.then_inc(zeroed, 1)

            def load_bias(c):
                for s in range(2):
                    for hh in range(HC):
                        src = bass.AP(rpb.tensor, c * (HC * RPB_R * RPB_C) + ((hh * RPB_R + 5 - s) * RPB_C + KW - GRID_W),
                                      [[1, GRID_W], [RPB_C, 6], [1, GRID_W]])
                        pool.dma_start(bias_t[64 * s:64 * s + 64, hh, NM:NM + 6 * GRID_W].rearrange(
                            "p (j k) -> p j k", j=6), src).then_inc(b_landed, 16)
                for lo in (0, NM + 6 * GRID_W):
                    pool.dma_start(bias_t[:, :, lo:lo + NM],
                                   mbias[bass.ds(c, 1), :].rearrange("a (h m) -> (a h) m", h=HC).partition_broadcast(128)
                                   ).then_inc(b_landed, 16)
                pool.wait_ge(b_landed, (c + 1) * (16 * (2 * HC + 2)))
                for hh in range(HC):
                    grid = bias_t[:, hh, NM:NM + 6 * GRID_W].rearrange("p (j k) -> p j k", j=6)
                    msk = mask[:, :].rearrange("p (a k) -> p a k", a=1).broadcast_to([128, 6, GRID_W])
                    last = nc.gpsimd.tensor_tensor(grid, grid, msk, ALU.add)
                last.then_inc(b_ready, 1)

            def load_spectrum(c, order):
                pool.dma_start(kspec[:, 0:2, :, :].rearrange("p f r n -> p (f r n)"),
                               kg_dram[bass.ds(c, 1), order, :, :].rearrange("a p n -> p (a n)")).then_inc(k_landed, 16)
                pool.dma_start(kspec[0:NM, 2, :, :].rearrange("p r n -> p (r n)"),
                               km_dram[bass.ds(c, 1), order, :, :].rearrange("a p n -> p (a n)")).then_inc(k_landed, 16)

            def second_order(c):
                pool.wait_ge(y_full, c * 6 + 3)
                load_spectrum(c, 1)

            def store_y(c, branch, done):
                pool.wait_ge(done, c + 1)
                pool.dma_start(y_dram[branch, :, bass.ds(c * 2, 2), :], ystage[:, :, :]).then_inc(y_written, 16)

            load_bias(0)
            load_spectrum(0, 0)
            def load_y(place_, branch, written):
                pool.wait_ge(y_written, written)
                pool.dma_start(y_raw[:, place_, :], y_dram[branch].rearrange("p k n -> p (k n)")).then_inc(y_landed[place_], 16)

            with pool.Fori(1, CH) as c:
                second_order(c - 1)
                store_y(c - 1, 0, ya_done)
                store_y(c - 1, 2, yc_done)
                pool.wait_ge(smax_done, c * HC)
                load_bias(c)
                pool.wait_ge(y_full, c * 6)
                load_spectrum(c, 0)
                store_y(c - 1, 1, yb_done)
            second_order(CH - 1)
            store_y(CH - 1, 0, ya_done)
            pool.wait_ge(inv_mm, 2 * CH)
            load_y(0, 0, 48 * CH - 16)
            store_y(CH - 1, 2, yc_done)
            pool.wait_ge(n1_mm, 3 * CH)
            load_y(1, 2, 48 * CH)
            store_y(CH - 1, 1, yb_done)
            pool.wait_ge(n2_mm, CH)
            load_y(2, 1, 48 * CH + 16)
            pool.wait_ge(slab_used, W3)
            for tt in range(2):
                pool.dma_start(h[:, tt, :], x[128 * tt:128 * tt + 128, :]).then_inc(h_landed, 16)
            pool.dma_start(fg[:, :], final_g.partition_broadcast(128)).then_inc(h_landed, 16)

        def slot_main(c, t):
            return t % 4, (c * 5 + (t // 4 + 2)) * 16

        def slot_merge(i, t):
            return t % 3, (i * 6 + (t // 3 + 22)) * 16

        def slot_out(i, t):
            return t % 4, (i + ((46 if t % 4 < 3 else 22) + t // 4)) * 16

        @block.tensor
        def _(pe):
            mm = nc.tensor.matmul

            def three(out_ap, a_hi, a_lo, b_hi, b_lo, first, last, skip=False):
                mm(out_ap, a_hi, b_hi, start=first, stop=False)
                mm(out_ap, a_hi, b_lo, start=False, stop=False)
                return mm(out_ap, a_lo, b_hi, start=False, stop=last)

            def stacked(out_ap, a, b, first, last):
                return mm(out_ap, a, b, start=first, stop=last)

            pe.wait_ge(first_landed, 48)
            for layer in range(3):
                if layer == 1:
                    pe.wait_ge(mlp_landed, 32)
                if layer == 0:
                    ins = mm(ps[0:HID, 7, 0:L], mlpw[0:EMB, 0:HID], zt[:, :], start=True, stop=True)
                else:
                    pe.wait_ge(mlp_sin, layer)
                    ins = mm(ps[0:HID, 7, 0:L], mlpw[:, HID * layer:HID * layer + HID], hid[:, :], start=True, stop=True)
                ins.then_inc(mlp_mm, 1)
            pe.wait_ge(ident_landed, 16)
            pe.wait_ge(x_scaled, 2)
            pe.wait_ge(x1_scaled, 1)
            for k in range(KT):
                if k >= 4:
                    pe.wait_ge(xt_lo, k - 3)
                for t, (p, n) in enumerate(TOK):
                    last = nc.tensor.transpose(ps[:, k % 4, p:p + n], xin[0:n, t, 128 * k:128 * k + 128], ident[0:n, 0:n])
                last.then_inc(xt_mm, 1)
            pe.wait_ge(mlp_sin, 3)
            pe.wait_ge(xt_lo, KT)
            pe.wait_ge(lo_done, 1)

            def make_h4(c, j, par):
                p, n = TOK[FORDER[j]]
                if j == 0:
                    pe.wait_ge(w4_landed[par], (c - par) * 8 + 16)
                pe.wait_ge(h4_read, c * 3 + (j + 1))
                for o_ in range(2):
                    last = mm(ps[0:n, 6 + o_, :], hid[:, p:p + n], w4s[:, par, o_, :, :].rearrange("p d n -> p (d n)"),
                              start=True, stop=True)
                last.then_inc(h4_mm, 1)

            def add_spectra(c, j, es):
                t = FORDER[j]
                n = TOK[t][1]
                for e in es:
                    f, ri = e // 2, e % 2
                    fp, fn = TOK[f]
                    if j == 0:
                        pe.wait_ge(k_evac, c * 6 + (e + 1))
                    if e == 0:
                        pe.wait_ge(sdlo_done, c * 3 + (j + 1))
                    if t == 2:
                        last = mm(ps[0:fn, e, :], filt_hi[0:STACK, t, ri, fp:fp + fn],
                                  sd_hi[0:STACK, t, ri, :, :].rearrange("p o n -> p (o n)"), start=False, stop=False)
                    else:
                        last = three(ps[0:fn, e, :], filt_hi[0:n, t, ri, fp:fp + fn], filt_lo[0:n, t, ri, fp:fp + fn],
                                     sd_hi[0:n, t, ri, :, :].rearrange("p o n -> p (o n)"),
                                     sd_lo[0:n, t, ri, :, :].rearrange("p o n -> p (o n)"), j == 0, j == 2)
                    if j == 2:
                        last.then_inc(k_mm, 1)

            def filters(c, par, more):
                for j in range(3):
                    add_spectra(c, j, (0, 1, 2))
                    if j == 0:
                        make_h4(c, 2, par)
                    elif more:
                        make_h4(c + 1, j - 1, 1 - par)
                    add_spectra(c, j, (3, 4, 5))

            make_h4(0, 0, 0)
            make_h4(0, 1, 0)
            with pe.Fori(0, CH // 2 - 1) as cc:
                filters(cc * 2, 0, True)
                filters(cc * 2 + 1, 1, True)
            filters(CH - 2, 0, True)
            filters(CH - 1, 1, False)

            def proj_slab(par, bank, half, p0):
                for nt in range(2):
                    for k in range(8):
                        last = three(ps[:, bank + nt, 0:L - p0], w_hi[:, par, k, 128 * nt:128 * nt + 128],
                                     w_lo[:, par, k, 128 * nt:128 * nt + 128], xn_hi[:, 8 * half + k, p0:L],
                                     xn_lo[:, 8 * half + k, p0:L], half == 0 and k == 0, half == 1 and k == 7)
                last.then_inc(slab_used, 1)

            def turn(src, bank):
                for t, (p, n) in enumerate(TOK):
                    for i in range(2):
                        dst = ps[:, bank, CC * t + 128 * i:CC * t + 128 * i + 128] if t < 2 else \
                            ps[0:n, bank + 1, 128 * i:128 * i + 128]
                        last = nc.tensor.transpose(dst, src[:, i, p:p + n], ident[:, :])
                last.then_inc(t_mm, 1)

            def forward(f, bank):
                fp, fn = TOK[f]
                for ri in range(2):
                    for t in range(2):
                        three(ps[0:fn, bank, CC * ri:CC * ri + CC], sym_hi[:, t, ri, fp:fp + fn],
                              sym_lo[:, t, ri, fp:fp + fn], uT_hi[:, t, :], uT_lo[:, t, :], t == 0, False)
                    last = stacked(ps[0:fn, bank, CC * ri:CC * ri + CC], sym_hi[0:STACK, 2, ri, fp:fp + fn],
                                   uT_hi[0:STACK, 2, :], False, True)
                last.then_inc(fwd_mm, 1)

            def inverse(p0):
                for i in range(2):
                    for e in range(4):
                        f, ri = e // 2, e % 2
                        three(ps[:, 4 + i, 0:L - p0], y_hi[:, f, ri, 128 * i:128 * i + 128],
                              y_lo[:, f, ri, 128 * i:128 * i + 128], sym_hi[:, f, ri, p0:L], sym_lo[:, f, ri, p0:L],
                              e == 0, False)
                    for ri in range(2):
                        last = stacked(ps[:, 4 + i, 0:L - p0], y_hi[0:STACK, 2, ri, 128 * i:128 * i + 128],
                                       sym_hi[0:STACK, 2, ri, p0:L], False, ri == 1)
                last.then_inc(inv_mm, 1)

            def scores(hh):
                i, r = hh // 2, slice(64 * (hh % 2), 64 * (hh % 2) + 64)
                for a in range(2):
                    ks = slice(NM, NM + L) if a == 0 else slice(0, L)
                    last = three(ps[:, 6 + a, 0:L], q_hi[r, i, 128 * a:128 * a + 128], q_lo[r, i, 128 * a:128 * a + 128],
                                 k_hi[r, i, ks], k_lo[r, i, ks], True, True)
                last.then_inc(s_mm, 1)

            def turn_p():
                for a in range(2):
                    g0 = 0 if a == 0 else NM
                    m0 = NG if a == 0 else 0
                    for kt in range(2):
                        nc.tensor.transpose(ps[:, 6, NG * kt + 128 * a:NG * kt + 128 * a + 128],
                                            sco[:, a, g0 + 128 * kt:g0 + 128 * kt + 128], ident[:, :])
                    last = nc.tensor.transpose(ps[0:NM, 7, 128 * a:128 * a + 128], sco[:, a, m0:m0 + NM], ident[:, :])
                last.then_inc(pt_mm, 1)

            def attend(hh):
                i = hh // 2
                for t in range(2):
                    three(ps[:, 7, NG:2 * NG], vT_hi[:, t, 128 * i:128 * i + 128], vT_lo[:, t, 128 * i:128 * i + 128],
                          pT_hi[:, t, :], pT_lo[:, t, :], t == 0, False)
                stacked(ps[:, 7, NG:2 * NG], vT_hi[0:STACK, 2, 128 * i:128 * i + 128], pT_hi[0:STACK, 2, :], False,
                        True).then_inc(pv_mm, 1)

            def fnet_channels(t, bank):
                p, n = TOK[t]
                for i in range(2):
                    last = three(ps[0:n, bank, 0:2 * FK], fi_hi[:, i, p:p + n], fi_lo[:, i, p:p + n], fch_hi[:, i, :], fch_lo[:, i, :],
                                 i == 0, i == 1)
                last.then_inc(n1_mm, 1)

            def fnet_tokens():
                for i in range(2):
                    out_ap = ps[:, 4, NG * i:NG * i + NG]
                    for e in range(6):
                        t, ri = e // 2, e % 2
                        k0 = FK * ri + i
                        tab = (fsin_hi[:, t, :] if i and ri else ftok_hi[:, t, ri, :])
                        if t == 2:
                            last = stacked(out_ap, p2_hi[0:STACK, t, k0:k0 + 128], tab[0:STACK], False, e == 5)
                        else:
                            tab_lo = (fsin_lo[:, t, :] if i and ri else ftok_lo[:, t, ri, :])
                            three(out_ap, p2_hi[:, t, k0:k0 + 128], p2_lo[:, t, k0:k0 + 128], tab, tab_lo, e == 0, False)
                last.then_inc(n2_mm, 1)

            pe.wait_ge(k_evac, CH * 6 + 2)
            with pe.Fori(0, CH) as c:
                for t in range(S1):
                    name, _, n = BLOCKS[t // 2]
                    if t % 2 == 0:
                        pe.wait_ge(proj_read, c * NBLK + (t // 2 + 1))
                    if t == 2:
                        pe.wait_ge(k_evac, CH * 6 + 4)
                    pe.wait_ge(lo_done, c * S1 + (NCONST + t + 1))
                    proj_slab(t % 2, 2 * (t // 2 % 2), t % 2, L - n)
                    if t == 3:
                        pe.wait_ge(proj_read, c * NBLK + 3)
                        pe.wait_ge(k_evac, CH * 6 + 6)
                        turn(u, 4)
                    if t == 4:
                        pe.wait_ge(t_lo, c * 3 + 1)
                        forward(0, 4)
                        forward(1, 5)
                    if t == 5:
                        pe.wait_ge(y_full, c * 6 + 1)
                        forward(2, 4)
                    if t == 6:
                        pe.wait_ge(proj_read, c * NBLK + 5)
                        scores(0)
                    if t == 8:
                        pe.wait_ge(p_done, c * HC + 1)
                        turn_p()
                        pe.wait_ge(proj_read, c * NBLK + 6)
                        pe.wait_ge(y_full, c * 6 + 3)
                        turn(v, 4)
                    if t == 9:
                        pe.wait_ge(pt_lo, c * HC + 1)
                        scores(1)
                        pe.wait_ge(t_lo, c * 3 + 2)
                        pe.wait_ge(ylo_done, c * 6 + 3)
                        inverse(0)
                    if t in (10, 12, 14):
                        hh = (t - 8) // 2
                        pe.wait_ge(p_done, c * HC + hh + 1)
                        attend(hh - 1)
                        turn_p()
                    if t in (11, 13):
                        hh = (t - 7) // 2
                        pe.wait_ge(o_done, c * HC + hh - 1)
                        scores(hh)
                    if t == 11:
                        pe.wait_ge(z_done, c + 1)
                        turn(x1, 4)
                    if t == 12:
                        pe.wait_ge(t_lo, c * 3 + 3)
                        forward(0, 4)
                        forward(1, 5)
                    if t == 13:
                        pe.wait_ge(y_full, c * 6 + 4)
                        forward(2, 4)
                    if t == 15:
                        pe.wait_ge(ylo_done, c * 6 + 6)
                        inverse(NM)
                        pe.wait_ge(o_done, c * HC + 3)
                        attend(3)
                    if t == 16:
                        pe.wait_ge(proj_read, c * NBLK + 10)
                        pe.wait_ge(ya_done, c + 1)
                        fnet_channels(0, 4)
                        fnet_channels(1, 5)
                    if t == 17:
                        pe.wait_ge(n1_lo, c * 3 + 1)
                        fnet_channels(2, 4)
                    if t == 19:
                        pe.wait_ge(n1_lo, c * 3 + 3)
                        fnet_tokens()

            with pe.Fori(0, JB // 2) as i:
                for t in range(S2):
                    b, part = t % 9 // 3, t % 3
                    m = t // 3
                    pair = 2 * ((2 * m + (part == 2)) % 4)
                    if part == 0:
                        pe.wait_ge(gate_done, i * 6 + (m + 1))
                        if m == 0:
                            pe.wait_ge(proj_read, NBLK * CH + 1)
                        if m == 1:
                            pe.wait_ge(yb_done, CH)
                    if part == 2:
                        pe.wait_ge(br_read, i * 6 + (m + 1))
                        if m == 0:
                            pe.wait_ge(proj_read, NBLK * CH + 2)
                        pe.wait_ge(blo_done, b + 1)
                    pe.wait_ge(lo_done, i * S2 + (NCONST + W2 + t + 1))
                    if part < 2:
                        proj_slab(t % 2, pair, part, NM)
                    else:
                        for nt in range(2):
                            for k in range(8):
                                last = three(ps[:, pair + nt, 0:NG], w_hi[:, t % 2, k, 128 * nt:128 * nt + 128],
                                             w_lo[:, t % 2, k, 128 * nt:128 * nt + 128], yb_hi[:, b, k, :], yb_lo[:, b, k, :],
                                             k == 0, k == 7)
                        last.then_inc(slab_used, 1)

            with pe.Fori(0, JB // 2) as i:
                for t in range(4):
                    half, nb = t // 2, t % 2
                    if half == 0:
                        pe.wait_ge(h_sum, i * 2 + (nb + 1))
                    if t == 0:
                        pe.wait_ge(gate_done, 3 * JB + 2)
                        pe.wait_ge(mlo_done, JB // 2)
                    if t == 1:
                        pe.wait_ge(br_read, 3 * JB + 2)
                    if t == 2:
                        pe.wait_ge(mlo_done, JB)
                    pe.wait_ge(lo_done, i * 4 + (NCONST + W3 + t + 1))
                    for tt in range(2):
                        for k in range(8):
                            kk = 8 * half + k
                            last = three(ps[:, 2 * nb + tt, 0:CC], m_hi[:, kk, 128 * tt:128 * tt + 128],
                                         m_lo[:, kk, 128 * tt:128 * tt + 128], w_hi[:, t % 2, k, :], w_lo[:, t % 2, k, :],
                                         kk == 0, kk == KT - 1)
                    last.then_inc(slab_used, 1)

        @block.scalar
        def _(act):
            A = nc.scalar.activation

            def split(where, par, w):
                slot, landed = where
                act.wait_ge(w_landed[slot], landed)
                act.wait_ge(slab_used, w - 1)
                A(w_hi[:, par, :, :].rearrange("p k n -> p (k n)"), raw[:, slot, :], ACT.Copy).then_inc(hi_done, 1)

            def split_const(i, dst, n):
                act.wait_ge(w_landed[i], 16)
                A(dst, raw[:, i, 0:n], ACT.Copy).then_inc(hi_done, 1)

            def flat4(t_):
                return t_[:, :, :, :].rearrange("p a b n -> p (a b n)")

            def square(t):
                n = TOK[t][1]
                act.wait_ge(x_landed[t], 16)
                if t:
                    act.wait_ge(x_sq, t)
                A(ps[0:n, 0:4, :].rearrange("p a n -> p (a n)"), xin[0:n, t, :], ACT.Square,
                  accum_out=stat[0:n, t:t + 1]).then_inc(x_sq, 1)

            def sine(layer):
                act.wait_ge(mlp_red, layer + 1)
                A(hid[:, :], red[:, 0, :], ACT.Sin).then_inc(mlp_sin, 1)

            act.wait_ge(first_landed, 48)
            A(stat[0:EMB, 15:16], zt[:, 0:1], ACT.Sin)
            square(0)
            sine(0)
            square(1)
            square(2)
            sine(1)
            act.wait_ge(x_var, 3)
            for t, (p, n) in enumerate(TOK):
                last = A(stat[0:n, 8 + t:9 + t], stat[0:n, 4 + t:5 + t], ACT.Sqrt)
            last.then_inc(x_std, 1)
            act.wait_ge(x_rstd, 1)
            A(xin[:, 1, :], xin[:, 1, :], ACT.Copy, scale=stat[:, 13:14]).then_inc(x1_scaled, 1)
            split_const(0, flat4(filt_hi), 6 * L)

            def magnitudes(c, par):
                act.wait_ge(dec_landed[par], (c - par) * 8 + 16)
                A(absd[:, par, :, :, :], absd[:, par, :, :, :], ACT.Abs).then_inc(dec_abs, 1)

            act.wait_ge(small_landed, 32)
            for k in range(KT):
                if k == 4:
                    sine(2)
                act.wait_ge(xt_mm, k + 1)
                ins = A(xn_hi[:, k, :], ps[:, k % 4, 0:L], ACT.Copy, scale=params[:, NGC + k:NGC + k + 1])
                ins.then_inc(xt_hi, 1)

            def envelope(c, j, par):
                t = FORDER[j]
                n = TOK[t][1]
                if j == 0:
                    act.wait_ge(dec_abs, c + 1)
                if c or j > 1:
                    act.wait_ge(h4_read, c * 3 + j)
                A(envel[0:n, (par + j) % 2, :, :, :], absd[0:n, par, :, :, :], ACT.Exp, scale=negt[0:n, t:t + 1]).then_inc(env_done, 1)

            def sd_high(c, j):
                t = FORDER[j]
                n = TOK[t][1]
                if t == 2 and c == 0:
                    act.wait_ge(sd_zeroed, 1)
                act.wait_ge(sd_done, c * 3 + j + 1)
                ins = A(sd_hi[0:n, t, :, :, :], sd[0:n, :, :, :], ACT.Copy)
                if t == 2:
                    ins = A(sd_hi[32:32 + n, t, :, :, :], sd[0:n, :, :, :], ACT.Copy)
                ins.then_inc(sdhi_done, 1)

            def store_spectra(c, es):
                act.wait_ge(k_written, 16 + 32 * c)
                for e in es:
                    f, ri = e // 2, e % 2
                    act.wait_ge(k_mm, c * 6 + (e + 1))
                    dst = kstage[:, :, f, ri, :] if f < 2 else kmstage[:, :, ri, :]
                    A(dst, ps[0:TOK[f][1], e, :].rearrange("p (o n) -> p o n", o=2), ACT.Copy,
                      scale=2.0 / FFT_N).then_inc(k_evac, 1)

            def split_first(w):
                act.wait_ge(w_landed[w], 32)
                A(w_hi[:, w, :, :].rearrange("p k n -> p (k n)"), raw[:, w, :], ACT.Copy).then_inc(hi_done, 1)

            act.wait_ge(xt_mm, KT)
            magnitudes(0, 0)
            envelope(0, 0, 0)
            envelope(0, 1, 0)
            for c in range(CH):
                sd_high(c, 0)
                if c:
                    store_spectra(c - 1, (0, 1, 2))
                envelope(c, 2, c % 2)
                if c:
                    store_spectra(c - 1, (3, 4, 5))
                sd_high(c, 1)
                if c == 0:
                    split_const(1, flat4(sym_hi), 6 * L)
                if c == 1:
                    act.wait_ge(w_landed[2], 16)
                    A(fch_hi[:, :, :].rearrange("p a n -> p (a n)"), raw[:, 2, 0:4 * FK], ACT.Copy)
                    A(fsin_hi[:, :, :].rearrange("p a n -> p (a n)"), raw[:, 2, 4 * FK:4 * FK + 3 * NG],
                      ACT.Copy).then_inc(hi_done, 1)
                if c == 2:
                    split_const(3, flat4(ftok_hi), 6 * NG)
                if c + 1 < CH:
                    magnitudes(c + 1, (c + 1) % 2)
                    envelope(c + 1, 0, (c + 1) % 2)
                if c == CH - 1:
                    split_first(0)
                sd_high(c, 2)
                if c + 1 < CH:
                    envelope(c + 1, 1, (c + 1) % 2)
            split_first(1)
            store_spectra(CH - 1, range(6))

            def evac(c, name, b):
                bank = 2 * (b % 2)
                act.wait_ge(slab_used, c * S1 + (2 * b + 2))
                src = ps[:, bank:bank + 2, 0:L]
                src16 = ps[:, bank:bank + 2, 0:NG]
                if name in ("u", "x1", "x2"):
                    dst = {"u": u, "x1": x1, "x2": x2}[name]
                    t0 = {"u": 0, "x1": 8, "x2": 16}[name]
                    p0 = L - BLOCKS[b][2]
                    for i in range(2):
                        ins = A(dst[:, i, p0:L], ps[:, bank + i, 0:L - p0], ACT.Identity,
                                bias=params[:, bass.ds(c * 2 + (CB + t0 + i), 1)],
                                scale=params[:, bass.ds(c * 2 + (CW + 24 + t0 + i), 1)])
                elif name == "q":
                    for i in range(2):
                        ins = A(q_hi[:, i, :].rearrange("p (r n) -> p r n", r=4),
                                ps[:, bank + i, 0:NG].rearrange("p (r n) -> p r n", r=4)[:, :, ::-1], ACT.Copy, scale=0.125)
                elif name == "k":
                    A(k_hi[:, :, 0:L], src, ACT.Copy)
                    ins = A(k_hi[:, :, L:L + NM], ps[:, bank:bank + 2, 0:NM], ACT.Copy)
                elif name == "fin":
                    ins = A(fi_hi[:, :, :], src, ACT.Copy)
                else:
                    act.wait_ge(proj_read, c * NBLK + {"hgate": 2, "ngate": 9, "fgate": 11}[name])
                    ins = A(gexp[:, :, :], src16, ACT.Exp, scale=-1.0)
                ins.then_inc(a_ev, 1)

            def turned(n_th, done, dst, bank, ready, w=CC, twin=32):
                act.wait_ge(ready, n_th)
                A(dst[:, 0:2, :], ps[:, bank, :].rearrange("p (t n) -> p t n", t=2), ACT.Copy)
                A(dst[0:NM, 2, :], ps[0:NM, bank + 1, 0:w], ACT.Copy)
                A(dst[twin:twin + NM, 2, :], ps[0:NM, bank + 1, 0:w], ACT.Copy).then_inc(done, 1)

            def spectra(c, fs, order):
                for f in fs:
                    n = TOK[f][1]
                    act.wait_ge(y_full, c * 6 + (3 * order + f + 1))
                    ins = A(y_hi[0:n, f, :, :], prod[0:n, 2, :, :], ACT.Copy)
                    if f == 2:
                        ins = A(y_hi[32:32 + n, f, :, :], prod[0:n, 2, :, :], ACT.Copy)
                    ins.then_inc(yhi_done, 1)

            def soft(c, hh):
                act.wait_ge(smax_done, c * HC + hh + 1)
                for a in range(2):
                    ins = A(sco[:, a, :], sco[:, a, :], ACT.Exp, bias=stat[:, 2 + a:3 + a], accum_out=stat[:, 4 + a:5 + a])
                ins.then_inc(exp_done, 1)

            with act.Fori(0, CH) as c:
                for t in range(S1):
                    split(slot_main(c, t + 2), t % 2, c * S1 + (t + 2))
                    if t == 1:
                        act.wait_ge(k_written, 16 + 32 * CH)
                        act.wait_ge(zeroed, 1)
                    if t % 2 and BLOCKS[t // 2][0] != "v":
                        evac(c, BLOCKS[t // 2][0], t // 2)
                    if t == 3:
                        turned(c * 3 + 1, t_hi, uT_hi, 4, t_mm)
                    if t == 4:
                        spectra(c, (0, 1), 0)
                    if t == 5:
                        spectra(c, (2,), 0)
                    if t == 6:
                        soft(c, 0)
                    if t in (8, 10, 12, 14):
                        turned(c * HC + (t - 6) // 2, pt_hi, pT_hi, 6, pt_mm, NG, 64)
                    if t == 8:
                        turned(c * 3 + 2, t_hi, vT_hi, 4, t_mm)
                    if t in (9, 11, 13):
                        soft(c, (t - 7) // 2)
                    if t == 11:
                        turned(c * 3 + 3, t_hi, uT_hi, 4, t_mm)
                    if t == 12:
                        spectra(c, (0, 1), 1)
                    if t == 13:
                        spectra(c, (2,), 1)
                    if t == 16:
                        for f in range(2):
                            act.wait_ge(n1_mm, c * 3 + f + 1)
                            A(p2_hi[:, f, :], ps[:, 4 + f, 0:2 * FK], ACT.Copy).then_inc(n1_hi, 1)
                    if t == 17:
                        act.wait_ge(n1_mm, c * 3 + 3)
                        for row in (0, 32):
                            ins = A(p2_hi[row:row + NM, 2, :], ps[0:NM, 4, 0:2 * FK], ACT.Copy)
                        ins.then_inc(n1_hi, 1)

            A(stat[:, 13:14], params[:, 0:1], ACT.Copy).then_inc(gate_done, 2)

            def split_branch(b):
                act.wait_ge(y_landed[b], 16)
                A(yb_hi[:, b, :, :].rearrange("p k n -> p (k n)"), y_raw[:, b, :], ACT.Copy).then_inc(bhi_done, 1)

            def merge_turn(i, first):
                for t in range(S2):
                    if first and t in (1, 3, 5):
                        split_branch((t - 1) // 2)
                    split(slot_merge(i, t + 2), t % 2, i * S2 + (W2 + t + 2))
                    m = t // 3
                    pair = 2 * ((2 * m) % 4)
                    if t % 3 == 1:
                        act.wait_ge(slab_used, i * S2 + (W2 + t + 1))
                        act.wait_ge(br_read, i * 6 + (m + 1))
                        A(mgate[:, m % 2, :, :], ps[:, pair:pair + 2, 0:NG], ACT.Sigmoid).then_inc(gate_done, 1)
                    if t % 9 == 8:
                        jj = t // 9
                        act.wait_ge(msum_done, i * 2 + (jj + 1))
                        A(m_hi[:, bass.ds(i * 4 + 2 * jj, 2), :], msum[:, :, :], ACT.Copy).then_inc(mhi_done, 1)

            act.wait_ge(n2_mm, CH)
            merge_turn(0, True)
            with act.Fori(1, JB // 2) as i:
                merge_turn(i, False)

            def squares(i, nb):
                act.wait_ge(h_sum, i * 2 + (nb + 3))
                for tt in range(2):
                    ins = A(fjunk[:, tt, bass.ds(i * (2 * CC) + CC * nb, CC)], h[:, tt, bass.ds(i * (2 * CC) + CC * nb, CC)], ACT.Square,
                            accum_out=fsq[:, tt, bass.ds(i * 2 + nb, 1)])
                ins.then_inc(f_sq, 1)

            A(stat[:, 12:13], ident[:, 0:1], ACT.Sqrt)

            def out_turn(i, loads):
                for t in range(4):
                    if t < loads:
                        split(slot_out(i, t + 2), t % 2, i * 4 + (W3 + t + 2))
                    if t >= 2:
                        squares(i, t - 2)

            with act.Fori(0, JB // 2 - 1) as i:
                out_turn(i, 4)
            out_turn(JB // 2 - 1, 2)
            act.wait_ge(f_var, 1)
            A(stat[:, 8:10], stat[:, 4:6], ACT.Sqrt).then_inc(f_std, 1)
            act.wait_ge(f_rstd, 1)
            for half in range(2):
                cols = slice(half * D // 2, (half + 1) * D // 2)
                A(hg[:, 1, cols], hg[:, 1, cols], ACT.Copy, scale=stat[:, 7:8]).then_inc(f1_done, 1)

        @block.vector
        def _(dve):
            V = nc.vector

            def lo_part(dst, src, hi):
                return V.tensor_tensor(dst, src, hi.bitcast(F32), ALU.subtract)

            def split(where, par, w):
                dve.wait_ge(hi_done, w + (NCONST + 1))
                lo_part(w_lo[:, par, :, :].rearrange("p k n -> p (k n)"), raw[:, where[0], :],
                        w_hi[:, par, :, :].rearrange("p k n -> p (k n)")).then_inc(lo_done, 1)

            class turn:
                n, c, per = 0, None, 0

            def link(ins):
                turn.n += 1
                ins.then_inc(dve_link, 1)
                dve.wait_ge(dve_link, turn.n if turn.c is None else turn.c * turn.per + turn.n)

            def enter(c, per):
                turn.c, turn.per, turn.before = c, per, turn.n

            def leave(times):
                assert turn.n - turn.before == turn.per, turn.n - turn.before
                turn.c, turn.n = None, turn.before + times * turn.per

            def mlp_layer(layer):
                dve.wait_ge(mlp_mm, layer + 1)
                link(V.tensor_scalar(red[:, 0, :], ps[0:HID, 7, 0:L], mlpw[:, 3 * HID + layer:3 * HID + layer + 1],
                                     mlpw[:, 3 * HID + 3:3 * HID + 4], ALU.add, ALU.mult))
                link(V.tensor_scalar(red[:, 1, :], red[:, 0, :], 1.0 / TWO_PI, MAGIC, ALU.mult, ALU.add))
                link(V.tensor_scalar(red[:, 2, :], red[:, 1, :], -MAGIC, None, ALU.add))
                c1 = float(np.float32(6.28125))
                c2 = float(np.float32(TWO_PI - c1))
                c3 = float(np.float32(TWO_PI - c1 - c2))
                link(V.scalar_tensor_tensor(red[:, 1, :], red[:, 2, :], -c1, red[:, 0, :], ALU.mult, ALU.add))
                link(V.scalar_tensor_tensor(red[:, 3, :], red[:, 2, :], -c2, red[:, 1, :], ALU.mult, ALU.add))
                link(V.scalar_tensor_tensor(red[:, 1, :], red[:, 2, :], -c3, red[:, 3, :], ALU.mult, ALU.add))
                V.tensor_scalar(red[:, 0, :], red[:, 1, :], CLAMP, -CLAMP, ALU.min, ALU.max).then_inc(mlp_red, 1)

            def mean_square():
                dve.wait_ge(x_sq, 3)
                for t, (p, n) in enumerate(TOK):
                    V.tensor_scalar(stat[0:n, 4 + t:5 + t], stat[0:n, t:t + 1], 1.0 / D, EPS, ALU.mult, ALU.add).then_inc(x_var, 1)

            dve.wait_ge(first_landed, 48)
            mlp_layer(0)
            mlp_layer(1)
            mean_square()

            dve.wait_ge(x_std, 1)
            for t, (p, n) in enumerate(TOK):
                last = V.reciprocal(stat[0:n, 12 + t:13 + t], stat[0:n, 8 + t:9 + t])
            last.then_inc(x_rstd, 1)
            dve.wait_ge(x_rstd, 1)
            for t in (0, 2):
                n = TOK[t][1]
                V.tensor_scalar(xin[0:n, t, :], xin[0:n, t, :], stat[0:n, 12 + t:13 + t], None, ALU.mult).then_inc(x_scaled, 1)
            mlp_layer(2)
            dve.wait_ge(small_landed, 32)
            for k in range(KT):
                dve.wait_ge(xt_hi, k + 1)
                ins = V.scalar_tensor_tensor(xn_lo[:, k, :], ps[:, k % 4, 0:L], params[:, NGC + k:NGC + k + 1],
                                             xn_hi[:, k, :].bitcast(F32), ALU.mult, ALU.subtract)
                ins.then_inc(xt_lo, 1)
            V.memset(stat[:, 15:16], 0.0).then_inc(k_evac, 6)
            V.memset(stat[:, 14:15], 0.0).then_inc(h4_read, 1)
            for c in range(CH):
                for j, t in enumerate(FORDER):
                    n = TOK[t][1]
                    nth = c * 3 + j + 1
                    env = envel[0:n, (c + j) % 2, :, :, :]
                    dve.wait_ge(env_done, nth)
                    if t == 2:
                        link(V.memset(env[0:1, :, 1, :], 0.0))
                    dve.wait_ge(h4_mm, nth)
                    V.tensor_tensor(hm[0:n, :, :, :].rearrange("p o d n -> p o (d n)"), ps[0:n, 6:8, :],
                                    env.rearrange("p o d n -> p o (d n)"), ALU.mult).then_inc(h4_read, 1)
                    dve.wait_ge(h4_read, nth + 1)
                    V.tensor_tensor(sd[0:n, 0, :, :], hm[0:n, :, 0, :], hm[0:n, :, 1, :], ALU.add)
                    V.tensor_tensor(sd[0:n, 1, :, :], hm[0:n, :, 0, :], hm[0:n, :, 1, :], ALU.subtract).then_inc(sd_done, 1)
                    dve.wait_ge(sdhi_done, nth)
                    lo = sd_lo[0:n, t, :, :, :] if t < 2 else sd_hi[64:64 + n, t, :, :, :]
                    lo_part(lo, sd[0:n, :, :, :], sd_hi[0:n, t, :, :, :]).then_inc(sdlo_done, 1)
            V.memset(stat[:, 11:12], 0.0).then_inc(proj_read, 2)
            dve.wait_ge(lo_done, NCONST)
            for w in range(2):
                split((w,), w, w)

            def evac(c, name, b):
                bank = 2 * (b % 2)
                src = ps[:, bank:bank + 2, 0:L]
                src16 = ps[:, bank:bank + 2, 0:NG]
                if name == "v":
                    dve.wait_ge(slab_used, c * S1 + (2 * b + 2))
                    V.tensor_copy(v[:, :, :], src).then_inc(proj_read, 1)
                    return
                dve.wait_ge(a_ev, c * (NBLK - 1) + (b + 1 if b < 3 else b))
                if name in ("u", "x1", "x2"):
                    dst = {"u": u, "x1": x1, "x2": x2}[name]
                    t0 = {"u": 0, "x1": 8, "x2": 16}[name]

                    def tap(j, i, to, frm):
                        return V.scalar_tensor_tensor(dst[:, i, to], ps[:, bank + i, frm],
                                                      params[:, bass.ds(c * 2 + (CW + 24 * j + t0 + i), 1)], dst[:, i, to],
                                                      ALU.mult, ALU.add)

                    p0 = L - BLOCKS[b][2]
                    tap(0, 0, slice(p0 + 1, L), slice(0, L - p0 - 1))
                    link(tap(0, 1, slice(p0 + 1, L), slice(0, L - p0 - 1)))
                    tap(2, 0, slice(p0, L - 1), slice(1, L - p0))
                    ins = tap(2, 1, slice(p0, L - 1), slice(1, L - p0))
                elif name == "q":
                    for i in range(2):
                        ins = V.scalar_tensor_tensor(q_lo[:, i, :].rearrange("p (r n) -> p r n", r=4),
                                                     ps[:, bank + i, 0:NG].rearrange("p (r n) -> p r n", r=4)[:, :, ::-1], 0.125,
                                                     q_hi[:, i, :].rearrange("p (r n) -> p r n", r=4).bitcast(F32),
                                                     ALU.mult, ALU.subtract)
                elif name == "k":
                    lo_part(k_lo[:, :, 0:L], src, k_hi[:, :, 0:L])
                    ins = lo_part(k_lo[:, :, L:L + NM], ps[:, bank:bank + 2, 0:NM], k_hi[:, :, L:L + NM])
                elif name == "fin":
                    ins = lo_part(fi_lo[:, :, :], src, fi_hi[:, :, :])
                else:
                    link(V.tensor_scalar(gexp[:, :, :], gexp[:, :, :], 1.0, None, ALU.add))
                    link(V.reciprocal(gexp[:, :, :], gexp[:, :, :]))
                    ins = V.tensor_tensor(gate[:, :, :], src16, gexp[:, :, :], ALU.mult)
                ins.then_inc(proj_read, 1)

            def turned(n_th, hi_ready, done, dst, hi, bank, w=CC, row=64):
                dve.wait_ge(hi_ready, n_th)
                lo_part(dst[:, 0:2, :], ps[:, bank, :].rearrange("p (t n) -> p t n", t=2), hi[:, 0:2, :])
                lo_part(hi[row:row + NM, 2, :], ps[0:NM, bank + 1, 0:w], hi[0:NM, 2, :]).then_inc(done, 1)

            def spectra(c, fs, order):
                for f in fs:
                    n = TOK[f][1]
                    nth = 3 * order + f + 1
                    if f == 0:
                        dve.wait_ge(k_landed, c * 64 + 32 * (order + 1))
                    dve.wait_ge(fwd_mm, c * 6 + nth)
                    bank = ps[0:n, 4 + f % 2, :].rearrange("p (r n) -> p r n", r=2)
                    V.tensor_tensor(prod[0:n, 0, :, :], bank, kspec[0:n, f, :, :], ALU.mult)
                    link(V.tensor_tensor(prod[0:n, 1, :, :], bank, kspec[0:n, f, ::-1, :], ALU.mult))
                    V.tensor_tensor(prod[0:n, 2, 0, :], prod[0:n, 0, 0, :], prod[0:n, 0, 1, :], ALU.subtract)
                    V.tensor_tensor(prod[0:n, 2, 1, :], prod[0:n, 1, 0, :], prod[0:n, 1, 1, :], ALU.add).then_inc(y_full, 1)
                    dve.wait_ge(yhi_done, c * 6 + nth)
                    lo_part(y_lo[0:n, f, :, :] if f < 2 else y_hi[64:64 + n, f, :, :], prod[0:n, 2, :, :],
                            y_hi[0:n, f, :, :]).then_inc(ylo_done, 1)

            def biased(c, hh):
                if hh == 0:
                    dve.wait_ge(b_ready, c + 1)
                dve.wait_ge(s_mm, c * HC + hh + 1)
                V.memset(stat[:, 11:12], 0.0)
                for a in range(2):
                    b0 = NM + 2 * GRID_W if a == 0 else 0
                    ins = V.tensor_tensor_reduce(sco[:, a, :], ps[:, 6 + a, 0:L], bias_t[:, hh, b0:b0 + L], 1.0, -3.0e38,
                                                 ALU.add, ALU.max, stat[:, 6 + a:7 + a])
                link(ins)
                V.tensor_scalar(stat[:, 2:4], stat[:, 6:8], -1.0, None, ALU.mult).then_inc(smax_done, 1)

            def normalized(c, hh):
                dve.wait_ge(exp_done, c * HC + hh + 1)
                link(V.reciprocal(stat[:, 8:10], stat[:, 4:6]))
                for a in range(2):
                    ins = V.tensor_scalar(sco[:, a, :], sco[:, a, :], stat[:, 8 + a:9 + a], None, ALU.mult)
                ins.then_inc(p_done, 1)

            def attended(c, hh):
                r = slice(64 * (hh % 2), 64 * (hh % 2) + 64)
                dve.wait_ge(pv_mm, c * HC + hh + 1)
                V.tensor_copy(o[r, hh // 2, :].rearrange("p (r n) -> p r n", r=4),
                              ps[r, 7, NG:2 * NG].rearrange("p (r n) -> p r n", r=4)[:, :, ::-1]).then_inc(o_done, 1)

            with dve.Fori(0, CH) as c:
                enter(c, 26)
                for t in range(S1):
                    if t in (9, 11, 13):
                        biased(c, (t - 7) // 2)
                    split(slot_main(c, t + 2), t % 2, c * S1 + (t + 2))
                    if t in (9, 11, 13):
                        normalized(c, (t - 7) // 2)
                    if t % 2:
                        evac(c, BLOCKS[t // 2][0], t // 2)
                    if t == 3:
                        turned(c * 3 + 1, t_hi, t_lo, uT_lo, uT_hi, 4)
                    if t == 4:
                        spectra(c, (0, 1), 0)
                    if t == 5:
                        spectra(c, (2,), 0)
                    if t == 6:
                        biased(c, 0)
                        normalized(c, 0)
                    if t in (8, 10, 12, 14):
                        turned(c * HC + (t - 6) // 2, pt_hi, pt_lo, pT_lo, pT_hi, 6, NG, 32)
                    if t in (10, 12, 14):
                        attended(c, (t - 10) // 2)
                    if t == 8:
                        turned(c * 3 + 2, t_hi, t_lo, vT_lo, vT_hi, 4)
                    if t == 9:
                        dve.wait_ge(inv_mm, c * 2 + 1)
                        for i in range(2):
                            ins = V.scalar_tensor_tensor(u[:, i, :], u[:, i, :], params[:, bass.ds(c * 2 + (SK + i), 1)],
                                                         ps[:, 4 + i, 0:L], ALU.mult, ALU.add)
                        link(ins)
                        V.tensor_tensor(x1[:, :, :], x1[:, :, :], u[:, :, :], ALU.mult).then_inc(z_done, 1)
                    if t == 11:
                        turned(c * 3 + 3, t_hi, t_lo, uT_lo, uT_hi, 4)
                    if t == 12:
                        spectra(c, (0, 1), 1)
                    if t == 13:
                        spectra(c, (2,), 1)
                    if t == 15:
                        dve.wait_ge(inv_mm, c * 2 + 2)
                        for i in range(2):
                            ins = V.scalar_tensor_tensor(u[:, i, NM:L], x1[:, i, NM:L],
                                                         params[:, bass.ds(c * 2 + (SK + 8 + i), 1)],
                                                         ps[:, 4 + i, 0:NG], ALU.mult, ALU.add)
                        link(ins)
                        link(V.tensor_tensor(u[:, :, NM:L], u[:, :, NM:L], x2[:, :, NM:L], ALU.mult))
                        dve.wait_ge(y_written, c * 48 + 16)
                        V.tensor_tensor(ystage[:, :, :], u[:, :, NM:L], gate[:, :, :], ALU.mult).then_inc(ya_done, 1)
                        attended(c, 3)
                    if t == 16:
                        for f in range(2):
                            dve.wait_ge(n1_hi, c * 3 + f + 1)
                            lo_part(p2_lo[:, f, :], ps[:, 4 + f, 0:2 * FK], p2_hi[:, f, :]).then_inc(n1_lo, 1)
                    if t == 17:
                        dve.wait_ge(n1_hi, c * 3 + 3)
                        lo_part(p2_hi[64:64 + NM, 2, :], ps[0:NM, 4, 0:2 * FK], p2_hi[0:NM, 2, :]).then_inc(n1_lo, 1)
                        dve.wait_ge(y_written, c * 48 + 32)
                        dve.wait_ge(proj_read, c * NBLK + 11)
                        V.tensor_tensor(ystage[:, :, :], o[:, :, :], gate[:, :, :], ALU.mult).then_inc(yc_done, 1)
                    if t == 19:
                        dve.wait_ge(n2_mm, c + 1)
                        dve.wait_ge(y_written, c * 48 + 48)
                        dve.wait_ge(proj_read, c * NBLK + 12)
                        V.tensor_tensor(ystage[:, :, :], ps[:, 4, :].rearrange("p (i n) -> p i n", i=2), gate[:, :, :],
                                        ALU.mult).then_inc(yb_done, 1)
            leave(CH)

            V.memset(stat[:, 10:11], 0.0).then_inc(br_read, 2)
            V.memset(stat[:, 14:15], 0.0).then_inc(h_sum, 2)

            def split_branch(b):
                dve.wait_ge(bhi_done, b + 1)
                lo_part(yb_lo[:, b, :, :].rearrange("p k n -> p (k n)"), y_raw[:, b, :],
                        yb_hi[:, b, :, :].rearrange("p k n -> p (k n)")).then_inc(blo_done, 1)

            def merge_turn(i, first):
                for t in range(S2):
                    if first and t in (1, 3, 5):
                        split_branch((t - 1) // 2)
                    split(slot_merge(i, t + 2), t % 2, i * S2 + (W2 + t + 2))
                    m = t // 3
                    pair = 2 * ((2 * m + 1) % 4)
                    if t % 3 == 2:
                        dve.wait_ge(slab_used, i * S2 + (W2 + t + 1))
                        dve.wait_ge(gate_done, i * 6 + (m + 3))
                        src = ps[:, pair:pair + 2, 0:NG]
                        if m % 3 == 0:
                            V.tensor_tensor(msum[:, :, :], mgate[:, m % 2, :, :], src, ALU.mult).then_inc(br_read, 1)
                        else:
                            V.tensor_tensor(mterm[:, :, :], mgate[:, m % 2, :, :], src, ALU.mult).then_inc(br_read, 1)
                            dve.wait_ge(br_read, i * 6 + (m + 3))
                            ins = V.tensor_tensor(msum[:, :, :], msum[:, :, :], mterm[:, :, :], ALU.add)
                            if m % 3 == 1:
                                link(ins)
                            else:
                                ins.then_inc(msum_done, 1)
                    if t % 9 == 8:
                        jj = t // 9
                        dve.wait_ge(mhi_done, i * 2 + (jj + 1))
                        lo_part(m_lo[:, bass.ds(i * 4 + 2 * jj, 2), :], msum[:, :, :],
                                m_hi[:, bass.ds(i * 4 + 2 * jj, 2), :]).then_inc(mlo_done, 1)

            merge_turn(0, True)
            with dve.Fori(1, JB // 2) as i:
                enter(i - 1, 2)
                merge_turn(i, False)
            leave(JB // 2 - 1)

            def add_block(i, nb):
                dve.wait_ge(h_landed, 48)
                dve.wait_ge(slab_used, i * 4 + (W3 + nb + 3))
                cols = h[:, :, bass.ds(i * (2 * CC) + CC * nb, CC)]
                V.tensor_tensor(cols, cols, ps[:, 2 * nb:2 * nb + 2, 0:CC], ALU.add).then_inc(h_sum, 1)
                dve.wait_ge(h_sum, i * 2 + (nb + 3))
                for tt in range(2):
                    ins = V.tensor_tensor(hg[:, tt, bass.ds(i * (2 * CC) + CC * nb, CC)],
                                          h[:, tt, bass.ds(i * (2 * CC) + CC * nb, CC)],
                                          fg[:, bass.ds(i * (2 * CC) + CC * nb, CC)], ALU.mult)
                ins.then_inc(hg_done, 1)

            with dve.Fori(0, JB // 2 - 1) as i:
                for t in range(4):
                    split(slot_out(i, t + 2), t % 2, i * 4 + (W3 + t + 2))
                    if t >= 2:
                        add_block(i, t - 2)
            for t in range(4):
                if t < 2:
                    split(slot_out(JB // 2 - 1, t + 2), t % 2, NW - 2 + t)
                if t >= 2:
                    add_block(JB // 2 - 1, t - 2)
            dve.wait_ge(f_sq, JB)
            link(V.tensor_reduce(stat[:, 0:2], fsq[:, :, :], mybir.AxisListType.X, ALU.add))
            V.tensor_scalar(stat[:, 4:6], stat[:, 0:2], 1.0 / D, EPS, ALU.mult, ALU.add).then_inc(f_var, 1)
            dve.wait_ge(f_std, 1)
            dve.wait_ge(hg_done, JB)
            V.reciprocal(stat[:, 6:8], stat[:, 8:10]).then_inc(f_rstd, 1)
            dve.wait_ge(f_rstd, 1)
            for half in range(2):
                cols = slice(half * D // 2, (half + 1) * D // 2)
                V.tensor_scalar(hg[:, 0, cols], hg[:, 0, cols], stat[:, 6:7], None, ALU.mult).then_inc(f_done, 1)


def slab_stream(w_in, wa, wb, wc, wo):
    def slab(w, k0, c0):
        return w[k0:k0 + 1024, c0:c0 + CC].reshape(8, 128, CC).transpose(1, 0, 2).reshape(128, 8 * CC)

    turned = np.concatenate([np.arange(128), np.arange(CC - 1, 127, -1)])
    by_chunk = (np.arange(CH)[:, None] * CC + turned[None, :]).reshape(-1)
    wb = wb[by_chunk]
    w_in = w_in.copy()
    w_in[:, 5 * C:6 * C] = w_in[:, 5 * C + by_chunk]

    slabs = []
    for c in range(CH):
        for _, col, _ in BLOCKS:
            for half in range(2):
                slabs.append(slab(w_in, 1024 * half, col + CC * c))
    for j in range(JB):
        for b in BRANCHES:
            w = (wa, wb, wc)[b]
            for half in range(2):
                slabs.append(slab(w_in, 1024 * half, 10 * C + D * b + CC * j))
            slabs.append(slab(w, 0, CC * j))
    for j in range(0, JB, 2):
        for half in range(2):
            for nb in range(2):
                slabs.append(slab(wo, 1024 * half, CC * (j + nb)))
    assert len(slabs) == NW
    return np.stack(slabs)


def kernel(x, meta_tokens, norm_g, w_in, hy_conv_w, hy_conv_b, hy_flt_w1, hy_flt_b1, hy_flt_w2, hy_flt_b2, hy_flt_w3,
           hy_flt_b3, hy_flt_w4, hy_flt_freq, hy_decay, hy_skip, na_rpb, na_meta_bias, w_branch_a, w_branch_b,
           w_branch_c, w_out, final_g):
    import concourse.bacc as bacc
    from concourse.bass_utils import run_bass_kernel_spmd

    def host(a):
        return np.asarray(a)

    tables, zT, negt, mask, ident = constants()
    by_tile = lambda a, n: host(a).reshape(-1, n, 128).transpose(2, 0, 1).reshape(128, -1)
    arrays = {
        "x": host(x)[0],
        "meta": host(meta_tokens),
        "w_stream": slab_stream(host(w_in)[0], host(w_branch_a)[0], host(w_branch_b)[0], host(w_branch_c)[0], host(w_out)[0]),
        "tables": tables,
        "zT": zT,
        "negt_in": negt,
        "mask_in": mask,
        "ident_in": ident,
        "params_in": np.concatenate([by_tile(hy_conv_w, 24), by_tile(hy_conv_b, 24), by_tile(hy_skip, 8),
                                     by_tile(norm_g, 16)], axis=1),
        "mlp_in": np.stack([host(hy_flt_b1)[0], host(hy_flt_b2)[0], host(hy_flt_b3)[0], host(hy_flt_freq)[0]], axis=1),
        "w1": host(hy_flt_w1)[0],
        "w2": host(hy_flt_w2)[0],
        "w3": host(hy_flt_w3)[0],
        "w4": host(hy_flt_w4)[0].reshape(HID, 4, CH, CC).transpose(2, 0, 1, 3).reshape(CH, HID, 4 * CC),
        "decay": host(hy_decay)[0].reshape(4, CH, CC).transpose(1, 0, 2).reshape(CH, 4 * CC),
        "rpb": host(na_rpb)[0].reshape(-1),
        "mbias": host(na_meta_bias)[0].reshape(CH, HC * NM),
        "final_g": host(final_g),
    }
    arrays = {n: np.ascontiguousarray(a) for n, a in arrays.items()}
    nc = bacc.Bacc("TRN2", target_bir_lowering=False, num_devices=1)
    args = {n: nc.dram_tensor(n, a.shape, mybir.dt.from_np(a.dtype), kind="ExternalInput").ap() for n, a in arrays.items()}
    out = nc.dram_tensor("out", [NG, D], F32, kind="ExternalOutput").ap()
    build(nc, out=out, **args)
    r = run_bass_kernel_spmd(nc, [arrays], core_ids=[0])
    return r.results[0]["out"].reshape(1, NG, D)
```
